# Optimizing a Trainium2 kernel written in Bass

```python
import math
import jax, jax.numpy as jnp
from jax import lax
import numpy as np

D_MODEL = 1024
BATCH = 1
SEQ = 256
DEPTH = 1

D_RNN = 1024
RG_BLOCKS = 4
RG_BW = D_RNN // RG_BLOCKS
CONV_W = 4
RG_C = 8.0
N_HEADS = 16
N_KV = 4
HEAD_DIM = 64
HPG = N_HEADS // N_KV
CMP_LEN = 32
CMP_STRIDE = 16
CMP_HID = 256
SEL_LEN = 64
SEL_TOPN = 16
WINDOW = 512
Q_BLK = 64
D_FF = -(-8 * D_MODEL // (3 * 256)) * 256
EPS = 1e-6
FORCE_SCORE = 1e6

Q_W = N_HEADS * HEAD_DIM
KV_W = N_KV * HEAD_DIM
IN_SPLITS = (D_RNN, D_RNN, Q_W, KV_W, KV_W, KV_W, KV_W, KV_W, KV_W, 3 * N_HEADS, 2 * D_MODEL)
D_IN = sum(IN_SPLITS)

kernel_name = "hawk_nsa_parallel_gated_hybrid"

def rmsnorm(x, g):
    xf = x.astype(jnp.float32)
    y = xf * lax.rsqrt(jnp.mean(xf * xf, axis=-1, keepdims=True) + EPS)
    return (y * g.astype(jnp.float32)).astype(x.dtype)

def masked_softmax(s, mask):
    s = jnp.where(mask, s.astype(jnp.float32), -1e30)
    m = jnp.max(s, axis=-1, keepdims=True)
    e = jnp.where(mask, jnp.exp(s - m), 0.0)
    return e / jnp.maximum(jnp.sum(e, axis=-1, keepdims=True), 1e-30)

def causal_conv(x, w, b):
    S = x.shape[1]
    xp = jnp.pad(x, ((0, 0), (CONV_W - 1, 0), (0, 0)))
    y = b
    for k in range(CONV_W):
        y = y + xp[:, k:k + S] * w[k]
    return y

def rg_lru(x, w_a, b_a, w_i, b_i, lam):
    B, S, _ = x.shape
    xb = x.reshape(B, S, RG_BLOCKS, RG_BW)
    r = jax.nn.sigmoid((jnp.einsum('bsnc,ncd->bsnd', xb, w_a).reshape(B, S, D_RNN) + b_a).astype(jnp.float32))
    i = jax.nn.sigmoid((jnp.einsum('bsnc,ncd->bsnd', xb, w_i).reshape(B, S, D_RNN) + b_i).astype(jnp.float32))
    log_a = -RG_C * r * jax.nn.softplus(-lam.astype(jnp.float32))
    a = jnp.exp(log_a)
    mult = jnp.sqrt(-jnp.expm1(2.0 * log_a))
    mult = jnp.where(jnp.arange(S)[None, :, None] == 0, 1.0, mult)
    u = mult * i * x.astype(jnp.float32)

    def comb(c1, c2):
        a1, b1 = c1
        a2, b2 = c2
        return a1 * a2, a2 * b1 + b2

    _, h = lax.associative_scan(comb, (a, u), axis=1)
    return h.astype(x.dtype)

def compress(kv, pos, w1, w2):
    B, S, G, dh = kv.shape
    n_c = (S - CMP_LEN) // CMP_STRIDE + 1
    idx = jnp.arange(n_c)[:, None] * CMP_STRIDE + jnp.arange(CMP_LEN)[None, :]
    blk = kv[:, idx] + pos[None, None, :, None, :]
    blk = blk.transpose(0, 1, 3, 2, 4).reshape(B, n_c, G, CMP_LEN * dh)
    return jax.nn.gelu(blk @ w1) @ w2

def nsa(q, kc, vc, k_slc, v_slc, k_win, v_win, gates):
    B, S = q.shape[0], q.shape[1]
    n_c = kc.shape[1]
    n_sel = S // SEL_LEN
    topn = min(SEL_TOPN, n_sel)
    scale = HEAD_DIM ** -0.5
    cmp_end = jnp.arange(n_c) * CMP_STRIDE + CMP_LEN - 1
    cs = jnp.arange(n_c) * CMP_STRIDE
    ss = jnp.arange(n_sel) * SEL_LEN
    overlap = ((cs[:, None] < ss[None, :] + SEL_LEN) & (cs[:, None] + CMP_LEN > ss[None, :])).astype(jnp.float32)
    ksb = k_slc.reshape(B, n_sel, SEL_LEN, N_KV, HEAD_DIM).transpose(0, 3, 1, 2, 4)
    vsb = v_slc.reshape(B, n_sel, SEL_LEN, N_KV, HEAD_DIM).transpose(0, 3, 1, 2, 4)
    kwp = jnp.pad(k_win, ((0, 0), (WINDOW, 0), (0, 0), (0, 0)))
    vwp = jnp.pad(v_win, ((0, 0), (WINDOW, 0), (0, 0), (0, 0)))
    bi = jnp.arange(B)[:, None, None]
    gi = jnp.arange(N_KV)[None, :, None]
    blk_ids = jnp.arange(n_sel)

    def q_block(qi):
        s0 = qi * Q_BLK
        tpos = s0 + jnp.arange(Q_BLK)
        qb = lax.dynamic_slice_in_dim(q, s0, Q_BLK, axis=1).reshape(B, Q_BLK, N_KV, HPG, HEAD_DIM)
        gb = lax.dynamic_slice_in_dim(gates, s0, Q_BLK, axis=1).reshape(B, Q_BLK, 3, N_KV, HPG)[..., None]
        s_c = jnp.einsum('bqgjd,bcgd->bqgjc', qb, kc) * scale
        mask_c = (cmp_end[None, :] <= tpos[:, None])[None, :, None, None, :]
        p_c = masked_softmax(s_c, mask_c)
        o_c = jnp.einsum('bqgjc,bcgd->bqgjd', p_c.astype(vc.dtype), vc)
        imp = jnp.einsum('bqgjc,cn->bqgn', p_c, overlap)
        cur = tpos // SEL_LEN
        valid = blk_ids[None, :] <= cur[:, None]
        forced = (blk_ids[None, :] == 0) | (blk_ids[None, :] == cur[:, None]) | (blk_ids[None, :] == cur[:, None] - 1)
        score = jnp.where(forced[None, :, None, :], FORCE_SCORE, imp)
        score = jnp.where(valid[None, :, None, :], score, -1.0)
        top_v, top_i = lax.top_k(score, topn)
        sel_ok = top_v >= 0.0
        idx_t = top_i.transpose(0, 2, 1, 3).reshape(B, N_KV, Q_BLK * topn)
        ksel = ksb[bi, gi, idx_t].reshape(B, N_KV, Q_BLK, topn * SEL_LEN, HEAD_DIM)
        vsel = vsb[bi, gi, idx_t].reshape(B, N_KV, Q_BLK, topn * SEL_LEN, HEAD_DIM)
        kpos = top_i[..., None] * SEL_LEN + jnp.arange(SEL_LEN)
        mask_s = ((kpos <= tpos[None, :, None, None, None]) & sel_ok[..., None]).reshape(B, Q_BLK, N_KV, topn * SEL_LEN)
        s_s = jnp.einsum('bqgjd,bgqkd->bqgjk', qb, ksel) * scale
        p_s = masked_softmax(s_s, mask_s[:, :, :, None, :])
        o_s = jnp.einsum('bqgjk,bgqkd->bqgjd', p_s.astype(vsel.dtype), vsel)
        kw = lax.dynamic_slice_in_dim(kwp, s0, WINDOW + Q_BLK, axis=1)
        vw = lax.dynamic_slice_in_dim(vwp, s0, WINDOW + Q_BLK, axis=1)
        kp = s0 - WINDOW + jnp.arange(WINDOW + Q_BLK)
        mask_w = (kp[None, :] <= tpos[:, None]) & (tpos[:, None] - kp[None, :] < WINDOW) & (kp[None, :] >= 0)
        s_w = jnp.einsum('bqgjd,bkgd->bqgjk', qb, kw) * scale
        p_w = masked_softmax(s_w, mask_w[None, :, None, None, :])
        o_w = jnp.einsum('bqgjk,bkgd->bqgjd', p_w.astype(vw.dtype), vw)
        o = gb[:, :, 0] * o_c + gb[:, :, 1] * o_s + gb[:, :, 2] * o_w
        return o.reshape(B, Q_BLK, Q_W)

    out = lax.map(q_block, jnp.arange(S // Q_BLK))
    return out.transpose(1, 0, 2, 3).reshape(B, S, Q_W)

def setup_inputs(seed: int = 0) -> dict:
    key = jax.random.key(seed)
    ks = jax.random.split(key, 32)
    f32 = jnp.float32
    L = DEPTH

    def nrm(k, shape, fan_in):
        return jax.random.normal(k, shape, f32) * (fan_in ** -0.5)

    a0 = jax.random.uniform(ks[8], (L, D_RNN), f32, 0.9, 0.999)
    return {
        "x": jax.random.normal(ks[0], (BATCH, SEQ, D_MODEL), f32),
        "norm1": 1.0 + 0.02 * jax.random.normal(ks[1], (L, D_MODEL), f32),
        "w_in": nrm(ks[2], (L, D_MODEL, D_IN), D_MODEL),
        "conv_w": nrm(ks[3], (L, CONV_W, D_RNN), CONV_W),
        "conv_b": 0.01 * jax.random.normal(ks[4], (L, D_RNN), f32),
        "rg_wa": nrm(ks[5], (L, RG_BLOCKS, RG_BW, RG_BW), RG_BW),
        "rg_ba": 0.01 * jax.random.normal(ks[6], (L, D_RNN), f32),
        "rg_wi": nrm(ks[7], (L, RG_BLOCKS, RG_BW, RG_BW), RG_BW),
        "rg_bi": 0.01 * jax.random.normal(ks[9], (L, D_RNN), f32),
        "rg_lambda": jnp.log(a0) - jnp.log1p(-a0),
        "q_norm": 1.0 + 0.02 * jax.random.normal(ks[10], (L, HEAD_DIM), f32),
        "k_norm": 1.0 + 0.02 * jax.random.normal(ks[11], (L, 3, HEAD_DIM), f32),
        "cmp_pos_k": 0.02 * jax.random.normal(ks[12], (L, CMP_LEN, HEAD_DIM), f32),
        "cmp_pos_v": 0.02 * jax.random.normal(ks[13], (L, CMP_LEN, HEAD_DIM), f32),
        "cmp_k_w1": nrm(ks[14], (L, CMP_LEN * HEAD_DIM, CMP_HID), CMP_LEN * HEAD_DIM),
        "cmp_k_w2": nrm(ks[15], (L, CMP_HID, HEAD_DIM), CMP_HID),
        "cmp_v_w1": nrm(ks[16], (L, CMP_LEN * HEAD_DIM, CMP_HID), CMP_LEN * HEAD_DIM),
        "cmp_v_w2": nrm(ks[17], (L, CMP_HID, HEAD_DIM), CMP_HID),
        "w_rg_out": nrm(ks[18], (L, D_RNN, D_MODEL), D_RNN),
        "w_nsa_out": nrm(ks[19], (L, Q_W, D_MODEL), Q_W),
        "w_o": nrm(ks[20], (L, D_MODEL, D_MODEL), D_MODEL),
        "norm2": 1.0 + 0.02 * jax.random.normal(ks[21], (L, D_MODEL), f32),
        "w_gate": nrm(ks[22], (L, D_MODEL, D_FF), D_MODEL),
        "w_up": nrm(ks[23], (L, D_MODEL, D_FF), D_MODEL),
        "w_down": nrm(ks[24], (L, D_FF, D_MODEL), D_FF),
    }

def reference(x, norm1, w_in, conv_w, conv_b, rg_wa, rg_ba, rg_wi, rg_bi, rg_lambda, q_norm, k_norm,
              cmp_pos_k, cmp_pos_v, cmp_k_w1, cmp_k_w2, cmp_v_w1, cmp_v_w2, w_rg_out, w_nsa_out, w_o,
              norm2, w_gate, w_up, w_down):
    B, S, _ = x.shape
    bounds = np.cumsum((0,) + IN_SPLITS)
    for l in range(DEPTH):
        h = rmsnorm(x, norm1[l])
        z = h @ w_in[l]
        (z_rx, z_ry, z_q, z_kc, z_vc, z_ks, z_vs, z_kw, z_vw, z_ng, z_mg) = [
            z[..., int(bounds[i]):int(bounds[i + 1])] for i in range(len(IN_SPLITS))]
        xr = causal_conv(z_rx, conv_w[l], conv_b[l])
        xr = rg_lru(xr, rg_wa[l], rg_ba[l], rg_wi[l], rg_bi[l], rg_lambda[l])
        y_a = (xr * jax.nn.gelu(z_ry)) @ w_rg_out[l]
        kvs = lambda t: t.reshape(B, S, N_KV, HEAD_DIM)
        q = rmsnorm(z_q.reshape(B, S, N_HEADS, HEAD_DIM), q_norm[l])
        kc = rmsnorm(compress(kvs(z_kc), cmp_pos_k[l], cmp_k_w1[l], cmp_k_w2[l]), k_norm[l, 0])
        vc = compress(kvs(z_vc), cmp_pos_v[l], cmp_v_w1[l], cmp_v_w2[l])
        k_s = rmsnorm(kvs(z_ks), k_norm[l, 1])
        k_w = rmsnorm(kvs(z_kw), k_norm[l, 2])
        ng = jax.nn.sigmoid(z_ng).reshape(B, S, 3, N_HEADS)
        y_b = nsa(q, kc, vc, k_s, kvs(z_vs), k_w, kvs(z_vw), ng) @ w_nsa_out[l]
        mg = jax.nn.sigmoid(z_mg).reshape(B, S, 2, D_MODEL)
        x = x + (mg[:, :, 0] * y_a + mg[:, :, 1] * y_b) @ w_o[l]
        h2 = rmsnorm(x, norm2[l])
        x = x + (jax.nn.silu(h2 @ w_gate[l]) * (h2 @ w_up[l])) @ w_down[l]
    return x


_drawn_inputs = setup_inputs


def setup_inputs(seed=0):
    import zlib

    import numpy as np

    out = dict(_drawn_inputs(seed))
    spreads = {}
    factors = {'norm1': 6.776,
     'conv_b': 7.174,
     'rg_ba': 38.505,
     'rg_bi': 34.521,
     'q_norm': 8.0,
     'k_norm': 8.0,
     'cmp_pos_k': 41.208,
     'cmp_pos_v': 64.0,
     'norm2': 13.037}
    for name, (base, spread) in spreads.items():
        noise = np.random.default_rng([zlib.crc32(name.encode()), seed]).standard_normal(out[name].shape)
        drawn = base * np.exp(spread * noise) if base else spread * noise
        out[name] = __import__('jax').numpy.asarray(drawn.astype(out[name].dtype))
    for name, factor in factors.items():
        out[name] = (out[name] * factor).astype(out[name].dtype)
    return out
```

```python
from contextlib import ExitStack

import numpy as np

import concourse.bass as bass
from concourse import mybir

F32 = mybir.dt.float32
F32R = mybir.dt.float32r
ALU = mybir.AluOpType
ACT = mybir.ActivationFunctionType
AX = mybir.AxisListType.X

P = 128
S = 256
D = 1024
T2 = S // P
KC = D // P
HEADS, GROUPS, DH = 16, 4, 64
DFF = 2816
FF = DFF // P
CONV = 4
EPS = 1e-6
NEG = -float(2 ** 120)
SCALE = DH ** -0.5
SLOT = 2048

ORDER = [("kc", 1), ("vc", 1), ("kk", 2), ("vv", 2), ("q", 4), ("w1k", 2), ("w1v", 2), ("rx", 4),
         ("rg", 2), ("ry", 4), ("rgo", 4), ("mg", 8), ("nso", 4), ("wo", 4), ("gu", FF), ("dn", FF // 2)]
FIRST = {}
NSLOT = 0
for _name, _n in ORDER:
    FIRST[_name] = NSLOT
    NSLOT += _n
ACC_ORDER = [("kc", 1), ("vc", 1), ("kk", 2), ("vv", 2), ("q", 4), ("w1k", 1), ("w1v", 1), ("rx", 4),
             ("rg", 8), ("ry", 4), ("rgo", 4), ("mg", 8), ("nso", 4), ("wo", 4), ("gu", FF), ("dn", 4)]
USE = {}
_u = 0
for _name, _n in ACC_ORDER:
    USE[_name] = _u
    _u += _n
MISC_ORDER = [("xT", 4), ("ng", 1), ("ngT", 1), ("kT", 4), ("qT", 4), ("hidk", 1), ("kcn", 1), ("hidv", 1), ("kcT", 1),
              ("vrep", 1), ("cmps", 1), ("pcT", 1), ("att", 4 * HEADS), ("mT", 4), ("hT2", 4)]
MISC = {}
_u = 0
for _name, _n in MISC_ORDER:
    MISC[_name] = _u
    _u += _n

RAW = 3
HL = 3
AHEAD = HL - 1
HEAD0 = FIRST["rx"] + 3
G1, G2, CW, CB, BA, BI, LAM, QN, KN, PK, PV, NPRM = 0, 8, 16, 48, 56, 64, 72, 80, 81, 84, 100, 116
NG_W, W2K, W2V, NSMALL = 0, 384, 512, 640


def hybrid_layer(nc, x, stream, small_w, params, out):
    ctx = ExitStack()
    with ctx:
        def sb(name, shape, dt=F32):
            return ctx.enter_context(nc.sbuf_tensor(name, shape, dt))

        def sem(name):
            return ctx.enter_context(nc.semaphore(name))

        raw = sb("raw", [P, RAW, SLOT])
        w_hi = sb("w_hi", [P, HL, SLOT], F32R)
        w_lo = sb("w_lo", [P, HL, SLOT], F32R)
        xs = sb("xs", [P, T2, D])
        scr = sb("scr", [P, 6144])
        h_hi = sb("h_hi", [P, KC, S], F32R)
        h_lo = sb("h_lo", [P, KC, S], F32R)
        act = sb("act", [P, 12416], F32R)
        v_sb = sb("v_sb", [P, T2, 512])
        pbuf = sb("pbuf", [P, 1536])
        vcx = sb("vcx", [P, 2, 8, DH])
        pcT = sb("pcT", [P, 2, S])
        rgt = sb("rgt", [P, 512])
        cmpr = sb("cmpr", [P, 1280 + 128], F32R)
        sw_hi = sb("sw_hi", [P, NSMALL], F32R)
        sw_lo = sb("sw_lo", [P, NSMALL], F32R)
        prm = sb("prm", [P, NPRM])
        ident = sb("ident", [P, P])
        identr = sb("identr", [P, P], F32R)
        maskf = sb("maskf", [P, 2 * P + 2 * 16])
        maskr = sb("maskr", [P, 2 * P + 2 * 16], F32R)
        bd = sb("bd", [P, 8])
        half = sb("half", [P, 16])
        ss = sb("ss", [P, 6, 16])
        ms = sb("ms", [P, 6, 16])
        rs = sb("rs", [P, 6, 16])
        gates = sb("gates", [P, T2, 3, HEADS])
        gtmp = sb("gtmp", [48, S])
        sm = sb("sm", [P, 13, 8])
        cst = sb("cst", [P, 4, 32])
        ast = sb("ast", [P, 5, 4])
        psum = [ctx.enter_context(nc.psum_tensor(f"bank{b}", [P, 512], F32)) for b in range(8)]

        xn = scr[:, 0:2048].rearrange("p (t n) -> p t n", t=T2)
        smraw = scr[:, 5504:6144]
        xsq = scr[:, 2048:3072]
        zc = [scr[:, 1040 * j:1040 * (j + 1)].rearrange("p (e n) -> p e n", e=2) for j in range(2)]
        kz = scr[:, 2080:3104].rearrange("p (t n) -> p t n", t=T2)
        kn = scr[:, 3104:5152].rearrange("p (t n) -> p t n", t=T2)
        qz = scr[:, 0:2048].rearrange("p (t n) -> p t n", t=T2)
        sq = pbuf[:, 0:1024].rearrange("p (t n) -> p t n", t=T2)
        hid = [scr[0:64, 2080 + 256 * j:2336 + 256 * j] for j in range(2)]
        kcn = scr[0:64, 2592:2720]
        kcsq = scr[0:64, 2720:2784]
        cexp = scr[:, 3104:3616]
        A = scr[:, 0:2048].rearrange("p (m s) -> p m s", m=KC)
        B = scr[:, 2048:4096].rearrange("p (m s) -> p m s", m=KC)
        C = scr[:, 4096:6144].rearrange("p (m s) -> p m s", m=KC)
        Dr = xs[:, :, :].rearrange("p t (m s) -> p (t m) s", s=S)
        mrg = scr[:, 0:2048].rearrange("p (t n) -> p t n", t=T2)
        mt1 = scr[:, 2048:4096].rearrange("p (t n) -> p t n", t=T2)
        mtt = scr[:, 4096:5120].rearrange("p (t n) -> p t n", t=T2)
        xn2 = scr[:, 4096:6144].rearrange("p (t n) -> p t n", t=T2)
        sg = scr[:, 0:512].rearrange("p (b n) -> p b n", b=2)
        sa = scr[:, 512:1024].rearrange("p (b n) -> p b n", b=2)
        k_hh = act[:, 0:2048].rearrange("p (g c) -> p g c", g=GROUPS)
        k_ll = act[:, 2048:4096].rearrange("p (g c) -> p g c", g=GROUPS)
        q_st = act[:, 4096:8192].rearrange("p (j e s) -> p j e s", j=8, e=2)
        oT = q_st
        y_hi = act[:, 8192:10240].rearrange("p (m s) -> p m s", m=KC)
        y_lo = act[:, 10240:12288].rearrange("p (m s) -> p m s", m=KC)
        z_hi = [act[:, 8192 + 2080 * j:8192 + 2080 * j + 1040] for j in range(2)]
        z_lo = [act[:, 8192 + 2080 * j + 1040:8192 + 2080 * (j + 1)] for j in range(2)]
        a_hi = act[:, 0:FF * S].rearrange("p (m s) -> p m s", m=FF)
        a_lo = act[:, FF * S:2 * FF * S].rearrange("p (m s) -> p m s", m=FF)
        hidk_hi, hidk_lo = cmpr[:, 0:128], cmpr[:, 128:256]
        hidv_hi, hidv_lo = cmpr[:, 256:768], cmpr[:, 768:1280]
        kc_hh, kc_ll = cmpr[:, 1280:1344], cmpr[:, 1344:1408]
        prob = pbuf[:, 0:768]
        pTa = pbuf[:, 768:1280]
        pTb = pbuf[:, 1280:1536]

        def f(ap):
            return ap.bitcast(F32)

        def acc(u):
            return psum[u % 4]

        def misc(m):
            return psum[4 + m % 4]

        o_bank = misc(MISC["att"] + 3)[:, S:2 * S]

        def misc_count(m):
            return m + 1 if m < MISC["att"] else m + 1 - 4 * HEADS

        landed = [sem(f"landed{i}") for i in range(RAW)]
        x_in, x1_in, small_in, prm_in, xr_in = sem("x_in"), sem("x1_in"), sem("small_in"), sem("prm_in"), sem("xr_in")
        hi_ready, lo_ready = sem("hi_ready"), sem("lo_ready")
        slot_done = sem("slot_done")
        acc_free = [sem(f"acc_free{i}") for i in range(4)]
        misc_done = sem("misc_done")
        s_done, ta_done, tb_done = sem("s_done"), sem("ta_done"), sem("tb_done")
        misc_free = [sem(f"misc_free{i}") for i in range(4)]
        consts, masks_r = sem("consts"), sem("masks_r")
        small_hi, small_lo = sem("small_hi"), sem("small_lo")
        squares, ms_ready, rs_ready = sem("squares"), sem("ms_ready"), sem("rs_ready")
        evac_hi = sem("evac_hi")
        xn_ready, xn1_ready = sem("xn_ready"), sem("xn1_ready")
        zc_ready, z_hi_ready, z_lo_ready = sem("zc_ready"), sem("z_hi_ready"), sem("z_lo_ready")
        k_copied, q_copied, kn_ready, qn_ready = sem("k_copied"), sem("q_copied"), sem("kn_ready"), sem("qn_ready")
        sq_summed = sem("sq_summed")
        gate_tanh, gates_ready = sem("gate_tanh"), sem("gates_ready")
        hid_ready, hid_hi, hid_lo = sem("hid_ready"), sem("hid_hi"), sem("hid_lo")
        kcn_ready, c_shift, c_exp, c_ready = sem("kcn_ready"), sem("c_shift"), sem("c_exp"), sem("c_ready")
        max_ready, scale_ready, prob_ready = sem("max_ready"), sem("scale_ready"), sem("prob_ready")
        pT_ready = sem("pT_ready")
        o_done, o_hi, o_ready = sem("o_done"), sem("o_hi"), sem("o_ready")
        sp_neg, sp_exp, sp_ready = sem("sp_neg"), sem("sp_exp"), sem("sp_ready")
        conv0, xr_ready, xr_hi, xr_lo = sem("conv0"), sem("xr_ready"), sem("xr_hi"), sem("xr_lo")
        rg_done, ta_ready, ti_ready = sem("rg_done"), sem("ta_ready"), sem("ti_ready")
        gated_x, log_a, w_ready, a_ready = sem("gated_x"), sem("log_a"), sem("w_ready"), sem("a_ready")
        asq_ready, asq_used, root_ready, ry_ready = sem("asq_ready"), sem("asq_used"), sem("root_ready"), sem("ry_ready")
        gelu_ready, y_ready, y_hi_ready, y_lo_ready = sem("gelu_ready"), sem("y_ready"), sem("y_hi_ready"), sem("y_lo_ready")
        ya_ready, g0_tanh, m_gated, g1_ready = sem("ya_ready"), sem("g0_tanh"), sem("m_gated"), sem("g1_ready")
        merged = sem("merged")
        x1_ready, silu_ready, a_prod, a_hi_ready, a_lo_ready = sem("x1_ready"), sem("silu_ready"), sem("a_prod"), sem("a_hi_ready"), sem("a_lo_ready")
        dn_done, res_ready, stored = sem("dn_done"), sem("res_ready"), sem("stored")
        act_chain, dve_chain, pool_chain = sem("act_chain"), sem("dve_chain"), sem("pool_chain")

        def wait_acc_free(eng, u):
            if u >= 4:
                eng.wait_ge(acc_free[u % 4], u // 4)

        def wait_misc_free(eng, m):
            if m >= 4:
                eng.wait_ge(misc_free[m % 4], m // 4)

        def wait_misc_read(eng, m):
            eng.wait_ge(misc_free[m % 4], m // 4 + 1)

        NORM_X, NORM_K, NORM_Q0, NORM_Q1, NORM_KC, NORM_X1 = range(6)
        NORM_SHAPE = [(P, 2), (P, 16), (P, 16), (P, 16), (64, 1), (P, 2)]

        block = ctx.enter_context(nc.Block())

        @block.sync
        def _(sp):
            sp.dma_start(xs[:, 0, :], x[0:P, :]).then_inc(x_in, 16)
            for i in range(NSLOT):
                if i >= RAW:
                    sp.wait_ge(lo_ready, i - RAW + 1)
                sp.dma_start(raw[:, i % RAW, :], stream[i, :, :]).then_inc(landed[i % RAW], 16)
            for t in range(T2):
                for n in range(2):
                    sp.wait_ge(res_ready, 2 * t + n + 1)
                    sp.dma_start(out[t * P:(t + 1) * P, n * 512:(n + 1) * 512],
                                 xs[:, t, n * 512:(n + 1) * 512]).then_inc(stored, 16)
            sp.wait_ge(stored, 16 * 4)

        @block.gpsimd
        def _(pool):
            pool.memset(ident[:, :], 0.0).then_inc(pool_chain, 1)
            pool.memset(maskf[:, :], 0.0).then_inc(pool_chain, 1)
            pool.memset(bd[:, :], 1.0).then_inc(pool_chain, 1)
            pool.memset(half[:, :], -0.5).then_inc(pool_chain, 1)
            pool.wait_ge(pool_chain, 4)
            pool.affine_select(out=ident[:, :], in_=ident[:, :], compare_op=ALU.not_equal, fill=1.0,
                               base=0, pattern=[[-1, P]], channel_multiplier=1).then_inc(consts, 1)
            cm = maskf[:, 0:2 * P].rearrange("p (b j) -> p b j", b=2)
            pool.affine_select(out=cm, in_=cm, compare_op=ALU.is_ge, fill=NEG, base=0,
                               pattern=[[0, 2], [-1, P]], channel_multiplier=1).then_inc(consts, 1)
            cc = maskf[:, 2 * P:].rearrange("p (t c) -> p t c", t=T2)
            pool.affine_select(out=cc, in_=cc, compare_op=ALU.is_ge, fill=NEG, base=-31,
                               pattern=[[P, T2], [-16, 16]], channel_multiplier=1).then_inc(consts, 1)
            pool.affine_select(out=bd[:, :], in_=bd[:, :], compare_op=ALU.is_ge, fill=0.0, base=0,
                               pattern=[[-16, 8]], channel_multiplier=1).then_inc(pool_chain, 1)
            pool.wait_ge(pool_chain, 5)
            pool.affine_select(out=bd[:, :], in_=bd[:, :], compare_op=ALU.is_ge, fill=0.0, base=15,
                               pattern=[[16, 8]], channel_multiplier=-1).then_inc(consts, 1)

            def rsqrt(n):
                p, w = NORM_SHAPE[n]
                pool.wait_ge(ms_ready, n + 1)
                pool.tensor_tensor(rs[0:p, n, 0:w], ms[0:p, n, 0:w], half[0:p, 0:w], ALU.pow).then_inc(rs_ready, 1)

            for n in (NORM_X, NORM_K, NORM_Q0, NORM_Q1, NORM_KC):
                rsqrt(n)
            for h in range(HEADS):
                pool.wait_ge(scale_ready, h + 1)
                for j, (a, b) in enumerate(((0, 128), (128, 256), (256, 512), (512, 768))):
                    ins = pool.tensor_scalar(prob[:, a:b], prob[:, a:b], ast[:, 4, j:j + 1], 1.0, ALU.mult, ALU.mult)
                ins.then_inc(prob_ready, 1)
                if h == 12:
                    pool.wait_ge(y_lo_ready, 4)
                    pool.dma_start(xs[:, :, :], x.rearrange("(t p) n -> p t n", p=P)).then_inc(xr_in, 16)
            rsqrt(NORM_X1)

        @block.scalar
        def _(sc):
            sc.dma_start(xs[:, 1, :], x[P:2 * P, :]).then_inc(x1_in, 16)
            sc.dma_start(prm[:, :], params[:, :]).then_inc(prm_in, 16)
            sc.dma_start(smraw, small_w[:, :]).then_inc(small_in, 16)

            def split_hi(i):
                if i >= NSLOT:
                    return
                sc.wait_ge(landed[i % RAW], 16 * (i // RAW + 1))
                if i >= HL:
                    sc.wait_ge(slot_done, i - HL + 1)
                sc.activation(w_hi[:, i % HL, :], raw[:, i % RAW, :], ACT.Copy).then_inc(hi_ready, 1)

            def acc_ready(slot):
                sc.wait_ge(slot_done, slot + 1)

            sc.wait_ge(x_in, 16)
            sc.activation(xsq, xs[:, 0, :], ACT.Square, accum_out=ss[:, NORM_X, 0:1]).then_inc(squares, 1)
            split_hi(0)
            sc.wait_ge(rs_ready, NORM_X + 1)
            sc.wait_ge(x1_in, 16)
            sc.activation(xn[:, 1, :], xs[:, 1, :], ACT.Copy, scale=rs[:, NORM_X, 1:2]).then_inc(xn1_ready, 1)

            def unit_hi(m, j, gain_col):
                sc.wait_ge(misc_done, misc_count(m))
                for e in range(2):
                    c = 2 * j + e
                    ins = sc.activation(h_hi[:, c, :], misc(m)[:, e * S:(e + 1) * S], ACT.Copy,
                                        scale=prm[:, gain_col + c:gain_col + c + 1])
                ins.then_inc(evac_hi, 1)

            sc.wait_ge(prm_in, 16)
            for j in range(4):
                unit_hi(MISC["xT"] + j, j, G1)
            sc.wait_ge(small_in, 16)
            sc.activation(sw_hi[:, :], smraw, ACT.Copy).then_inc(small_hi, 1)
            split_hi(1)

            def squares_and_copy(name, first_slot, use, dst, n, copied):
                acc_ready(first_slot + 1)
                if n > NORM_K:
                    sc.wait_ge(sq_summed, 2 * (n - NORM_K))
                for t in range(T2):
                    sc.activation(sq[:, t, :], acc(use + t)[:, :], ACT.Square).then_inc(squares, 1)
                for t in range(T2):
                    sc.activation(dst[:, t, :], acc(use + t)[:, :], ACT.Copy).then_inc(acc_free[(use + t) % 4], 1)

            for i in range(NSLOT + 2):
                h = i - HEAD0
                if h >= 3 and h % 2 == 1 and h <= HEADS + 1:
                    pair = (h - 3) // 2
                    sc.wait_ge(o_done, 2 * pair + 2)
                    sc.activation(oT[:, pair, 0, :], o_bank, ACT.Copy).then_inc(o_hi, 1)
                if 1 <= h <= HEADS:
                    m = MISC["att"] + 4 * (h - 1)
                    sc.wait_ge(ta_done, h)
                    if h >= 2:
                        sc.wait_ge(o_done, h - 1)
                    sc.activation(pTa, misc(m + 2)[:, :], ACT.Copy).then_inc(misc_free[(m + 2) % 4], 1)
                    sc.wait_ge(tb_done, h)
                    sc.activation(pTb, misc(m + 3)[:, 0:256], ACT.Copy).then_inc(misc_free[(m + 3) % 4], 1)
                split_hi(i + AHEAD)
                if 0 <= h < HEADS:
                    m = MISC["att"] + 4 * h
                    sc.wait_ge(max_ready, h + 1)
                    if h >= 1:
                        sc.wait_ge(tb_done, h)
                    for j, (a, b) in enumerate(((0, 128), (128, 256), (256, 512), (512, 768))):
                        bank = misc(m + j // 2)
                        off = 0 if j % 2 == 0 else (b - a)
                        ins = sc.activation(prob[:, a:b], bank[:, off:off + b - a], ACT.Exp, bias=ast[:, 1, j:j + 1],
                                            scale=SCALE, accum_out=ast[:, 2, j:j + 1])
                        if j % 2 == 1:
                            ins.then_inc(misc_free[(m + j // 2) % 4], 1)

                if i == 2:
                    sc.wait_ge(misc_done, misc_count(MISC["ng"]))
                    sc.activation(gtmp[:, :], misc(MISC["ng"])[0:48, 0:S], ACT.Tanh,
                                  scale=0.5).then_inc(misc_free[MISC["ng"] % 4], 1)
                if i == 5:
                    sc.wait_ge(sp_neg, 1)
                    sc.activation(sm[:, 1, :], sm[:, 0, :], ACT.Exp).then_inc(sp_exp, 1)
                for j, name in enumerate(("kc", "vc")):
                    if i == FIRST[name] + 1:
                        sc.wait_ge(zc_ready, j + 1)
                        sc.activation(z_hi[j], zc[j].rearrange("p e n -> p (e n)"), ACT.Copy).then_inc(z_hi_ready, 1)
                if i == FIRST["kk"] + 2:
                    squares_and_copy("kk", FIRST["kk"], USE["kk"], kz, NORM_K, k_copied)
                if i == FIRST["vv"] + 2:
                    acc_ready(FIRST["vv"] + 1)
                    for t in range(T2):
                        u = USE["vv"] + t
                        sc.activation(v_sb[:, t, :], acc(u)[:, :], ACT.Copy).then_inc(acc_free[u % 4], 1)
                if i == FIRST["vv"] + 2:
                    for g in range(GROUPS):
                        m = MISC["kT"] + g
                        sc.wait_ge(misc_done, misc_count(m))
                        for b in range(2):
                            ins = sc.activation(k_hh[:, g, b * S:(b + 1) * S], misc(m)[:, b * S:(b + 1) * S], ACT.Copy,
                                                scale=prm[:, KN + 1 + b:KN + 2 + b])
                        ins.then_inc(evac_hi, 1)
                for pnl in range(2):
                    if i == FIRST["q"] + 2 * pnl + 2:
                        if pnl == 0:
                            sc.wait_ge(z_lo_ready, 2)
                        squares_and_copy("q", FIRST["q"] + 2 * pnl, USE["q"] + 2 * pnl,
                                         qz[:, :, pnl * 512:(pnl + 1) * 512], NORM_Q0 + pnl, q_copied)
                    if i == FIRST["q"] + 2 * pnl + 4:
                        for v in range(2):
                            m = MISC["qT"] + 2 * pnl + v
                            sc.wait_ge(misc_done, misc_count(m))
                            pr = 4 * pnl + 2 * v
                            for e in range(2):
                                ins = sc.activation(q_st[0:64, pr:pr + 2, e, :],
                                                    misc(m)[64 * e:64 * e + 64, :].rearrange("p (j s) -> p j s", j=2),
                                                    ACT.Copy, scale=prm[64 * e:64 * e + 64, QN:QN + 1])
                            ins.then_inc(evac_hi, 1)
                for j, name in enumerate(("w1k", "w1v")):
                    if i == FIRST[name] + 2:
                        acc_ready(FIRST[name] + 1)
                        if j == 0:
                            sc.wait_ge(kn_ready, 2)
                        sc.activation(hid[j], acc(USE[name])[0:64, 0:256], ACT.Gelu_apprx_tanh).then_inc(hid_ready, 1)
                    if i == FIRST[name] + 3:
                        m = MISC["hidk"] if j == 0 else MISC["hidv"]
                        sc.wait_ge(misc_done, misc_count(m))
                        if j == 0:
                            ins = sc.activation(hidk_hi, misc(m)[:, 0:128], ACT.Copy)
                        else:
                            ins = sc.activation(hidv_hi.rearrange("p (c j n) -> p c j n", c=8, j=4),
                                                misc(m)[:, 0:128].rearrange("p (c n) -> p c n", c=8).unsqueeze(2)
                                                .broadcast_to([P, 8, 4, 16]), ACT.Copy)
                        ins.then_inc(hid_hi, 1)
                if i == FIRST["w1v"] + 2:
                    sc.wait_ge(misc_done, misc_count(MISC["kcn"]))
                    sc.activation(kcsq, misc(MISC["kcn"])[0:64, 0:64], ACT.Square,
                                  accum_out=ss[0:64, NORM_KC, 0:1]).then_inc(squares, 1)
                if i == FIRST["rx"] + 1:
                    sc.wait_ge(misc_done, misc_count(MISC["kcT"]))
                    sc.activation(kc_hh, misc(MISC["kcT"])[:, 0:64], ACT.Copy, scale=prm[:, KN:KN + 1]).then_inc(evac_hi, 1)
                if i == FIRST["rx"] + 2:
                    sc.wait_ge(c_shift, 1)
                    sc.activation(cexp, cexp, ACT.Exp, scale=SCALE).then_inc(c_exp, 1)
                r = i - FIRST["rx"] - 1
                if 0 <= r < 4:
                    acc_ready(FIRST["rx"] + r)
                    for e in range(2):
                        m = 2 * r + e
                        ins = sc.activation(A[:, m, :], acc(USE["rx"] + r)[:, e * S:(e + 1) * S], ACT.Identity,
                                            scale=prm[:, CW + 24 + m:CW + 25 + m], bias=prm[:, CB + m:CB + m + 1])
                        ins.then_inc(conv0, 1)
                    sc.wait_ge(xr_ready, r + 1)
                    sc.activation(y_hi[:, 2 * r:2 * r + 2, :], A[:, 2 * r:2 * r + 2, :], ACT.Copy).then_inc(xr_hi, 1)
                r = i - FIRST["rg"] - 1
                if 0 <= r < 2:
                    for n in (2 * r, 2 * r + 1):
                        for kind in range(2):
                            u = USE["rg"] + 2 * n + kind
                            if n % 2 == 1 and kind == 1:
                                acc_ready(FIRST["rg"] + r)
                            else:
                                sc.wait_ge(rg_done, 3 * r + 2 * (n % 2) + kind + 1)
                            for e in range(2):
                                m = 2 * n + e
                                dst = (C, Dr)[kind]
                                ins = sc.activation(dst[:, m, :], acc(u)[:, e * S:(e + 1) * S], ACT.Tanh, scale=0.5,
                                                    bias=sm[:, 10 + kind, m:m + 1])
                                if e == 0:
                                    ins.then_inc((ta_ready, ti_ready)[kind], 1)
                            ins.then_inc(acc_free[u % 4], 1)
                if i == FIRST["rg"] + 3:
                    sc.wait_ge(log_a, 8)
                    sc.wait_ge(gated_x, 4)
                    sc.activation(Dr[:, :, :], C[:, :, :], ACT.Tanh, scale=-1.0).then_inc(w_ready, 1)
                    sc.activation(C[:, :, :], C[:, :, :], ACT.Exp).then_inc(a_ready, 1)
                    sc.wait_ge(a_ready, 1)
                if i == FIRST["rg"] + 4:
                    for n in range(4):
                        if n >= 1:
                            sc.wait_ge(asq_used, n)
                        sc.activation(rgt[:, :].rearrange("p (m s) -> p m s", m=2), C[:, 2 * n:2 * n + 2, :],
                                      ACT.Square).then_inc(asq_ready, 1)
                    sc.wait_ge(asq_used, 4)
                    sc.activation(Dr[:, :, :], Dr[:, :, :], ACT.Sqrt, scale=0.25).then_inc(root_ready, 1)
                r = i - FIRST["ry"] - 1
                if 0 <= r < 4:
                    acc_ready(FIRST["ry"] + r)
                    u = USE["ry"] + r
                    sc.activation(B[:, 2 * r:2 * r + 2, :], acc(u)[:, :].rearrange("p (m s) -> p m s", m=2),
                                  ACT.Copy).then_inc(acc_free[u % 4], 1)
                    if r % 2 == 1:
                        sc.wait_ge(acc_free[u % 4], u // 4 + 1)
                        v = r - 1
                        sc.activation(B[:, 2 * v:2 * v + 4, :], B[:, 2 * v:2 * v + 4, :],
                                      ACT.Gelu_apprx_tanh).then_inc(gelu_ready, 1)
                for v in range(2):
                    if i == FIRST["rg"] + 5 + v:
                        for n in (2 * v, 2 * v + 1):
                            sc.wait_ge(y_ready, n + 1)
                            sc.activation(y_hi[:, 2 * n:2 * n + 2, :], A[:, 2 * n:2 * n + 2, :], ACT.Copy).then_inc(y_hi_ready, 1)
                for pnl in range(2):
                    if i == FIRST["rgo"] + 2 * pnl + 2:
                        acc_ready(FIRST["rgo"] + 2 * pnl + 1)
                        if pnl == 0:
                            sc.wait_ge(y_lo_ready, 4)
                        for t in range(T2):
                            u = USE["rgo"] + 2 * pnl + t
                            sc.activation(mrg[:, t, pnl * 512:(pnl + 1) * 512], acc(u)[:, :], ACT.Copy).then_inc(acc_free[u % 4], 1)
                for pnl in range(4):
                    if i == FIRST["mg"] + 2 * pnl + 2:
                        acc_ready(FIRST["mg"] + 2 * pnl + 1)
                        if pnl == 1:
                            sc.wait_ge(m_gated, 2)
                        for t in range(T2):
                            u = USE["mg"] + 2 * pnl + t
                            dst = mtt[:, t, :] if pnl < 2 else mt1[:, t, (pnl - 2) * 512:(pnl - 1) * 512]
                            sc.activation(dst, acc(u)[:, :], ACT.Tanh, scale=0.5).then_inc(acc_free[u % 4], 1)
                for v in range(2):
                    if i == FIRST["wo"] - 1 + 2 * v:
                        for j in (2 * v, 2 * v + 1):
                            m = MISC["mT"] + j
                            sc.wait_ge(misc_done, misc_count(m))
                            sc.activation(h_hi[:, 2 * j:2 * j + 2, :], misc(m)[:, :].rearrange("p (c s) -> p c s", c=2),
                                          ACT.Copy, scale=0.5).then_inc(evac_hi, 1)
                for pnl in range(2):
                    if i == FIRST["wo"] + 2 * pnl + 2:
                        for t in range(T2):
                            sc.wait_ge(x1_ready, 2 * pnl + t + 1)
                            c = 2 * pnl + t
                            sc.activation(scr[:, 512 * c:512 * (c + 1)], xs[:, t, pnl * 512:(pnl + 1) * 512], ACT.Square,
                                          accum_out=ss[:, NORM_X1, c:c + 1]).then_inc(squares, 1)
                if i == FIRST["wo"] + 4:
                    for j in range(4):
                        unit_hi(MISC["hT2"] + j, j, G2)
                j = i - FIRST["gu"] - 1
                if 0 <= j < FF:
                    acc_ready(FIRST["gu"] + j)
                    if j >= 2:
                        sc.wait_ge(a_prod, j - 1)
                    sc.activation(sg[:, j % 2, :], acc(USE["gu"] + j)[:, 0:S], ACT.Silu).then_inc(silu_ready, 1)
                if 1 <= j <= FF:
                    sc.wait_ge(a_prod, j)
                    sc.activation(a_hi[:, j - 1, :], sa[:, (j - 1) % 2, :], ACT.Copy).then_inc(a_hi_ready, 1)

        @block.vector
        def _(ve):
            chain = [0]

            def link(ins):
                chain[0] += 1
                ins.then_inc(dve_chain, 1)
                ve.wait_ge(dve_chain, chain[0])

            def split_lo(i):
                if i >= NSLOT:
                    return
                ve.wait_ge(hi_ready, i + 1)
                ve.tensor_tensor(w_lo[:, i % HL, :], raw[:, i % RAW, :], f(w_hi[:, i % HL, :]),
                                 ALU.subtract).then_inc(lo_ready, 1)

            def mean(n, scale):
                p, w = NORM_SHAPE[n]
                ve.tensor_scalar(ms[0:p, n, 0:w], ss[0:p, n, 0:w], scale, EPS, ALU.mult, ALU.add).then_inc(ms_ready, 1)

            ve.wait_ge(x1_in, 16)
            ve.scalar_tensor_tensor(out=scr[:, 3072:4096], in0=xs[:, 1, :], scalar=1.0, in1=xs[:, 1, :], op0=ALU.mult,
                                    op1=ALU.mult, accum_out=ss[:, NORM_X, 1:2]).then_inc(dve_chain, 1)
            chain[0] += 1
            ve.wait_ge(dve_chain, chain[0])
            ve.wait_ge(squares, 1)
            mean(NORM_X, 1.0 / D)
            ve.wait_ge(rs_ready, NORM_X + 1)
            ve.wait_ge(x_in, 16)
            ve.tensor_scalar(xn[:, 0, :], xs[:, 0, :], rs[:, NORM_X, 0:1], None, ALU.mult).then_inc(xn_ready, 1)
            split_lo(0)
            ve.wait_ge(prm_in, 16)

            def softplus():
                lam = prm[:, LAM:LAM + 8]
                link(ve.tensor_scalar(sm[:, 2, :], lam, -1.0, None, ALU.mult))
                ve.tensor_tensor(sm[:, 0, :], sm[:, 2, :], lam, ALU.min).then_inc(sp_neg, 1)
                link(ve.tensor_scalar(sm[:, 3, :], sm[:, 2, :], 0.0, None, ALU.max))
                ve.wait_ge(sp_exp, 1)
                link(ve.tensor_scalar(sm[:, 4, :], sm[:, 1, :], 2.0, None, ALU.add))
                link(ve.reciprocal(sm[:, 5, :], sm[:, 4, :]))
                link(ve.tensor_tensor(sm[:, 6, :], sm[:, 1, :], sm[:, 5, :], ALU.mult))
                link(ve.tensor_tensor(sm[:, 7, :], sm[:, 6, :], sm[:, 6, :], ALU.mult))
                link(ve.tensor_scalar(sm[:, 8, :], sm[:, 7, :], 1.0 / 17, 1.0 / 15, ALU.mult, ALU.add))
                for c in (13, 11, 9, 7, 5, 3, 1):
                    link(ve.tensor_tensor(sm[:, 9, :], sm[:, 8, :], sm[:, 7, :], ALU.mult))
                    link(ve.tensor_scalar(sm[:, 8, :], sm[:, 9, :], 1.0 / c, None, ALU.add))
                link(ve.scalar_tensor_tensor(out=sm[:, 9, :], in0=sm[:, 8, :], scalar=2.0, in1=sm[:, 6, :],
                                             op0=ALU.mult, op1=ALU.mult))
                link(ve.tensor_tensor(sm[:, 4, :], sm[:, 9, :], sm[:, 3, :], ALU.add))
                link(ve.tensor_scalar(sm[:, 12, :], sm[:, 4, :], -4.0, None, ALU.mult))
                ve.tensor_scalar(sm[:, 10, :], prm[:, BA:BA + 8], 0.5, None, ALU.mult)
                ve.tensor_scalar(sm[:, 11, :], prm[:, BI:BI + 8], 0.5, None, ALU.mult).then_inc(sp_ready, 1)

            def unit_lo(m, j, gain_col, count):
                ve.wait_ge(evac_hi, count)
                for e in range(2):
                    c = 2 * j + e
                    ins = ve.scalar_tensor_tensor(out=h_lo[:, c, :], in0=misc(m)[:, e * S:(e + 1) * S],
                                                  scalar=prm[:, gain_col + c:gain_col + c + 1],
                                                  in1=f(h_hi[:, c, :]), op0=ALU.mult, op1=ALU.subtract)
                ins.then_inc(misc_free[m % 4], 1)

            for j in range(4):
                unit_lo(MISC["xT"] + j, j, G1, j + 1)
            ve.wait_ge(small_hi, 1)
            ve.tensor_tensor(sw_lo[:, :], smraw, f(sw_hi[:, :]), ALU.subtract).then_inc(small_lo, 1)
            split_lo(1)
            ve.wait_ge(consts, 4)
            ve.tensor_copy(identr[:, :], ident[:, :])
            ve.tensor_copy(maskr[:, :], maskf[:, :]).then_inc(masks_r, 1)
            for j in range(2):
                ve.memset(zc[j][:, :, 512:520], 0.0)

            def sums(n, count):
                for t in range(T2):
                    ve.wait_ge(squares, count + t + 1)
                    ins = ve.tensor_reduce(ss[:, n, 8 * t:8 * t + 8], sq[:, t, :].rearrange("p (h d) -> p h d", d=DH),
                                           AX, ALU.add).then_inc(sq_summed, 1)
                ve.wait_ge(sq_summed, 2 * (n - NORM_K) + 2)
                mean(n, 1.0 / DH)

            def rs_wide(n, t, shape):
                r = rs[:, n, 8 * t:8 * t + 8]
                for _ in range(len(shape) - 2):
                    r = r.unsqueeze(len(r.shape))
                return r.broadcast_to(shape)

            for i in range(NSLOT + 2):
                h = i - HEAD0
                if h >= 3 and h % 2 == 1 and h <= HEADS + 1:
                    pair = (h - 3) // 2
                    ve.wait_ge(o_hi, pair + 1)
                    ve.tensor_tensor(oT[:, pair, 1, :], o_bank, f(oT[:, pair, 0, :]),
                                     ALU.subtract).then_inc(o_ready, 1)
                if 0 <= h < HEADS:
                    m = MISC["att"] + 4 * h
                    for t in range(T2):
                        ve.wait_ge(s_done, 2 * h + t + 1)
                        w = P * (t + 1)
                        ins = ve.tensor_reduce(ast[:, 0, 2 * t:2 * t + 2],
                                               misc(m + t)[:, 0:2 * w].rearrange("p (b c) -> p b c", b=2), AX, ALU.max)
                    link(ins)
                    ve.tensor_scalar(ast[:, 1, :], ast[:, 0, :], -SCALE, None, ALU.mult).then_inc(max_ready, 1)
                split_lo(i + AHEAD)
                if 0 <= h < HEADS:
                    wait_misc_read(ve, MISC["att"] + 4 * h)
                    wait_misc_read(ve, MISC["att"] + 4 * h + 1)
                    link(ve.reciprocal(ast[:, 3, :], ast[:, 2, :]))
                    ve.tensor_tensor(ast[:, 4, :].rearrange("p (t b) -> p t b", t=T2),
                                     ast[:, 3, :].rearrange("p (t b) -> p t b", t=T2),
                                     gates[:, :, 1:3, h], ALU.mult).then_inc(scale_ready, 1)

                if i == 5:
                    softplus()
                if i == 3:
                    m = MISC["ngT"]
                    ve.wait_ge(misc_done, misc_count(m))
                    ve.tensor_scalar(gates[:, :, :, :].rearrange("p t b h -> p (t b h)"), misc(m)[:, 0:96], 1.0, 0.5,
                                     ALU.add, ALU.mult).then_inc(misc_free[m % 4], 1)
                for j, name in enumerate(("kc", "vc")):
                    if i == FIRST[name] + 1:
                        ve.wait_ge(slot_done, FIRST[name] + 1)
                        if j == 0:
                            ve.wait_ge(misc_done, 4)
                        u = USE[name]
                        pos = (PK, PV)[j]
                        last = None
                        for e in range(2):
                            for par in range(2):
                                for gp in range(2):
                                    src = acc(u)[64 * gp:64 * gp + 64, :].rearrange("p (n l r) -> p n l r", l=8, r=2)[:, :, :, par]
                                    pv = prm[64 * par:64 * par + 64, pos + 8 * e:pos + 8 * e + 8].unsqueeze(1).broadcast_to([64, 32, 8])
                                    dst = zc[j][64 * par:64 * par + 64, e, 256 * gp:256 * gp + 256].rearrange("p (n l) -> p n l", l=8)
                                    last = (dst, src, pv)
                                    if (e, par, gp) != (1, 1, 1):
                                        ve.tensor_tensor(dst, src, pv, ALU.add)
                        ve.tensor_tensor(*last, ALU.add).then_inc(zc_ready, 1)
                        ve.wait_ge(z_hi_ready, j + 1)
                        ve.tensor_tensor(z_lo[j], zc[j].rearrange("p e n -> p (e n)"), f(z_hi[j]),
                                         ALU.subtract).then_inc(z_lo_ready, 1)
                        ve.wait_ge(zc_ready, j + 1)
                        ve.engine_nop().then_inc(acc_free[u % 4], 1)
                if i == FIRST["kk"] + 2:
                    sums(NORM_K, 1)
                    ve.wait_ge(rs_ready, NORM_K + 1)
                    for t in range(T2):
                        u = USE["kk"] + t
                        ve.wait_ge(acc_free[u % 4], u // 4 + 1)
                        ve.tensor_tensor(kn[:, t, :].rearrange("p (c e d) -> p c e d", c=8, e=2),
                                         kz[:, t, :].rearrange("p (c d) -> p c d", c=8).unsqueeze(2).broadcast_to([P, 8, 2, DH]),
                                         rs_wide(NORM_K, t, [P, 8, 2, DH]), ALU.mult).then_inc(kn_ready, 1)
                if i == FIRST["vv"] + 2:
                    for g in range(GROUPS):
                        m = MISC["kT"] + g
                        ve.wait_ge(evac_hi, 4 + g + 1)
                        for b in range(2):
                            ins = ve.scalar_tensor_tensor(out=k_ll[:, g, b * S:(b + 1) * S], in0=misc(m)[:, b * S:(b + 1) * S],
                                                          scalar=prm[:, KN + 1 + b:KN + 2 + b],
                                                          in1=f(k_hh[:, g, b * S:(b + 1) * S]), op0=ALU.mult, op1=ALU.subtract)
                        ins.then_inc(misc_free[m % 4], 1)
                for pnl in range(2):
                    if i == FIRST["q"] + 2 * pnl + 2:
                        sums(NORM_Q0 + pnl, 3 + 2 * pnl)
                        ve.wait_ge(rs_ready, NORM_Q0 + pnl + 1)
                        for t in range(T2):
                            u = USE["q"] + 2 * pnl + t
                            ve.wait_ge(acc_free[u % 4], u // 4 + 1)
                            qv = qz[:, t, pnl * 512:(pnl + 1) * 512].rearrange("p (h d) -> p h d", d=DH)
                            ve.tensor_tensor(qv, qv, rs_wide(NORM_Q0 + pnl, t, [P, 8, DH]), ALU.mult).then_inc(qn_ready, 1)
                    if i == FIRST["q"] + 2 * pnl + 4:
                        for v in range(2):
                            m = MISC["qT"] + 2 * pnl + v
                            pr = 4 * pnl + 2 * v
                            ve.wait_ge(evac_hi, 8 + 2 * pnl + v + 1)
                            for e in range(2):
                                ins = ve.scalar_tensor_tensor(out=q_st[64:128, pr:pr + 2, e, :],
                                                              in0=misc(m)[64 * e:64 * e + 64, :].rearrange("p (j s) -> p j s", j=2),
                                                              scalar=prm[0:64, QN:QN + 1], in1=f(q_st[0:64, pr:pr + 2, e, :]),
                                                              op0=ALU.mult, op1=ALU.subtract)
                            ins.then_inc(misc_free[m % 4], 1)
                for j, name in enumerate(("w1k", "w1v")):
                    if i == FIRST[name] + 2:
                        ve.wait_ge(hid_ready, j + 1)
                        ve.engine_nop().then_inc(acc_free[USE[name] % 4], 1)
                    if i == FIRST[name] + 3:
                        m = MISC["hidk"] if j == 0 else MISC["hidv"]
                        ve.wait_ge(hid_hi, j + 1)
                        if j == 0:
                            ins = ve.tensor_tensor(hidk_lo, misc(m)[:, 0:128], f(hidk_hi), ALU.subtract)
                        else:
                            ins = ve.tensor_tensor(hidv_lo.rearrange("p (c j n) -> p c j n", c=8, j=4),
                                                   misc(m)[:, 0:128].rearrange("p (c n) -> p c n", c=8).unsqueeze(2)
                                                   .broadcast_to([P, 8, 4, 16]),
                                                   f(hidv_hi).rearrange("p (c j n) -> p c j n", c=8, j=4), ALU.subtract)
                        ins.then_inc(misc_free[m % 4], 1)
                if i == FIRST["w1v"] + 2:
                    ve.wait_ge(squares, 8)
                    mean(NORM_KC, 1.0 / DH)
                    ve.wait_ge(rs_ready, NORM_KC + 1)
                    ve.tensor_scalar(kcn.rearrange("p (e d) -> p e d", e=2),
                                     misc(MISC["kcn"])[0:64, 0:64].unsqueeze(1).broadcast_to([64, 2, DH]),
                                     rs[0:64, NORM_KC, 0:1], None, ALU.mult).then_inc(misc_free[MISC["kcn"] % 4], 1)
                if i == FIRST["rx"] + 1:
                    m = MISC["kcT"]
                    ve.wait_ge(evac_hi, 13)
                    ve.scalar_tensor_tensor(out=kc_ll, in0=misc(m)[:, 0:64], scalar=prm[:, KN:KN + 1], in1=f(kc_hh),
                                            op0=ALU.mult, op1=ALU.subtract).then_inc(misc_free[m % 4], 1)
                if i == FIRST["rx"] + 2:
                    m = MISC["vrep"]
                    ve.wait_ge(misc_done, misc_count(m))
                    for hf in range(2):
                        ins = ve.tensor_tensor(vcx[:, hf, :, :], misc(m)[:, hf * DH:(hf + 1) * DH].unsqueeze(1).broadcast_to([P, 8, DH]),
                                               bd[:, :].unsqueeze(2).broadcast_to([P, 8, DH]), ALU.mult)
                    ins.then_inc(misc_free[m % 4], 1)
                if i == FIRST["rx"] + 2:
                    m = MISC["cmps"]
                    ve.wait_ge(misc_done, misc_count(m))
                    sc3 = misc(m)[:, :].rearrange("p (c n) -> p c n", n=16)
                    ex3 = cexp.rearrange("p (c n) -> p c n", n=16)
                    link(ve.tensor_reduce(cst[:, 0, :], sc3, AX, ALU.max))
                    link(ve.tensor_scalar(cst[:, 1, :], cst[:, 0, :], -1e30, None, ALU.max))
                    ve.tensor_tensor(ex3, sc3, cst[:, 1, :].unsqueeze(2).broadcast_to([P, 32, 16]), ALU.subtract).then_inc(c_shift, 1)
                    ve.wait_ge(c_exp, 1)
                    link(ve.tensor_reduce(cst[:, 0, :], ex3, AX, ALU.add))
                    link(ve.tensor_scalar(cst[:, 2, :], cst[:, 0, :], 1e-30, None, ALU.max))
                    link(ve.reciprocal(cst[:, 3, :], cst[:, 2, :]))
                    link(ve.tensor_tensor(cst[:, 2, :].rearrange("p (t h) -> p t h", t=T2),
                                          cst[:, 3, :].rearrange("p (t h) -> p t h", t=T2), gates[:, :, 0, :], ALU.mult))
                    ve.tensor_tensor(ex3, ex3, cst[:, 2, :].unsqueeze(2).broadcast_to([P, 32, 16]), ALU.mult).then_inc(misc_free[m % 4], 1)
                if i == HEAD0:
                    m = MISC["pcT"]
                    ve.wait_ge(misc_done, misc_count(m))
                    ve.tensor_copy(pcT[:, :, :].rearrange("p a s -> p (a s)"), misc(m)[:, :]).then_inc(misc_free[m % 4], 1)
                r = i - FIRST["rx"] - 1
                if 0 <= r < 4:
                    ve.wait_ge(conv0, 2 * r + 2)
                    ps = acc(USE["rx"] + r)
                    for s in range(1, CONV):
                        for e in range(2):
                            m = 2 * r + e
                            ins = ve.scalar_tensor_tensor(out=A[:, m, s:S], in0=ps[:, e * S:(e + 1) * S - s],
                                                          scalar=prm[:, CW + 8 * (3 - s) + m:CW + 8 * (3 - s) + m + 1],
                                                          in1=A[:, m, s:S], op0=ALU.mult, op1=ALU.add)
                        if s < CONV - 1:
                            link(ins)
                    ins.then_inc(xr_ready, 1)
                    ve.wait_ge(xr_hi, r + 1)
                    ve.tensor_tensor(y_lo[:, 2 * r:2 * r + 2, :], A[:, 2 * r:2 * r + 2, :], f(y_hi[:, 2 * r:2 * r + 2, :]),
                                     ALU.subtract).then_inc(acc_free[(USE["rx"] + r) % 4], 1)
                r = i - FIRST["rg"] - 1
                if 0 <= r < 2:
                    for n in (2 * r, 2 * r + 1):
                        u = USE["rg"] + 2 * n
                        ve.wait_ge(acc_free[u % 4], u // 4 + 1)
                        for m in (2 * n, 2 * n + 1):
                            ve.tensor_scalar(C[:, m, :], C[:, m, :], 1.0, sm[:, 12, m:m + 1], ALU.add, ALU.mult).then_inc(log_a, 1)
                        ve.wait_ge(acc_free[(u + 1) % 4], (u + 1) // 4 + 1)
                        ve.scalar_tensor_tensor(out=A[:, 2 * n:2 * n + 2, :], in0=Dr[:, 2 * n:2 * n + 2, :], scalar=1.0,
                                                in1=A[:, 2 * n:2 * n + 2, :], op0=ALU.add, op1=ALU.mult).then_inc(gated_x, 1)
                if i == FIRST["rg"] + 4:
                    ve.wait_ge(w_ready, 1)
                    for n in range(4):
                        ve.wait_ge(asq_ready, n + 1)
                        d = Dr[:, 2 * n:2 * n + 2, :]
                        ve.scalar_tensor_tensor(out=d, in0=rgt[:, :].rearrange("p (m s) -> p m s", m=2), scalar=1.0, in1=d,
                                                op0=ALU.add, op1=ALU.mult).then_inc(asq_used, 1)
                if i == FIRST["rg"] + 5 or i == FIRST["rg"] + 6:
                    v = i - FIRST["rg"] - 5
                    if v == 0:
                        ve.wait_ge(root_ready, 1)
                        link(ve.memset(Dr[:, :, 0:1], 0.5))
                    link(ve.tensor_tensor(A[:, 4 * v:4 * v + 4, :], A[:, 4 * v:4 * v + 4, :], Dr[:, 4 * v:4 * v + 4, :], ALU.mult))
                    for m in range(4 * v, 4 * v + 4):
                        ins = ve.tensor_tensor_scan(Dr[:, m, :], C[:, m, :], A[:, m, :], 0.0, ALU.mult, ALU.add)
                    link(ins)
                    for n in (2 * v, 2 * v + 1):
                        ve.wait_ge(gelu_ready, v + 1)
                        ve.tensor_tensor(A[:, 2 * n:2 * n + 2, :], Dr[:, 2 * n:2 * n + 2, :], B[:, 2 * n:2 * n + 2, :],
                                         ALU.mult).then_inc(y_ready, 1)
                    for n in (2 * v, 2 * v + 1):
                        ve.wait_ge(y_hi_ready, n + 1)
                        ve.tensor_tensor(y_lo[:, 2 * n:2 * n + 2, :], A[:, 2 * n:2 * n + 2, :], f(y_hi[:, 2 * n:2 * n + 2, :]),
                                         ALU.subtract).then_inc(y_lo_ready, 1)
                for pnl in range(2):
                    if i == FIRST["mg"] + 2 * pnl + 2:
                        for t in range(T2):
                            u = USE["mg"] + 2 * pnl + t
                            ve.wait_ge(acc_free[u % 4], u // 4 + 1)
                            mv = mrg[:, t, pnl * 512:(pnl + 1) * 512]
                            ve.scalar_tensor_tensor(out=mv, in0=mtt[:, t, :], scalar=1.0, in1=mv, op0=ALU.add,
                                                    op1=ALU.mult).then_inc(m_gated, 1)
                for pnl in range(2):
                    if i == FIRST["nso"] + 2 * pnl + 2:
                        ve.wait_ge(slot_done, FIRST["nso"] + 2 * pnl + 2)
                        ug = USE["mg"] + 4 + 2 * pnl + 1
                        ve.wait_ge(acc_free[ug % 4], ug // 4 + 1)
                        for t in range(T2):
                            u = USE["nso"] + 2 * pnl + t
                            tv = mt1[:, t, pnl * 512:(pnl + 1) * 512]
                            ve.scalar_tensor_tensor(out=tv, in0=tv, scalar=1.0, in1=acc(u)[:, :], op0=ALU.add,
                                                    op1=ALU.mult).then_inc(acc_free[u % 4], 1)
                        for t in range(T2):
                            u = USE["nso"] + 2 * pnl + t
                            ve.wait_ge(acc_free[u % 4], u // 4 + 1)
                            mv, tv = (z[:, t, pnl * 512:(pnl + 1) * 512] for z in (mrg, mt1))
                            ve.tensor_tensor(mv, mv, tv, ALU.add).then_inc(merged, 1)
                for v in range(2):
                    if i == FIRST["wo"] - 1 + 2 * v:
                        for j in (2 * v, 2 * v + 1):
                            m = MISC["mT"] + j
                            ve.wait_ge(evac_hi, 13 + j + 1)
                            ve.scalar_tensor_tensor(out=h_lo[:, 2 * j:2 * j + 2, :], in0=misc(m)[:, :].rearrange("p (c s) -> p c s", c=2),
                                                    scalar=0.5, in1=f(h_hi[:, 2 * j:2 * j + 2, :]), op0=ALU.mult,
                                                    op1=ALU.subtract).then_inc(misc_free[m % 4], 1)
                for pnl in range(2):
                    if i == FIRST["wo"] + 2 * pnl + 2:
                        ve.wait_ge(slot_done, FIRST["wo"] + 2 * pnl + 2)
                        ve.wait_ge(xr_in, 16)
                        for t in range(T2):
                            xv = xs[:, t, pnl * 512:(pnl + 1) * 512]
                            ve.tensor_tensor(xv, acc(USE["wo"] + 2 * pnl + t)[:, :], xv, ALU.add).then_inc(x1_ready, 1)
                        ve.wait_ge(x1_ready, 2 * pnl + 2)
                        for t in range(T2):
                            ve.engine_nop().then_inc(acc_free[(USE["wo"] + 2 * pnl + t) % 4], 1)
                if i == FIRST["wo"] + 4:
                    ve.wait_ge(squares, 12)
                    link(ve.tensor_tensor(ss[:, NORM_X1, 4:6], ss[:, NORM_X1, 0:2], ss[:, NORM_X1, 2:4], ALU.add))
                    ve.tensor_scalar(ms[:, NORM_X1, 0:2], ss[:, NORM_X1, 4:6], 1.0 / D, EPS, ALU.mult, ALU.add).then_inc(ms_ready, 1)
                    ve.wait_ge(rs_ready, NORM_X1 + 1)
                    for t in range(T2):
                        ve.tensor_scalar(xn2[:, t, :], xs[:, t, :], rs[:, NORM_X1, t:t + 1], None, ALU.mult).then_inc(xn_ready, 1)
                    for j in range(4):
                        unit_lo(MISC["hT2"] + j, j, G2, 17 + j + 1)
                j = i - FIRST["gu"] - 1
                if 1 <= j <= FF:
                    ve.wait_ge(a_hi_ready, j)
                    ve.tensor_tensor(a_lo[:, j - 1, :], sa[:, (j - 1) % 2, :], f(a_hi[:, j - 1, :]), ALU.subtract).then_inc(a_lo_ready, 1)
                if 0 <= j < FF:
                    u = USE["gu"] + j
                    ve.wait_ge(silu_ready, j + 1)
                    ve.tensor_tensor(sa[:, j % 2, :], acc(u)[:, S:2 * S], sg[:, j % 2, :], ALU.mult).then_inc(a_prod, 1)
                    ve.wait_ge(a_prod, j + 1)
                    ve.engine_nop().then_inc(acc_free[u % 4], 1)
            for t in range(T2):
                for n in range(2):
                    if 2 * t + n < 3:
                        ve.wait_ge(dn_done, 2 * t + n + 1)
                    else:
                        ve.wait_ge(slot_done, NSLOT)
                    xv = xs[:, t, n * 512:(n + 1) * 512]
                    ve.tensor_tensor(xv, acc(USE["dn"] + 2 * t + n)[:, :], xv, ALU.add).then_inc(res_ready, 1)

        @block.tensor
        def _(pe):
            def three(out_, l_hi, l_lo, r_hi, r_lo, start, stop):
                pe.matmul(out_, l_hi, r_hi, start=start, stop=False)
                pe.matmul(out_, l_hi, r_lo, start=False, stop=False)
                return pe.matmul(out_, l_lo, r_hi, start=False, stop=stop)

            def slot_ready(i):
                pe.wait_ge(lo_ready, i + 1)

            def direct(i, u, a_h, a_l, units=None):
                slot_ready(i)
                wait_acc_free(pe, u)
                s = i % HL
                for mt in range(2):
                    for k in range(KC):
                        if units is not None and mt == 0 and k % 2 == 0:
                            wait_misc_read(pe, units + k // 2)
                        c = k * 256 + mt * P
                        ins = three(acc(u)[:, mt * S:(mt + 1) * S], w_hi[:, s, c:c + P], w_lo[:, s, c:c + P],
                                    a_h[:, k, :], a_l[:, k, :], k == 0, k == KC - 1)
                ins.then_inc(slot_done, 1)

            def panel(i, e, u, a_h, a_l):
                slot_ready(i)
                s = i % HL
                for t in range(T2):
                    if e == 0:
                        wait_acc_free(pe, u + t)
                    for kk in range(4):
                        k = 4 * e + kk
                        w = slice(kk * 512, (kk + 1) * 512)
                        ins = three(acc(u + t)[:, :], a_h(k, t), a_l(k, t), w_hi[:, s, w], w_lo[:, s, w],
                                    k == 0, k == KC - 1)
                ins.then_inc(slot_done, 1)

            def h_of(t_):
                return lambda k, t: t_[:, k, t * P:(t + 1) * P]

            def o_of(e):
                return lambda k, t: oT[:, k, e, t * P:(t + 1) * P]

            def transposed_unit(m, src, j):
                wait_misc_free(pe, m)
                for e in range(2):
                    for t in range(T2):
                        c = 2 * j + e
                        ins = pe.transpose(misc(m)[:, e * S + t * P:e * S + (t + 1) * P], src[:, t, c * P:(c + 1) * P], ident[:, :])
                ins.then_inc(misc_done, 1)

            pe.wait_ge(consts, 4)
            pe.wait_ge(xn_ready, 1)
            pe.wait_ge(xn1_ready, 1)
            for j in range(4):
                transposed_unit(MISC["xT"] + j, xn, j)
            def scores(h):
                g = h // (HEADS // GROUPS)
                m = MISC["att"] + 4 * h
                for t in range(T2):
                    wait_misc_free(pe, m + t)
                    bank = misc(m + t)
                    w = P * (t + 1)
                    q = q_st[:, h // 2, h % 2, t * P:(t + 1) * P]
                    o3 = bank[:, 0:2 * w].rearrange("p (b c) -> p b c", b=2)
                    for n, kt in enumerate((k_hh, k_ll)):
                        pe.matmul(o3, q, kt[:, g, :].rearrange("p (b c) -> p b c", b=2)[:, :, 0:w], start=n == 0, stop=n == 1)
                    pe.matmul(o3[:, :, t * P:(t + 1) * P], identr[:, :],
                              maskr[:, 0:2 * P].rearrange("p (b c) -> p b c", b=2), start=False, stop=True,
                              skip_group_check=True).then_inc(s_done, 1)

            def turn_a(h):
                m = MISC["att"] + 4 * h + 2
                pe.wait_ge(prob_ready, h + 1)
                wait_misc_free(pe, m)
                for b, t, src in ((0, 0, 0), (0, 1, 256), (1, 0, 128), (1, 1, 512)):
                    ins = pe.transpose(misc(m)[:, b * S + t * P:b * S + (t + 1) * P], prob[:, src:src + P], ident[:, :])
                ins.then_inc(ta_done, 1)

            def turn_b(h):
                m = MISC["att"] + 4 * h + 3
                wait_misc_free(pe, m)
                if h >= 2 and h % 2 == 0:
                    pe.wait_ge(o_ready, h // 2)
                for b, src in ((0, 384), (1, 640)):
                    ins = pe.transpose(misc(m)[:, b * P:(b + 1) * P], prob[:, src:src + P], ident[:, :])
                ins.then_inc(tb_done, 1)

            def values(h):
                g = h // (HEADS // GROUPS)
                m = MISC["att"] + 4 * h + 2
                o = o_bank[64 * (h % 2):64 * (h % 2) + 64, :]
                wait_misc_read(pe, m)
                wait_misc_read(pe, m + 1)
                for b in range(2):
                    pe.matmul(o, v_sb[:, 0, b * S + g * DH:b * S + (g + 1) * DH], pTa[:, b * S:(b + 1) * S],
                              start=b == 0, stop=False)
                pe.matmul(o, vcx[:, h // 8, h % 8, :], pcT[:, h // 8, :], start=False, stop=True)
                for b in range(2):
                    ins = pe.matmul(o[:, P:S], v_sb[:, 1, b * S + g * DH:b * S + (g + 1) * DH], pTb[:, b * P:(b + 1) * P],
                                    start=False, stop=True, skip_group_check=True)
                ins.then_inc(o_done, 1)

            for i in range(NSLOT):
                h = i - HEAD0
                if h == 0:
                    m = MISC["pcT"]
                    wait_misc_read(pe, MISC["cmps"])
                    wait_misc_free(pe, m)
                    for hf in range(2):
                        for t in range(T2):
                            ins = pe.transpose(misc(m)[:, hf * S + t * P:hf * S + (t + 1) * P],
                                               cexp[:, t * S + hf * P:t * S + (hf + 1) * P], ident[:, :])
                    ins.then_inc(misc_done, 1)
                if 1 <= h <= HEADS:
                    turn_a(h - 1)
                if 0 <= h < HEADS:
                    scores(h)
                if 1 <= h <= HEADS:
                    turn_b(h - 1)
                for name in ("kc", "vc", "rx", "ry", "gu"):
                    r = i - FIRST[name]
                    if 0 <= r < dict(ORDER)[name]:
                        units = {FIRST["kc"]: MISC["xT"], FIRST["gu"]: MISC["hT2"]}.get(i)
                        direct(i, USE[name] + r, h_hi, h_lo, units)
                for name in ("kk", "vv", "q", "rgo", "mg", "nso", "wo"):
                    r = i - FIRST[name]
                    if 0 <= r < dict(ORDER)[name]:
                        src = {"rgo": (h_of(y_hi), h_of(y_lo)), "nso": (o_of(0), o_of(1))}.get(name, (h_of(h_hi), h_of(h_lo)))
                        if name == "rgo" and r < 2:
                            pe.wait_ge(y_lo_ready, 2 * r + 2)
                        if name == "nso" and r == 0:
                            pe.wait_ge(o_ready, HEADS // 2)
                        if name == "wo" and r < 2:
                            wait_misc_read(pe, MISC["mT"] + 2 * r + 1)
                        panel(i, r % 2, USE[name] + r // 2 * 2, *src)
                for j, name in enumerate(("w1k", "w1v")):
                    r = i - FIRST[name]
                    if 0 <= r < 2:
                        u = USE[name]
                        slot_ready(i)
                        if r == 0:
                            wait_acc_free(pe, u)
                            pe.wait_ge(z_lo_ready, j + 1)
                        for lp in range(8):
                            at = r * 520 + 8 * r + lp
                            cols = slice(at, at + 8 * 63 + 1, 8)
                            w = slice(lp * 256, (lp + 1) * 256)
                            ins = three(acc(u)[0:64, 0:256], z_hi[j][:, cols], z_lo[j][:, cols],
                                        w_hi[:, i % HL, w], w_lo[:, i % HL, w], r == 0 and lp == 0, r == 1 and lp == 7)
                        ins.then_inc(slot_done, 1)
                r = i - FIRST["rg"]
                if 0 <= r < 2:
                    slot_ready(i)
                    for nn in range(2):
                        n = 2 * r + nn
                        pe.wait_ge(acc_free[(USE["rx"] + n) % 4], (USE["rx"] + n) // 4 + 1)
                        for kind in range(2):
                            u = USE["rg"] + 2 * n + kind
                            wait_acc_free(pe, u)
                            for dt in range(2):
                                for c in range(2):
                                    w = ((nn * 2 + kind) * 2 + c) * 256 + dt * P
                                    ins = three(acc(u)[:, dt * S:(dt + 1) * S], w_hi[:, i % HL, w:w + P], w_lo[:, i % HL, w:w + P],
                                                y_hi[:, 2 * n + c, :], y_lo[:, 2 * n + c, :], c == 0, c == 1)
                            ins.then_inc(slot_done if (nn, kind) == (1, 1) else rg_done, 1)
                r = i - FIRST["dn"]
                if 0 <= r < FF // 2:
                    slot_ready(i)
                    pe.wait_ge(a_lo_ready, 2 * r + 2)
                    for t in range(T2):
                        for n in range(2):
                            u = USE["dn"] + 2 * t + n
                            if r == 0:
                                wait_acc_free(pe, u)
                            if r == FF // 2 - 1 and 2 * t + n > 0:
                                ins.then_inc(dn_done, 1)
                            for kk in range(2):
                                k = 2 * r + kk
                                w = slice(kk * 1024 + n * 512, kk * 1024 + (n + 1) * 512)
                                ins = three(acc(u)[:, :], a_hi[:, k, t * P:(t + 1) * P], a_lo[:, k, t * P:(t + 1) * P],
                                            w_hi[:, i % HL, w], w_lo[:, i % HL, w], k == 0, k == FF - 1)
                    ins.then_inc(slot_done, 1)

                if i == 1:
                    m = MISC["ng"]
                    pe.wait_ge(small_lo, 1)
                    wait_misc_free(pe, m)
                    for k in range(KC):
                        c = NG_W + 48 * k
                        ins = three(misc(m)[0:48, 0:S], sw_hi[:, c:c + 48], sw_lo[:, c:c + 48], h_hi[:, k, :], h_lo[:, k, :],
                                    k == 0, k == KC - 1)
                    ins.then_inc(misc_done, 1)
                if i == 2:
                    m = MISC["ngT"]
                    wait_misc_read(pe, MISC["ng"])
                    wait_misc_free(pe, m)
                    for t in range(T2):
                        ins = pe.transpose(misc(m)[:, 48 * t:48 * t + 48], gtmp[:, t * P:(t + 1) * P], ident[0:48, 0:48])
                    ins.then_inc(misc_done, 1)
                if 1 <= h <= HEADS:
                    values(h - 1)
                if i == FIRST["vv"] + 1:
                    pe.wait_ge(kn_ready, 2)
                    for g in range(GROUPS):
                        m = MISC["kT"] + g
                        wait_misc_free(pe, m)
                        for b in range(2):
                            for t in range(T2):
                                c = (4 * b + g) * P
                                ins = pe.transpose(misc(m)[:, b * S + t * P:b * S + (t + 1) * P], kn[:, t, c:c + P], ident[:, :])
                        ins.then_inc(misc_done, 1)
                for pnl in range(2):
                    if i == FIRST["q"] + 2 * pnl + 3:
                        pe.wait_ge(qn_ready, 2 * pnl + 2)
                        for v in range(2):
                            m = MISC["qT"] + 2 * pnl + v
                            wait_misc_free(pe, m)
                            for jj in range(2):
                                for t in range(T2):
                                    c = (4 * pnl + 2 * v + jj) * P
                                    ins = pe.transpose(misc(m)[:, jj * S + t * P:jj * S + (t + 1) * P], qz[:, t, c:c + P], ident[:, :])
                            ins.then_inc(misc_done, 1)
                if i == FIRST["w1v"] or i == FIRST["rx"]:
                    j = 0 if i == FIRST["w1v"] else 1
                    m = MISC["hidk"] if j == 0 else MISC["hidv"]
                    pe.wait_ge(hid_ready, j + 1)
                    wait_misc_free(pe, m)
                    for c in range(2):
                        ins = pe.transpose(misc(m)[:, 64 * c:64 * c + 64], hid[j][:, c * P:(c + 1) * P], ident[0:64, 0:64])
                    ins.then_inc(misc_done, 1)
                if i == FIRST["w1v"] + 1:
                    m = MISC["kcn"]
                    wait_misc_read(pe, MISC["hidk"])
                    wait_misc_free(pe, m)
                    for c in range(2):
                        w = slice(W2K + 64 * c, W2K + 64 * c + 64)
                        l = slice(64 * c, 64 * c + 64)
                        ins = three(misc(m)[0:64, 0:64], hidk_hi[:, l], hidk_lo[:, l], sw_hi[:, w], sw_lo[:, w], c == 0, c == 1)
                    ins.then_inc(misc_done, 1)
                if i == FIRST["rx"]:
                    m = MISC["kcT"]
                    wait_misc_read(pe, MISC["kcn"])
                    wait_misc_free(pe, m)
                    pe.transpose(misc(m)[:, 0:64], kcn, ident[0:64, 0:64]).then_inc(misc_done, 1)
                if i == FIRST["rx"] + 1:
                    wait_misc_read(pe, MISC["hidv"])
                    m = MISC["vrep"]
                    wait_misc_free(pe, m)
                    for hf in range(2):
                        for c in range(2):
                            w = slice(W2V + 64 * c, W2V + 64 * c + 64)
                            l = slice(256 * c + P * hf, 256 * c + P * (hf + 1))
                            ins = three(misc(m)[:, DH * hf:DH * (hf + 1)], hidv_hi[:, l], hidv_lo[:, l], sw_hi[:, w], sw_lo[:, w],
                                        c == 0, c == 1)
                    ins.then_inc(misc_done, 1)
                if i == FIRST["rx"] + 1:
                    m = MISC["cmps"]
                    wait_misc_read(pe, MISC["kcT"])
                    wait_misc_read(pe, MISC["qT"] + 3)
                    pe.wait_ge(masks_r, 1)
                    wait_misc_free(pe, m)
                    for t in range(T2):
                        for hh in range(HEADS):
                            g = hh // (HEADS // GROUPS)
                            c = (t * HEADS + hh) * 16
                            for n, kt in enumerate((kc_hh, kc_ll)):
                                pe.matmul(misc(m)[:, c:c + 16], q_st[:, hh // 2, hh % 2, t * P:(t + 1) * P], kt[:, g * 16:(g + 1) * 16],
                                          start=(t, hh, n) == (0, 0, 0), stop=n == 1, skip_group_check=True)
                    for t in range(T2):
                        ins = pe.matmul(misc(m)[:, t * S:(t + 1) * S].rearrange("p (h c) -> p h c", c=16), identr[:, :],
                                        maskr[:, 2 * P + 16 * t:2 * P + 16 * t + 16].unsqueeze(1).broadcast_to([P, HEADS, 16]),
                                        start=False, stop=True, skip_group_check=True)
                    ins.then_inc(misc_done, 1)
                for v in range(2):
                    if i == FIRST["nso"] + 2 + 2 * v:
                        pe.wait_ge(merged, 2 * v + 2)
                        for j in (2 * v, 2 * v + 1):
                            transposed_unit(MISC["mT"] + j, mrg, j)
                if i == FIRST["wo"] + 3:
                    pe.wait_ge(xn_ready, 3)
                    for j in range(4):
                        transposed_unit(MISC["hT2"] + j, xn2, j)


def _chunks(w, n):
    return w.reshape(-1, 128, n).transpose(1, 0, 2)


def _direct(w):
    c = _chunks(w, w.shape[1])
    return [c[:, :, 256 * j:256 * (j + 1)].reshape(128, SLOT) for j in range(w.shape[1] // 256)]


def _panels(w):
    c = _chunks(w, w.shape[1])
    return [c[:, 4 * e:4 * e + 4, 512 * j:512 * (j + 1)].reshape(128, SLOT)
            for j in range(w.shape[1] // 512) for e in range(2)]


def lay_out(inputs):
    a = {k: np.asarray(v) for k, v in inputs.items()}
    w_in = a["w_in"][0]
    at = np.cumsum([0, 1024, 1024, 1024] + [256] * 6 + [48, 2048])
    rx, ry, q, kc, vc, ks, vs, kw, vw, ng, mg = [w_in[:, at[i]:at[i + 1]] for i in range(11)]

    def pairs(w):
        return w.reshape(1024, 2, 2, 64).transpose(0, 2, 1, 3).reshape(1024, 256)

    slots = []
    slots += _direct(pairs(kc)) + _direct(pairs(vc))
    slots += _panels(np.concatenate([ks, kw], 1)) + _panels(np.concatenate([vs, vw], 1)) + _panels(q)
    for w1 in (a["cmp_k_w1"][0], a["cmp_v_w1"][0]):
        c = _chunks(w1, 256)
        slots += [c[:, 8 * e:8 * e + 8].reshape(128, SLOT) for e in range(2)]
    slots += _direct(rx)
    rg = np.stack([a["rg_wa"][0], a["rg_wi"][0]], 1).reshape(4, 2, 2, 128, 256)
    for r in range(2):
        slots.append(rg[2 * r:2 * r + 2].transpose(3, 0, 1, 2, 4).reshape(128, SLOT))
    slots += _direct(ry) + _panels(a["w_rg_out"][0]) + _panels(mg) + _panels(a["w_nsa_out"][0]) + _panels(a["w_o"][0])
    gu = np.concatenate([a["w_gate"][0].reshape(1024, FF, 1, 128), a["w_up"][0].reshape(1024, FF, 1, 128)], 2)
    slots += _direct(gu.reshape(1024, 2 * DFF))
    dn = _chunks(a["w_down"][0], 1024)
    slots += [dn[:, 2 * r:2 * r + 2].reshape(128, SLOT) for r in range(FF // 2)]
    stream = np.ascontiguousarray(np.stack(slots, 0))

    def cols(v):
        return v.reshape(-1, 128).T

    small = np.concatenate([_chunks(ng, 48).reshape(128, 384), _chunks(a["cmp_k_w2"][0], 64).reshape(128, 128),
                            _chunks(a["cmp_v_w2"][0], 64).reshape(128, 128)], 1)

    def both(v):
        return np.concatenate([v, v]).reshape(128, 1)

    params = np.concatenate(
        [cols(a["norm1"][0]), cols(a["norm2"][0])] + [cols(a["conv_w"][0, k]) for k in range(4)]
        + [cols(a["conv_b"][0]), cols(a["rg_ba"][0]), cols(a["rg_bi"][0]), cols(a["rg_lambda"][0]), both(a["q_norm"][0])]
        + [both(a["k_norm"][0, b]) for b in range(3)]
        + [a[n][0].reshape(16, 128).T for n in ("cmp_pos_k", "cmp_pos_v")], 1)
    return {"x_dram": np.ascontiguousarray(a["x"][0]), "stream_dram": stream,
            "small_dram": np.ascontiguousarray(small), "params_dram": np.ascontiguousarray(params)}


def kernel(**inputs):
    import concourse.bacc as _bacc
    from concourse.bass_utils import run_bass_kernel_spmd as _run

    nc = _bacc.Bacc("TRN2", target_bir_lowering=False, num_devices=1)
    arrays = lay_out(inputs)
    args = [nc.dram_tensor(n, a.shape, mybir.dt.from_np(a.dtype), kind="ExternalInput").ap() for n, a in arrays.items()]
    res = nc.dram_tensor("out_dram", (S, D), F32, kind="ExternalOutput").ap()
    hybrid_layer(nc, *args, res)
    r = _run(nc, [arrays], core_ids=[0])
    return r.results[0]["out_dram"].reshape(1, S, D)
```

```python
from contextlib import ExitStack

import numpy as np

import concourse.bass as bass
from concourse import mybir

F32 = mybir.dt.float32
F32R = mybir.dt.float32r
ALU = mybir.AluOpType
ACT = mybir.ActivationFunctionType
AX = mybir.AxisListType.X

P = 128
S = 256
D = 1024
T2 = S // P
KC = D // P
HEADS, GROUPS, DH = 16, 4, 64
DFF = 2816
FF = DFF // P
CONV = 4
EPS = 1e-6
NEG = -float(2 ** 120)
SCALE = DH ** -0.5
SLOT = 2048

ORDER = [("rx", 4), ("kk", 2), ("rg", 2), ("kc", 1), ("vc", 1), ("qa", 2), ("w1k", 2), ("qb", 2), ("w1v", 2), ("vv", 2),
         ("ry", 4), ("rgo", 4), ("mg", 8), ("nso", 4), ("wo", 4), ("gu", FF), ("dn", FF // 2)]
FIRST = {}
NSLOT = 0
for _name, _n in ORDER:
    FIRST[_name] = NSLOT
    NSLOT += _n
ACC_ORDER = [("rx", 4), ("kk", 2), ("rg", 8), ("kc", 1), ("vc", 1), ("qa", 2), ("w1k", 1), ("qb", 2), ("w1v", 1),
             ("vv", 2), ("ry", 4), ("rgo", 4), ("mg", 8), ("nso", 4), ("wo", 4), ("gu", FF), ("dn", 4)]
USE = {}
_u = 0
for _name, _n in ACC_ORDER:
    USE[_name] = _u
    _u += _n
MISC_ORDER = [("xT", 4), ("ng", 1), ("ngT", 1), ("kT", 4), ("qTa", 2), ("hidk", 1), ("kcn", 1), ("kcT", 1),
              ("qTb", 2), ("hidv", 1), ("cmps", 1), ("vrep", 1), ("pcT", 1), ("att", 4 * HEADS), ("mT", 4), ("hT2", 4)]
MISC = {}
_u = 0
for _name, _n in MISC_ORDER:
    MISC[_name] = _u
    _u += _n

RAW = 3
HL = 3
AHEAD = HL - 1
RG_A = FIRST["rg"] + 3
RG_SQ = RG_A + 2
RG_ROOT = RG_SQ + 1
RG_SCAN = (RG_ROOT + 1, RG_ROOT + 3)
SPLIT_LAST = {FIRST["rg"], FIRST["rg"] + 1, FIRST["nso"] + 3, FIRST["wo"] + 3, FIRST["wo"] + 4}
HEAD0 = FIRST["ry"]
G1, G2, CW, CB, BA, BI, LAM, QN, KN, PK, PV, NPRM = 0, 8, 16, 48, 56, 64, 72, 80, 81, 84, 100, 116
NG_W, W2K, W2V, NSMALL = 0, 384, 512, 640


def hybrid_layer(nc, x, stream, small_w, params, out):
    ctx = ExitStack()
    with ctx:
        def sb(name, shape, dt=F32):
            return ctx.enter_context(nc.sbuf_tensor(name, shape, dt))

        def sem(name):
            return ctx.enter_context(nc.semaphore(name))

        raw = sb("raw", [P, RAW, SLOT])
        w_hi = sb("w_hi", [P, HL, SLOT], F32R)
        w_lo = sb("w_lo", [P, HL, SLOT], F32R)
        xs = sb("xs", [P, T2, D])
        scr = sb("scr", [P, 6144])
        h_hi = sb("h_hi", [P, KC, S], F32R)
        h_lo = sb("h_lo", [P, KC, S], F32R)
        act = sb("act", [P, 12416], F32R)
        v_sb = sb("v_sb", [P, T2, 512])
        pbuf = sb("pbuf", [P, 1536])
        vcx = sb("vcx", [P, 2, 8, DH])
        pcT = sb("pcT", [P, 2, S])
        rgt = sb("rgt", [P, 512])
        cmpr = sb("cmpr", [P, 1280 + 128], F32R)
        sw_hi = sb("sw_hi", [P, NSMALL], F32R)
        sw_lo = sb("sw_lo", [P, NSMALL], F32R)
        prm = sb("prm", [P, NPRM])
        ident = sb("ident", [P, P])
        identr = sb("identr", [P, P], F32R)
        maskf = sb("maskf", [P, 2 * P + 2 * 16])
        maskr = sb("maskr", [P, 2 * P + 2 * 16], F32R)
        bd = sb("bd", [P, 8])
        half = sb("half", [P, 16])
        ss = sb("ss", [P, 6, 16])
        ms = sb("ms", [P, 6, 16])
        rs = sb("rs", [P, 6, 16])
        gates = sb("gates", [P, T2, 3, HEADS])
        gtmp = sb("gtmp", [48, S])
        sm = sb("sm", [P, 13, 8])
        cst = sb("cst", [P, 4, 32])
        ast = sb("ast", [P, 5, 4])
        psum = [ctx.enter_context(nc.psum_tensor(f"bank{b}", [P, 512], F32)) for b in range(8)]

        xn = scr[:, 0:2048].rearrange("p (t n) -> p t n", t=T2)
        smraw = scr[:, 5504:6144]
        xsq = scr[:, 2048:3072]
        zc = scr[:, 2048:2048 + 1040].rearrange("p (e n) -> p e n", e=2)
        kz = v_sb
        kn = scr[:, 2048:4096].rearrange("p (t n) -> p t n", t=T2)
        qz = scr[:, 2048:4096].rearrange("p (t n) -> p t n", t=T2)
        sq = pbuf[:, 0:1024].rearrange("p (t n) -> p t n", t=T2)
        hid = [v_sb[0:64, 0, 256 * j:256 * (j + 1)] for j in range(2)]
        kcn = v_sb[0:64, 1, 0:P]
        kcsq = v_sb[0:64, 1, P:P + 64]
        cexp = scr[:, 2048:2560]
        A = scr[:, 0:2048].rearrange("p (m s) -> p m s", m=KC)
        B = scr[:, 2048:4096].rearrange("p (m s) -> p m s", m=KC)
        C = scr[:, 4096:6144].rearrange("p (m s) -> p m s", m=KC)
        Dr = xs[:, :, :].rearrange("p t (m s) -> p (t m) s", s=S)
        asq = [(vcx[:, :, :, :].rearrange("p a b d -> p (a b d)").rearrange("p (m s) -> p m s", s=S), 0, 4),
               (pcT[:, :, :], 4, 6), (rgt[:, :].rearrange("p (m s) -> p m s", s=S), 6, 8)]
        mrg = scr[:, 0:2048].rearrange("p (t n) -> p t n", t=T2)
        mt1 = scr[:, 2048:4096].rearrange("p (t n) -> p t n", t=T2)
        mtt = scr[:, 4096:5120].rearrange("p (t n) -> p t n", t=T2)
        xn2 = scr[:, 4096:6144].rearrange("p (t n) -> p t n", t=T2)
        sg = scr[:, 0:512].rearrange("p (b n) -> p b n", b=2)
        sa = scr[:, 512:1024].rearrange("p (b n) -> p b n", b=2)
        k_hh = act[:, 0:2048].rearrange("p (g c) -> p g c", g=GROUPS)
        k_ll = act[:, 2048:4096].rearrange("p (g c) -> p g c", g=GROUPS)
        q_st = act[:, 4096:8192].rearrange("p (j e s) -> p j e s", j=8, e=2)
        oT = q_st
        y_hi = act[:, 8192:10240].rearrange("p (m s) -> p m s", m=KC)
        y_lo = act[:, 10240:12288].rearrange("p (m s) -> p m s", m=KC)
        z_hi = [act[:, 8192 + 2080 * j:8192 + 2080 * j + 1040] for j in range(2)]
        z_lo = [act[:, 8192 + 2080 * j + 1040:8192 + 2080 * (j + 1)] for j in range(2)]
        a_hi = act[:, 0:FF * S].rearrange("p (m s) -> p m s", m=FF)
        a_lo = act[:, FF * S:2 * FF * S].rearrange("p (m s) -> p m s", m=FF)
        hidk_hi, hidk_lo = cmpr[:, 0:128], cmpr[:, 128:256]
        hidv_hi, hidv_lo = cmpr[:, 256:768], cmpr[:, 768:1280]
        kc_hh, kc_ll = cmpr[:, 1280:1344], cmpr[:, 1344:1408]
        prob = pbuf[:, 0:768]
        pTa = pbuf[:, 768:1280]
        pTb = pbuf[:, 1280:1536]

        def f(ap):
            return ap.bitcast(F32)

        def acc(u):
            return psum[u % 4]

        def misc(m):
            return psum[4 + m % 4]

        o_bank = misc(MISC["att"] + 3)[:, S:2 * S]

        def misc_count(m):
            return m + 1 if m < MISC["att"] else m + 1 - 4 * HEADS

        landed = [sem(f"landed{i}") for i in range(RAW)]
        x_in, x1_in, small_in, prm_in, xr_in = sem("x_in"), sem("x1_in"), sem("small_in"), sem("prm_in"), sem("xr_in")
        hi_ready, lo_ready = sem("hi_ready"), sem("lo_ready")
        slot_done = sem("slot_done")
        acc_free = [sem(f"acc_free{i}") for i in range(4)]
        misc_done = sem("misc_done")
        s_done, ta_done, tb_done = sem("s_done"), sem("ta_done"), sem("tb_done")
        misc_free = [sem(f"misc_free{i}") for i in range(4)]
        consts, masks_r = sem("consts"), sem("masks_r")
        small_hi, small_lo = sem("small_hi"), sem("small_lo")
        squares, ms_ready, rs_ready = sem("squares"), sem("ms_ready"), sem("rs_ready")
        evac_hi = sem("evac_hi")
        xn_ready, xn1_ready = sem("xn_ready"), sem("xn1_ready")
        zc_ready, z_hi_ready, z_lo_ready = sem("zc_ready"), sem("z_hi_ready"), sem("z_lo_ready")
        k_copied, q_copied, kn_ready, qn_ready = sem("k_copied"), sem("q_copied"), sem("kn_ready"), sem("qn_ready")
        sq_summed = sem("sq_summed")
        gate_tanh, gates_ready = sem("gate_tanh"), sem("gates_ready")
        hid_ready, hid_hi, hid_lo = sem("hid_ready"), sem("hid_hi"), sem("hid_lo")
        kcn_ready, c_shift, c_exp, c_ready = sem("kcn_ready"), sem("c_shift"), sem("c_exp"), sem("c_ready")
        max_ready, scale_ready, prob_ready = sem("max_ready"), sem("scale_ready"), sem("prob_ready")
        pT_ready = sem("pT_ready")
        o_done, o_hi, o_ready = sem("o_done"), sem("o_hi"), sem("o_ready")
        sp_neg, sp_exp, sp_ready = sem("sp_neg"), sem("sp_exp"), sem("sp_ready")
        conv0, xr_ready, xr_hi, xr_lo = sem("conv0"), sem("xr_ready"), sem("xr_hi"), sem("xr_lo")
        rg_done, ta_ready, ti_ready = sem("rg_done"), sem("ta_ready"), sem("ti_ready")
        gated_x, log_a, w_ready, a_ready = sem("gated_x"), sem("log_a"), sem("w_ready"), sem("a_ready")
        asq_ready, asq_used, root_ready, ry_ready = sem("asq_ready"), sem("asq_used"), sem("root_ready"), sem("ry_ready")
        gelu_ready, y_ready, y_hi_ready, y_lo_ready = sem("gelu_ready"), sem("y_ready"), sem("y_hi_ready"), sem("y_lo_ready")
        ya_ready, g0_tanh, m_gated, g1_ready = sem("ya_ready"), sem("g0_tanh"), sem("m_gated"), sem("g1_ready")
        merged = sem("merged")
        x1_ready, silu_ready, a_prod, a_hi_ready, a_lo_ready = sem("x1_ready"), sem("silu_ready"), sem("a_prod"), sem("a_hi_ready"), sem("a_lo_ready")
        wo_half = sem("wo_half")
        dn_done, res_ready, stored = sem("dn_done"), sem("res_ready"), sem("stored")
        act_chain, dve_chain, pool_chain = sem("act_chain"), sem("dve_chain"), sem("pool_chain")

        def wait_acc_free(eng, u):
            if u >= 4:
                eng.wait_ge(acc_free[u % 4], u // 4)

        def wait_misc_free(eng, m):
            if m >= 4:
                eng.wait_ge(misc_free[m % 4], m // 4)

        def wait_misc_read(eng, m):
            eng.wait_ge(misc_free[m % 4], m // 4 + 1)

        NORM_X, NORM_K, NORM_Q0, NORM_Q1, NORM_KC, NORM_X1 = range(6)
        NORM_SHAPE = [(P, 2), (P, 16), (P, 16), (P, 16), (64, 1), (P, 2)]

        block = ctx.enter_context(nc.Block())

        @block.sync
        def _(sp):
            sp.dma_start(xs[:, 0, :], x[0:P, :]).then_inc(x_in, 16)
            for i in range(NSLOT):
                if i >= RAW:
                    sp.wait_ge(lo_ready, i - RAW + 1)
                sp.dma_start(raw[:, i % RAW, :], stream[i, :, :]).then_inc(landed[i % RAW], 16)
            for t in range(T2):
                for n in range(2):
                    sp.wait_ge(res_ready, 2 * t + n + 1)
                    sp.dma_start(out[t * P:(t + 1) * P, n * 512:(n + 1) * 512],
                                 xs[:, t, n * 512:(n + 1) * 512]).then_inc(stored, 16)
            sp.wait_ge(stored, 16 * 4)

        @block.gpsimd
        def _(pool):
            pool.memset(ident[:, :], 0.0).then_inc(pool_chain, 1)
            pool.memset(maskf[:, :], 0.0).then_inc(pool_chain, 1)
            pool.memset(bd[:, :], 1.0).then_inc(pool_chain, 1)
            pool.memset(half[:, :], -0.5).then_inc(pool_chain, 1)
            pool.wait_ge(pool_chain, 4)
            pool.affine_select(out=ident[:, :], in_=ident[:, :], compare_op=ALU.not_equal, fill=1.0,
                               base=0, pattern=[[-1, P]], channel_multiplier=1).then_inc(consts, 1)
            cm = maskf[:, 0:2 * P].rearrange("p (b j) -> p b j", b=2)
            pool.affine_select(out=cm, in_=cm, compare_op=ALU.is_ge, fill=NEG, base=0,
                               pattern=[[0, 2], [-1, P]], channel_multiplier=1).then_inc(consts, 1)
            cc = maskf[:, 2 * P:].rearrange("p (t c) -> p t c", t=T2)
            pool.affine_select(out=cc, in_=cc, compare_op=ALU.is_ge, fill=NEG, base=-31,
                               pattern=[[P, T2], [-16, 16]], channel_multiplier=1).then_inc(consts, 1)
            pool.affine_select(out=bd[:, :], in_=bd[:, :], compare_op=ALU.is_ge, fill=0.0, base=0,
                               pattern=[[-16, 8]], channel_multiplier=1).then_inc(pool_chain, 1)
            pool.wait_ge(pool_chain, 5)
            pool.affine_select(out=bd[:, :], in_=bd[:, :], compare_op=ALU.is_ge, fill=0.0, base=15,
                               pattern=[[16, 8]], channel_multiplier=-1).then_inc(consts, 1)

            def rsqrt(n):
                p, w = NORM_SHAPE[n]
                pool.wait_ge(ms_ready, n + 1)
                pool.tensor_tensor(rs[0:p, n, 0:w], ms[0:p, n, 0:w], half[0:p, 0:w], ALU.pow).then_inc(rs_ready, 1)

            for n in (NORM_X, NORM_K, NORM_Q0, NORM_Q1, NORM_KC):
                rsqrt(n)
            for h in range(HEADS):
                pool.wait_ge(scale_ready, h + 1)
                for j, (a, b) in enumerate(((0, 128), (128, 256), (256, 512), (512, 768))):
                    ins = pool.tensor_scalar(prob[:, a:b], prob[:, a:b], ast[:, 4, j:j + 1], 1.0, ALU.mult, ALU.mult)
                ins.then_inc(prob_ready, 1)
                if h == 12:
                    pool.wait_ge(y_lo_ready, 4)
                    pool.dma_start(xs[:, :, :], x.rearrange("(t p) n -> p t n", p=P)).then_inc(xr_in, 16)
            for t in range(T2):
                pool.wait_ge(ms_ready, NORM_X1 + t + 1)
                pool.tensor_tensor(rs[:, NORM_X1, t:t + 1], ms[:, NORM_X1, t:t + 1], half[:, 0:1], ALU.pow).then_inc(rs_ready, 1)

        @block.scalar
        def _(sc):
            sc.dma_start(xs[:, 1, :], x[P:2 * P, :]).then_inc(x1_in, 16)
            sc.dma_start(prm[:, :], params[:, :]).then_inc(prm_in, 16)
            sc.dma_start(smraw, small_w[:, :]).then_inc(small_in, 16)

            def split_hi(i):
                if i >= NSLOT:
                    return
                sc.wait_ge(landed[i % RAW], 16 * (i // RAW + 1))
                if i >= HL:
                    sc.wait_ge(slot_done, i - HL + 1)
                sc.activation(w_hi[:, i % HL, :], raw[:, i % RAW, :], ACT.Copy).then_inc(hi_ready, 1)

            def acc_ready(slot):
                sc.wait_ge(slot_done, slot + 1)

            sc.wait_ge(x_in, 16)
            sc.activation(xsq, xs[:, 0, :], ACT.Square, accum_out=ss[:, NORM_X, 0:1]).then_inc(squares, 1)
            sc.wait_ge(rs_ready, NORM_X + 1)
            sc.wait_ge(x1_in, 16)
            sc.activation(xn[:, 1, :], xs[:, 1, :], ACT.Copy, scale=rs[:, NORM_X, 1:2]).then_inc(xn1_ready, 1)
            split_hi(0)

            def unit_hi(m, j, gain_col):
                sc.wait_ge(misc_done, misc_count(m))
                for e in range(2):
                    c = 2 * j + e
                    ins = sc.activation(h_hi[:, c, :], misc(m)[:, e * S:(e + 1) * S], ACT.Copy,
                                        scale=prm[:, gain_col + c:gain_col + c + 1])
                ins.then_inc(evac_hi, 1)

            sc.wait_ge(prm_in, 16)
            for j in range(4):
                unit_hi(MISC["xT"] + j, j, G1)
            sc.wait_ge(small_in, 16)
            sc.activation(sw_hi[:, :], smraw, ACT.Copy).then_inc(small_hi, 1)
            split_hi(1)

            def squares_and_copy(name, first_slot, use, dst, n, copied):
                acc_ready(first_slot + 1)
                if n > NORM_K:
                    sc.wait_ge(sq_summed, 2 * (n - NORM_K))
                for t in range(T2):
                    sc.activation(sq[:, t, :], acc(use + t)[:, :], ACT.Square).then_inc(squares, 1)
                for t in range(T2):
                    sc.activation(dst[:, t, :], acc(use + t)[:, :], ACT.Copy).then_inc(acc_free[(use + t) % 4], 1)

            for i in range(NSLOT + 2):
                h = i - HEAD0
                if h >= 3 and h % 2 == 1 and h <= HEADS + 1:
                    pair = (h - 3) // 2
                    sc.wait_ge(o_done, 2 * pair + 2)
                    sc.activation(oT[:, pair, 0, :], o_bank, ACT.Copy).then_inc(o_hi, 1)
                if 1 <= h <= HEADS:
                    m = MISC["att"] + 4 * (h - 1)
                    sc.wait_ge(ta_done, h)
                    if h >= 2:
                        sc.wait_ge(o_done, h - 1)
                    sc.activation(pTa, misc(m + 2)[:, :], ACT.Copy).then_inc(misc_free[(m + 2) % 4], 1)
                    sc.wait_ge(tb_done, h)
                    sc.activation(pTb, misc(m + 3)[:, 0:256], ACT.Copy).then_inc(misc_free[(m + 3) % 4], 1)
                if i not in SPLIT_LAST:
                    split_hi(i + AHEAD)
                if 0 <= h < HEADS:
                    m = MISC["att"] + 4 * h
                    sc.wait_ge(max_ready, h + 1)
                    if h >= 1:
                        sc.wait_ge(tb_done, h)
                    for j, (a, b) in enumerate(((0, 128), (128, 256), (256, 512), (512, 768))):
                        bank = misc(m + j // 2)
                        off = 0 if j % 2 == 0 else (b - a)
                        ins = sc.activation(prob[:, a:b], bank[:, off:off + b - a], ACT.Exp, bias=ast[:, 1, j:j + 1],
                                            scale=SCALE, accum_out=ast[:, 2, j:j + 1])
                        if j % 2 == 1:
                            ins.then_inc(misc_free[(m + j // 2) % 4], 1)

                if i == 2:
                    sc.wait_ge(misc_done, misc_count(MISC["ng"]))
                    sc.activation(gtmp[:, :], misc(MISC["ng"])[0:48, 0:S], ACT.Tanh,
                                  scale=0.5).then_inc(misc_free[MISC["ng"] % 4], 1)
                if i == 0:
                    sc.wait_ge(sp_neg, 1)
                    sc.activation(sm[:, 1, :], sm[:, 0, :], ACT.Exp).then_inc(sp_exp, 1)
                for j, name in enumerate(("kc", "vc")):
                    if i == FIRST[name] + 1:
                        sc.wait_ge(zc_ready, j + 1)
                        sc.activation(z_hi[j], zc.rearrange("p e n -> p (e n)"), ACT.Copy).then_inc(z_hi_ready, 1)
                if i == FIRST["kk"] + 2:
                    squares_and_copy("kk", FIRST["kk"], USE["kk"], kz, NORM_K, k_copied)
                if i == FIRST["vv"] + 2:
                    acc_ready(FIRST["vv"] + 1)
                    for t in range(T2):
                        u = USE["vv"] + t
                        sc.activation(v_sb[:, t, :], acc(u)[:, :], ACT.Copy).then_inc(acc_free[u % 4], 1)
                if i == FIRST["kk"] + 4:
                    for g in range(GROUPS):
                        m = MISC["kT"] + g
                        sc.wait_ge(misc_done, misc_count(m))
                        for b in range(2):
                            ins = sc.activation(k_hh[:, g, b * S:(b + 1) * S], misc(m)[:, b * S:(b + 1) * S], ACT.Copy,
                                                scale=prm[:, KN + 1 + b:KN + 2 + b])
                        ins.then_inc(evac_hi, 1)
                for pnl, name in enumerate(("qa", "qb")):
                    if i == FIRST[name] + 2:
                        if pnl == 0:
                            sc.wait_ge(z_lo_ready, 2)
                        squares_and_copy("q", FIRST[name], USE[name],
                                         qz[:, :, pnl * 512:(pnl + 1) * 512], NORM_Q0 + pnl, q_copied)
                    if i == FIRST[name] + 4:
                        for v in range(2):
                            m = MISC[("qTa", "qTb")[pnl]] + v
                            sc.wait_ge(misc_done, misc_count(m))
                            pr = 4 * pnl + 2 * v
                            for e in range(2):
                                ins = sc.activation(q_st[0:64, pr:pr + 2, e, :],
                                                    misc(m)[64 * e:64 * e + 64, :].rearrange("p (j s) -> p j s", j=2),
                                                    ACT.Copy, scale=prm[64 * e:64 * e + 64, QN:QN + 1])
                            ins.then_inc(evac_hi, 1)
                for j, name in enumerate(("w1k", "w1v")):
                    if i == FIRST[name] + 2:
                        acc_ready(FIRST[name] + 1)
                        sc.activation(hid[j], acc(USE[name])[0:64, 0:256], ACT.Gelu_apprx_tanh).then_inc(hid_ready, 1)
                    if i == FIRST[name] + 3:
                        m = MISC["hidk"] if j == 0 else MISC["hidv"]
                        sc.wait_ge(misc_done, misc_count(m))
                        if j == 0:
                            ins = sc.activation(hidk_hi, misc(m)[:, 0:128], ACT.Copy)
                        else:
                            ins = sc.activation(hidv_hi.rearrange("p (c j n) -> p c j n", c=8, j=4),
                                                misc(m)[:, 0:128].rearrange("p (c n) -> p c n", c=8).unsqueeze(2)
                                                .broadcast_to([P, 8, 4, 16]), ACT.Copy)
                        ins.then_inc(hid_hi, 1)
                if i == FIRST["w1k"] + 4:
                    sc.wait_ge(misc_done, misc_count(MISC["kcn"]))
                    sc.activation(kcsq, misc(MISC["kcn"])[0:64, 0:64], ACT.Square,
                                  accum_out=ss[0:64, NORM_KC, 0:1]).then_inc(squares, 1)
                if i == FIRST["w1k"] + 5:
                    sc.wait_ge(misc_done, misc_count(MISC["kcT"]))
                    sc.activation(kc_hh, misc(MISC["kcT"])[:, 0:64], ACT.Copy, scale=prm[:, KN:KN + 1]).then_inc(evac_hi, 1)
                if i == HEAD0 - 1:
                    sc.wait_ge(c_shift, 1)
                    sc.activation(cexp, cexp, ACT.Exp, scale=SCALE).then_inc(c_exp, 1)
                r = i - FIRST["rx"] - 2
                if 0 <= r < 4:
                    sc.wait_ge(xr_ready, r + 1)
                    sc.activation(y_hi[:, 2 * r:2 * r + 2, :], A[:, 2 * r:2 * r + 2, :], ACT.Copy).then_inc(xr_hi, 1)
                r = i - FIRST["rx"] - 1
                if 0 <= r < 4:
                    acc_ready(FIRST["rx"] + r)
                    for e in range(2):
                        m = 2 * r + e
                        ins = sc.activation(A[:, m, :], acc(USE["rx"] + r)[:, e * S:(e + 1) * S], ACT.Identity,
                                            scale=prm[:, CW + 24 + m:CW + 25 + m], bias=prm[:, CB + m:CB + m + 1])
                        ins.then_inc(conv0, 1)
                for n in range(4):
                    if i == FIRST["rg"] + n // 2 + n % 2:
                        if n == 0:
                            sc.wait_ge(sp_ready, 1)
                        for kind in range(2):
                            u = USE["rg"] + 2 * n + kind
                            if n % 2 == 1 and kind == 1:
                                acc_ready(FIRST["rg"] + n // 2)
                            else:
                                sc.wait_ge(rg_done, 3 * (n // 2) + 2 * (n % 2) + kind + 1)
                            for e in range(2):
                                m = 2 * n + e
                                dst = (C, Dr)[kind]
                                ins = sc.activation(dst[:, m, :], acc(u)[:, e * S:(e + 1) * S], ACT.Tanh, scale=0.5,
                                                    bias=sm[:, 10 + kind, m:m + 1])
                            ins.then_inc(acc_free[u % 4], 1)
                if i == RG_A:
                    sc.wait_ge(log_a, 8)
                    sc.wait_ge(gated_x, 4)
                    for e, (buf, a, b) in enumerate(asq):
                        sc.activation(buf, C[:, a:b, :], ACT.Exp, scale=2.0).then_inc(asq_ready, 1)
                    sc.activation(Dr[:, :, :], C[:, :, :], ACT.Tanh, scale=-1.0).then_inc(w_ready, 1)
                    sc.wait_ge(w_ready, 1)
                    sc.wait_ge(asq_ready, 3)
                    sc.activation(C[:, :, :], C[:, :, :], ACT.Exp).then_inc(a_ready, 1)
                    sc.wait_ge(a_ready, 1)
                if i == RG_ROOT:
                    sc.wait_ge(asq_used, 3)
                    sc.activation(Dr[:, :, :], Dr[:, :, :], ACT.Sqrt, scale=0.25).then_inc(root_ready, 1)
                r = i - FIRST["ry"] - 1
                if 0 <= r < 4:
                    acc_ready(FIRST["ry"] + r)
                    u = USE["ry"] + r
                    sc.activation(B[:, 2 * r:2 * r + 2, :], acc(u)[:, :].rearrange("p (m s) -> p m s", m=2),
                                  ACT.Copy).then_inc(acc_free[u % 4], 1)
                    if r % 2 == 1:
                        sc.wait_ge(acc_free[u % 4], u // 4 + 1)
                        v = r - 1
                        sc.activation(B[:, 2 * v:2 * v + 4, :], B[:, 2 * v:2 * v + 4, :],
                                      ACT.Gelu_apprx_tanh).then_inc(gelu_ready, 1)
                for v in range(2):
                    if i == FIRST["ry"] + 2 + 2 * v:
                        for n in (2 * v, 2 * v + 1):
                            sc.wait_ge(y_ready, n + 1)
                            sc.activation(y_hi[:, 2 * n:2 * n + 2, :], A[:, 2 * n:2 * n + 2, :], ACT.Copy).then_inc(y_hi_ready, 1)
                for pnl in range(2):
                    if i == FIRST["rgo"] + pnl + 3:
                        acc_ready(FIRST["rgo"] + pnl + 2)
                        if pnl == 0:
                            sc.wait_ge(y_lo_ready, 4)
                        for t in range(T2):
                            u = USE["rgo"] + 2 * pnl + t
                            sc.activation(mrg[:, t, pnl * 512:(pnl + 1) * 512], acc(u)[:, :], ACT.Copy).then_inc(acc_free[u % 4], 1)
                for pnl in range(4):
                    if i == FIRST["mg"] + 2 * pnl + 2:
                        acc_ready(FIRST["mg"] + 2 * pnl + 1)
                        if pnl == 1:
                            sc.wait_ge(m_gated, 2)
                        for t in range(T2):
                            u = USE["mg"] + 2 * pnl + t
                            dst = mtt[:, t, :] if pnl < 2 else mt1[:, t, (pnl - 2) * 512:(pnl - 1) * 512]
                            sc.activation(dst, acc(u)[:, :], ACT.Tanh, scale=0.5).then_inc(acc_free[u % 4], 1)
                for v in range(2):
                    if i == FIRST["wo"] - 1 + 2 * v:
                        for j in (2 * v, 2 * v + 1):
                            m = MISC["mT"] + j
                            sc.wait_ge(misc_done, misc_count(m))
                            sc.activation(h_hi[:, 2 * j:2 * j + 2, :], misc(m)[:, :].rearrange("p (c s) -> p c s", c=2),
                                          ACT.Copy, scale=0.5).then_inc(evac_hi, 1)
                for pnl in range(2):
                    if i == FIRST["wo"] + pnl + 3:
                        for t in range(T2):
                            sc.wait_ge(x1_ready, 2 * pnl + t + 1)
                            c = 2 * pnl + t
                            sc.activation(scr[:, 512 * c:512 * (c + 1)], xs[:, t, pnl * 512:(pnl + 1) * 512], ACT.Square,
                                          accum_out=ss[:, NORM_X1, c:c + 1]).then_inc(squares, 1)
                if i == FIRST["wo"] + 4:
                    sc.wait_ge(rs_ready, NORM_X1 + 2)
                    sc.activation(xn2[:, 1, 512:1024], xs[:, 1, 512:1024], ACT.Copy, scale=rs[:, NORM_X1, 1:2]).then_inc(xn1_ready, 1)
                    for j in range(4):
                        unit_hi(MISC["hT2"] + j, j, G2)
                j = i - FIRST["gu"] - 1
                if 0 <= j < FF:
                    acc_ready(FIRST["gu"] + j)
                    if j >= 2:
                        sc.wait_ge(a_prod, j - 1)
                    sc.activation(sg[:, j % 2, :], acc(USE["gu"] + j)[:, 0:S], ACT.Silu).then_inc(silu_ready, 1)
                if 1 <= j <= FF:
                    sc.wait_ge(a_prod, j)
                    sc.activation(a_hi[:, j - 1, :], sa[:, (j - 1) % 2, :], ACT.Copy).then_inc(a_hi_ready, 1)
                if i in SPLIT_LAST:
                    split_hi(i + AHEAD)

        @block.vector
        def _(ve):
            chain = [0]

            def link(ins):
                chain[0] += 1
                ins.then_inc(dve_chain, 1)
                ve.wait_ge(dve_chain, chain[0])

            def split_lo(i):
                if i >= NSLOT:
                    return
                ve.wait_ge(hi_ready, i + 1)
                ve.tensor_tensor(w_lo[:, i % HL, :], raw[:, i % RAW, :], f(w_hi[:, i % HL, :]),
                                 ALU.subtract).then_inc(lo_ready, 1)

            def mean(n, scale):
                p, w = NORM_SHAPE[n]
                ve.tensor_scalar(ms[0:p, n, 0:w], ss[0:p, n, 0:w], scale, EPS, ALU.mult, ALU.add).then_inc(ms_ready, 1)

            ve.wait_ge(x1_in, 16)
            ve.scalar_tensor_tensor(out=scr[:, 3072:4096], in0=xs[:, 1, :], scalar=1.0, in1=xs[:, 1, :], op0=ALU.mult,
                                    op1=ALU.mult, accum_out=ss[:, NORM_X, 1:2]).then_inc(dve_chain, 1)
            chain[0] += 1
            ve.wait_ge(dve_chain, chain[0])
            ve.wait_ge(squares, 1)
            mean(NORM_X, 1.0 / D)
            ve.wait_ge(rs_ready, NORM_X + 1)
            ve.wait_ge(x_in, 16)
            ve.tensor_scalar(xn[:, 0, :], xs[:, 0, :], rs[:, NORM_X, 0:1], None, ALU.mult).then_inc(xn_ready, 1)
            split_lo(0)
            ve.wait_ge(prm_in, 16)

            def softplus():
                lam = prm[:, LAM:LAM + 8]
                link(ve.tensor_scalar(sm[:, 2, :], lam, -1.0, None, ALU.mult))
                ve.tensor_tensor(sm[:, 0, :], sm[:, 2, :], lam, ALU.min).then_inc(sp_neg, 1)
                link(ve.tensor_scalar(sm[:, 3, :], sm[:, 2, :], 0.0, None, ALU.max))
                ve.wait_ge(sp_exp, 1)
                link(ve.tensor_scalar(sm[:, 4, :], sm[:, 1, :], 2.0, None, ALU.add))
                link(ve.reciprocal(sm[:, 5, :], sm[:, 4, :]))
                link(ve.tensor_tensor(sm[:, 6, :], sm[:, 1, :], sm[:, 5, :], ALU.mult))
                link(ve.tensor_tensor(sm[:, 7, :], sm[:, 6, :], sm[:, 6, :], ALU.mult))
                link(ve.tensor_scalar(sm[:, 8, :], sm[:, 7, :], 1.0 / 17, 1.0 / 15, ALU.mult, ALU.add))
                for c in (13, 11, 9, 7, 5, 3, 1):
                    link(ve.tensor_tensor(sm[:, 9, :], sm[:, 8, :], sm[:, 7, :], ALU.mult))
                    link(ve.tensor_scalar(sm[:, 8, :], sm[:, 9, :], 1.0 / c, None, ALU.add))
                link(ve.scalar_tensor_tensor(out=sm[:, 9, :], in0=sm[:, 8, :], scalar=2.0, in1=sm[:, 6, :],
                                             op0=ALU.mult, op1=ALU.mult))
                link(ve.tensor_tensor(sm[:, 4, :], sm[:, 9, :], sm[:, 3, :], ALU.add))
                link(ve.tensor_scalar(sm[:, 12, :], sm[:, 4, :], -4.0, None, ALU.mult))
                ve.tensor_scalar(sm[:, 10, :], prm[:, BA:BA + 8], 0.5, None, ALU.mult)
                ve.tensor_scalar(sm[:, 11, :], prm[:, BI:BI + 8], 0.5, None, ALU.mult).then_inc(sp_ready, 1)

            def unit_lo(m, j, gain_col, count):
                ve.wait_ge(evac_hi, count)
                for e in range(2):
                    c = 2 * j + e
                    ins = ve.scalar_tensor_tensor(out=h_lo[:, c, :], in0=misc(m)[:, e * S:(e + 1) * S],
                                                  scalar=prm[:, gain_col + c:gain_col + c + 1],
                                                  in1=f(h_hi[:, c, :]), op0=ALU.mult, op1=ALU.subtract)
                ins.then_inc(misc_free[m % 4], 1)

            for j in range(4):
                unit_lo(MISC["xT"] + j, j, G1, j + 1)
            ve.wait_ge(small_hi, 1)
            ve.tensor_tensor(sw_lo[:, :], smraw, f(sw_hi[:, :]), ALU.subtract).then_inc(small_lo, 1)
            split_lo(1)
            ve.wait_ge(consts, 4)
            ve.tensor_copy(identr[:, :], ident[:, :])
            ve.tensor_copy(maskr[:, :], maskf[:, :]).then_inc(masks_r, 1)

            def sums(n, count):
                for t in range(T2):
                    ve.wait_ge(squares, count + t + 1)
                    ins = ve.tensor_reduce(ss[:, n, 8 * t:8 * t + 8], sq[:, t, :].rearrange("p (h d) -> p h d", d=DH),
                                           AX, ALU.add).then_inc(sq_summed, 1)
                ve.wait_ge(sq_summed, 2 * (n - NORM_K) + 2)
                mean(n, 1.0 / DH)

            def rs_wide(n, t, shape):
                r = rs[:, n, 8 * t:8 * t + 8]
                for _ in range(len(shape) - 2):
                    r = r.unsqueeze(len(r.shape))
                return r.broadcast_to(shape)

            for i in range(NSLOT + 2):
                h = i - HEAD0
                if h >= 3 and h % 2 == 1 and h <= HEADS + 1:
                    pair = (h - 3) // 2
                    ve.wait_ge(o_hi, pair + 1)
                    ve.tensor_tensor(oT[:, pair, 1, :], o_bank, f(oT[:, pair, 0, :]),
                                     ALU.subtract).then_inc(o_ready, 1)
                if 0 <= h < HEADS:
                    m = MISC["att"] + 4 * h
                    for t in range(T2):
                        ve.wait_ge(s_done, 2 * h + t + 1)
                        w = P * (t + 1)
                        ins = ve.tensor_reduce(ast[:, 0, 2 * t:2 * t + 2],
                                               misc(m + t)[:, 0:2 * w].rearrange("p (b c) -> p b c", b=2), AX, ALU.max)
                    link(ins)
                    ve.tensor_scalar(ast[:, 1, :], ast[:, 0, :], -SCALE, None, ALU.mult).then_inc(max_ready, 1)
                if i == FIRST["kk"] + 3:
                    ve.wait_ge(rs_ready, NORM_K + 1)
                    for t in range(T2):
                        u = USE["kk"] + t
                        ve.wait_ge(acc_free[u % 4], u // 4 + 1)
                        ve.tensor_tensor(kn[:, t, :].rearrange("p (c e d) -> p c e d", c=8, e=2),
                                         kz[:, t, :].rearrange("p (c d) -> p c d", c=8).unsqueeze(2).broadcast_to([P, 8, 2, DH]),
                                         rs_wide(NORM_K, t, [P, 8, 2, DH]), ALU.mult).then_inc(kn_ready, 1)
                for pnl, name in enumerate(("qa", "qb")):
                    if i == FIRST[name] + 3:
                        ve.wait_ge(rs_ready, NORM_Q0 + pnl + 1)
                        for t in range(T2):
                            u = USE[name] + t
                            ve.wait_ge(acc_free[u % 4], u // 4 + 1)
                            qv = qz[:, t, pnl * 512:(pnl + 1) * 512].rearrange("p (h d) -> p h d", d=DH)
                            ve.tensor_tensor(qv, qv, rs_wide(NORM_Q0 + pnl, t, [P, 8, DH]), ALU.mult).then_inc(qn_ready, 1)
                if i not in SPLIT_LAST:
                    split_lo(i + AHEAD)
                if 0 <= h < HEADS:
                    wait_misc_read(ve, MISC["att"] + 4 * h)
                    wait_misc_read(ve, MISC["att"] + 4 * h + 1)
                    link(ve.reciprocal(ast[:, 3, :], ast[:, 2, :]))
                    ve.tensor_tensor(ast[:, 4, :].rearrange("p (t b) -> p t b", t=T2),
                                     ast[:, 3, :].rearrange("p (t b) -> p t b", t=T2),
                                     gates[:, :, 1:3, h], ALU.mult).then_inc(scale_ready, 1)

                if i == 0:
                    softplus()
                if i == 3:
                    m = MISC["ngT"]
                    ve.wait_ge(misc_done, misc_count(m))
                    ve.tensor_scalar(gates[:, :, :, :].rearrange("p t b h -> p (t b h)"), misc(m)[:, 0:96], 1.0, 0.5,
                                     ALU.add, ALU.mult).then_inc(misc_free[m % 4], 1)
                for j, name in enumerate(("kc", "vc")):
                    if i == FIRST[name] + 1:
                        ve.wait_ge(slot_done, FIRST[name] + 1)
                        if j == 0:
                            ve.memset(zc[:, :, 512:520], 0.0)
                        else:
                            ve.wait_ge(z_lo_ready, 1)
                        u = USE[name]
                        pos = (PK, PV)[j]
                        last = None
                        for e in range(2):
                            for par in range(2):
                                for gp in range(2):
                                    src = acc(u)[64 * gp:64 * gp + 64, :].rearrange("p (n l r) -> p n l r", l=8, r=2)[:, :, :, par]
                                    pv = prm[64 * par:64 * par + 64, pos + 8 * e:pos + 8 * e + 8].unsqueeze(1).broadcast_to([64, 32, 8])
                                    dst = zc[64 * par:64 * par + 64, e, 256 * gp:256 * gp + 256].rearrange("p (n l) -> p n l", l=8)
                                    last = (dst, src, pv)
                                    if (e, par, gp) != (1, 1, 1):
                                        ve.tensor_tensor(dst, src, pv, ALU.add)
                        ve.tensor_tensor(*last, ALU.add).then_inc(zc_ready, 1)
                        ve.wait_ge(z_hi_ready, j + 1)
                        ve.tensor_tensor(z_lo[j], zc.rearrange("p e n -> p (e n)"), f(z_hi[j]),
                                         ALU.subtract).then_inc(z_lo_ready, 1)
                        ve.wait_ge(zc_ready, j + 1)
                        ve.engine_nop().then_inc(acc_free[u % 4], 1)
                if i == FIRST["kk"] + 2:
                    sums(NORM_K, 1)
                if i == FIRST["kk"] + 4:
                    for g in range(GROUPS):
                        m = MISC["kT"] + g
                        ve.wait_ge(evac_hi, 4 + g + 1)
                        for b in range(2):
                            ins = ve.scalar_tensor_tensor(out=k_ll[:, g, b * S:(b + 1) * S], in0=misc(m)[:, b * S:(b + 1) * S],
                                                          scalar=prm[:, KN + 1 + b:KN + 2 + b],
                                                          in1=f(k_hh[:, g, b * S:(b + 1) * S]), op0=ALU.mult, op1=ALU.subtract)
                        ins.then_inc(misc_free[m % 4], 1)
                for pnl, name in enumerate(("qa", "qb")):
                    if i == FIRST[name] + 2:
                        sums(NORM_Q0 + pnl, 3 + 2 * pnl)
                    if i == FIRST[name] + 4:
                        for v in range(2):
                            m = MISC[("qTa", "qTb")[pnl]] + v
                            pr = 4 * pnl + 2 * v
                            ve.wait_ge(evac_hi, 8 + 3 * pnl + v + 1)
                            for e in range(2):
                                ins = ve.scalar_tensor_tensor(out=q_st[64:128, pr:pr + 2, e, :],
                                                              in0=misc(m)[64 * e:64 * e + 64, :].rearrange("p (j s) -> p j s", j=2),
                                                              scalar=prm[0:64, QN:QN + 1], in1=f(q_st[0:64, pr:pr + 2, e, :]),
                                                              op0=ALU.mult, op1=ALU.subtract)
                            ins.then_inc(misc_free[m % 4], 1)
                for j, name in enumerate(("w1k", "w1v")):
                    if i == FIRST[name] + 2:
                        ve.wait_ge(hid_ready, j + 1)
                        ve.engine_nop().then_inc(acc_free[USE[name] % 4], 1)
                    if i == FIRST[name] + 3:
                        m = MISC["hidk"] if j == 0 else MISC["hidv"]
                        ve.wait_ge(hid_hi, j + 1)
                        if j == 0:
                            ins = ve.tensor_tensor(hidk_lo, misc(m)[:, 0:128], f(hidk_hi), ALU.subtract)
                        else:
                            ins = ve.tensor_tensor(hidv_lo.rearrange("p (c j n) -> p c j n", c=8, j=4),
                                                   misc(m)[:, 0:128].rearrange("p (c n) -> p c n", c=8).unsqueeze(2)
                                                   .broadcast_to([P, 8, 4, 16]),
                                                   f(hidv_hi).rearrange("p (c j n) -> p c j n", c=8, j=4), ALU.subtract)
                        ins.then_inc(misc_free[m % 4], 1)
                if i == FIRST["w1k"] + 4:
                    ve.wait_ge(squares, 8)
                    mean(NORM_KC, 1.0 / DH)
                    ve.wait_ge(rs_ready, NORM_KC + 1)
                    ve.tensor_scalar(kcn.rearrange("p (e d) -> p e d", e=2),
                                     misc(MISC["kcn"])[0:64, 0:64].unsqueeze(1).broadcast_to([64, 2, DH]),
                                     rs[0:64, NORM_KC, 0:1], None, ALU.mult).then_inc(misc_free[MISC["kcn"] % 4], 1)
                if i == FIRST["w1k"] + 5:
                    m = MISC["kcT"]
                    ve.wait_ge(evac_hi, 11)
                    ve.scalar_tensor_tensor(out=kc_ll, in0=misc(m)[:, 0:64], scalar=prm[:, KN:KN + 1], in1=f(kc_hh),
                                            op0=ALU.mult, op1=ALU.subtract).then_inc(misc_free[m % 4], 1)
                if i == HEAD0:
                    m = MISC["vrep"]
                    ve.wait_ge(misc_done, misc_count(m))
                    for hf in range(2):
                        ins = ve.tensor_tensor(vcx[:, hf, :, :], misc(m)[:, hf * DH:(hf + 1) * DH].unsqueeze(1).broadcast_to([P, 8, DH]),
                                               bd[:, :].unsqueeze(2).broadcast_to([P, 8, DH]), ALU.mult)
                    ins.then_inc(misc_free[m % 4], 1)
                if i == HEAD0 - 1:
                    m = MISC["cmps"]
                    ve.wait_ge(misc_done, misc_count(m))
                    sc3 = misc(m)[:, :].rearrange("p (c n) -> p c n", n=16)
                    ex3 = cexp.rearrange("p (c n) -> p c n", n=16)
                    link(ve.tensor_reduce(cst[:, 0, :], sc3, AX, ALU.max))
                    link(ve.tensor_scalar(cst[:, 1, :], cst[:, 0, :], -1e30, None, ALU.max))
                    ve.tensor_tensor(ex3, sc3, cst[:, 1, :].unsqueeze(2).broadcast_to([P, 32, 16]), ALU.subtract).then_inc(c_shift, 1)
                    ve.wait_ge(c_exp, 1)
                    link(ve.tensor_reduce(cst[:, 0, :], ex3, AX, ALU.add))
                    link(ve.tensor_scalar(cst[:, 2, :], cst[:, 0, :], 1e-30, None, ALU.max))
                    link(ve.reciprocal(cst[:, 3, :], cst[:, 2, :]))
                    link(ve.tensor_tensor(cst[:, 2, :].rearrange("p (t h) -> p t h", t=T2),
                                          cst[:, 3, :].rearrange("p (t h) -> p t h", t=T2), gates[:, :, 0, :], ALU.mult))
                    ve.tensor_tensor(ex3, ex3, cst[:, 2, :].unsqueeze(2).broadcast_to([P, 32, 16]), ALU.mult).then_inc(misc_free[m % 4], 1)
                if i == HEAD0:
                    m = MISC["pcT"]
                    ve.wait_ge(misc_done, misc_count(m))
                    ve.tensor_copy(pcT[:, :, :].rearrange("p a s -> p (a s)"), misc(m)[:, :]).then_inc(misc_free[m % 4], 1)
                r = i - FIRST["rx"] - 2
                if 0 <= r < 4:
                    ve.wait_ge(xr_hi, r + 1)
                    ve.tensor_tensor(y_lo[:, 2 * r:2 * r + 2, :], A[:, 2 * r:2 * r + 2, :], f(y_hi[:, 2 * r:2 * r + 2, :]),
                                     ALU.subtract).then_inc(xr_lo, 1)
                r = i - FIRST["rx"] - 1
                if 0 <= r < 4:
                    ve.wait_ge(conv0, 2 * r + 2)
                    ps = acc(USE["rx"] + r)
                    for s in range(1, CONV):
                        for e in range(2):
                            m = 2 * r + e
                            ins = ve.scalar_tensor_tensor(out=A[:, m, s:S], in0=ps[:, e * S:(e + 1) * S - s],
                                                          scalar=prm[:, CW + 8 * (3 - s) + m:CW + 8 * (3 - s) + m + 1],
                                                          in1=A[:, m, s:S], op0=ALU.mult, op1=ALU.add)
                        if s < CONV - 1:
                            link(ins)
                    ins.then_inc(xr_ready, 1)
                    ve.wait_ge(xr_ready, r + 1)
                    ve.engine_nop().then_inc(acc_free[(USE["rx"] + r) % 4], 1)
                for n in range(4):
                    if i == FIRST["rg"] + n // 2 + 1:
                        u = USE["rg"] + 2 * n
                        ve.wait_ge(acc_free[u % 4], u // 4 + 1)
                        for m in (2 * n, 2 * n + 1):
                            ve.tensor_scalar(C[:, m, :], C[:, m, :], 1.0, sm[:, 12, m:m + 1], ALU.add, ALU.mult).then_inc(log_a, 1)
                        ve.wait_ge(acc_free[(u + 1) % 4], (u + 1) // 4 + 1)
                        ve.scalar_tensor_tensor(out=A[:, 2 * n:2 * n + 2, :], in0=Dr[:, 2 * n:2 * n + 2, :], scalar=1.0,
                                                in1=A[:, 2 * n:2 * n + 2, :], op0=ALU.add, op1=ALU.mult).then_inc(gated_x, 1)
                if i == RG_SQ:
                    ve.wait_ge(w_ready, 1)
                    for e, (buf, a, b) in enumerate(asq):
                        ve.wait_ge(asq_ready, e + 1)
                        ve.scalar_tensor_tensor(out=Dr[:, a:b, :], in0=buf, scalar=1.0, in1=Dr[:, a:b, :],
                                                op0=ALU.add, op1=ALU.mult).then_inc(asq_used, 1)
                for v in range(2):
                    if i == RG_SCAN[v]:
                        if v == 0:
                            ve.wait_ge(root_ready, 1)
                            link(ve.memset(Dr[:, :, 0:1], 0.5))
                        link(ve.tensor_tensor(A[:, 4 * v:4 * v + 4, :], A[:, 4 * v:4 * v + 4, :], Dr[:, 4 * v:4 * v + 4, :], ALU.mult))
                        for m in range(4 * v, 4 * v + 4):
                            ins = ve.tensor_tensor_scan(Dr[:, m, :], C[:, m, :], A[:, m, :], 0.0, ALU.mult, ALU.add)
                        link(ins)
                for v in range(2):
                    if i == FIRST["ry"] + 2 + 2 * v:
                        for n in (2 * v, 2 * v + 1):
                            ve.wait_ge(gelu_ready, v + 1)
                            ve.tensor_tensor(A[:, 2 * n:2 * n + 2, :], Dr[:, 2 * n:2 * n + 2, :], B[:, 2 * n:2 * n + 2, :],
                                             ALU.mult).then_inc(y_ready, 1)
                        for n in (2 * v, 2 * v + 1):
                            ve.wait_ge(y_hi_ready, n + 1)
                            ve.tensor_tensor(y_lo[:, 2 * n:2 * n + 2, :], A[:, 2 * n:2 * n + 2, :], f(y_hi[:, 2 * n:2 * n + 2, :]),
                                             ALU.subtract).then_inc(y_lo_ready, 1)
                for pnl in range(2):
                    if i == FIRST["mg"] + 2 * pnl + 2:
                        for t in range(T2):
                            u = USE["mg"] + 2 * pnl + t
                            ve.wait_ge(acc_free[u % 4], u // 4 + 1)
                            mv = mrg[:, t, pnl * 512:(pnl + 1) * 512]
                            ve.scalar_tensor_tensor(out=mv, in0=mtt[:, t, :], scalar=1.0, in1=mv, op0=ALU.add,
                                                    op1=ALU.mult).then_inc(m_gated, 1)
                for pnl in range(2):
                    if i == FIRST["nso"] + pnl + 3:
                        ve.wait_ge(slot_done, FIRST["nso"] + pnl + 3)
                        ug = USE["mg"] + 4 + 2 * pnl + 1
                        ve.wait_ge(acc_free[ug % 4], ug // 4 + 1)
                        for t in range(T2):
                            u = USE["nso"] + 2 * pnl + t
                            tv = mt1[:, t, pnl * 512:(pnl + 1) * 512]
                            ve.scalar_tensor_tensor(out=tv, in0=tv, scalar=1.0, in1=acc(u)[:, :], op0=ALU.add,
                                                    op1=ALU.mult).then_inc(acc_free[u % 4], 1)
                        for t in range(T2):
                            u = USE["nso"] + 2 * pnl + t
                            ve.wait_ge(acc_free[u % 4], u // 4 + 1)
                            mv, tv = (z[:, t, pnl * 512:(pnl + 1) * 512] for z in (mrg, mt1))
                            ve.tensor_tensor(mv, mv, tv, ALU.add).then_inc(merged, 1)
                for v in range(2):
                    if i == FIRST["wo"] - 1 + 2 * v:
                        for j in (2 * v, 2 * v + 1):
                            m = MISC["mT"] + j
                            ve.wait_ge(evac_hi, 13 + j + 1)
                            ve.scalar_tensor_tensor(out=h_lo[:, 2 * j:2 * j + 2, :], in0=misc(m)[:, :].rearrange("p (c s) -> p c s", c=2),
                                                    scalar=0.5, in1=f(h_hi[:, 2 * j:2 * j + 2, :]), op0=ALU.mult,
                                                    op1=ALU.subtract).then_inc(misc_free[m % 4], 1)
                if i == FIRST["wo"] + 3:
                    ve.wait_ge(slot_done, FIRST["wo"] + 3)
                    ve.wait_ge(xr_in, 16)
                    for t in range(T2):
                        u = USE["wo"] + t
                        ve.tensor_tensor(xs[:, t, 0:512], acc(u)[:, :], xs[:, t, 0:512], ALU.add).then_inc(x1_ready, 1)
                    ve.wait_ge(x1_ready, 2)
                    for t in range(T2):
                        ve.engine_nop().then_inc(acc_free[(USE["wo"] + t) % 4], 1)
                    ve.wait_ge(squares, 10)
                    link(ve.tensor_scalar(ss[:, NORM_X1, 4:6], ss[:, NORM_X1, 0:2], 1.0 / D, EPS, ALU.mult, ALU.add))
                if i == FIRST["wo"] + 4:
                    for t in range(T2):
                        if t == 0:
                            ve.wait_ge(wo_half, 1)
                        else:
                            ve.wait_ge(slot_done, FIRST["wo"] + 4)
                        ve.tensor_tensor(xs[:, t, 512:1024], acc(USE["wo"] + 2 + t)[:, :], xs[:, t, 512:1024], ALU.add).then_inc(x1_ready, 1)
                        ve.wait_ge(squares, 11 + t)
                        ve.tensor_scalar(ms[:, NORM_X1, t:t + 1], ss[:, NORM_X1, 2 + t:3 + t], 1.0 / D, ss[:, NORM_X1, 4 + t:5 + t],
                                         ALU.mult, ALU.add).then_inc(ms_ready, 1)
                        ve.wait_ge(rs_ready, NORM_X1 + t + 1)
                        w = (D, 512)[t]
                        ve.tensor_scalar(xn2[:, t, 0:w], xs[:, t, 0:w], rs[:, NORM_X1, t:t + 1], None, ALU.mult).then_inc(xn_ready, 1)
                    ve.wait_ge(x1_ready, 4)
                    for t in range(T2):
                        ve.engine_nop().then_inc(acc_free[(USE["wo"] + 2 + t) % 4], 1)
                    for j in range(4):
                        unit_lo(MISC["hT2"] + j, j, G2, 17 + j + 1)
                j = i - FIRST["gu"] - 1
                if 1 <= j <= FF:
                    ve.wait_ge(a_hi_ready, j)
                    ve.tensor_tensor(a_lo[:, j - 1, :], sa[:, (j - 1) % 2, :], f(a_hi[:, j - 1, :]), ALU.subtract).then_inc(a_lo_ready, 1)
                if 0 <= j < FF:
                    u = USE["gu"] + j
                    ve.wait_ge(silu_ready, j + 1)
                    ve.tensor_tensor(sa[:, j % 2, :], acc(u)[:, S:2 * S], sg[:, j % 2, :], ALU.mult).then_inc(a_prod, 1)
                    ve.wait_ge(a_prod, j + 1)
                    ve.engine_nop().then_inc(acc_free[u % 4], 1)
                if i in SPLIT_LAST:
                    split_lo(i + AHEAD)
            for t in range(T2):
                for n in range(2):
                    if 2 * t + n < 3:
                        ve.wait_ge(dn_done, 2 * t + n + 1)
                    else:
                        ve.wait_ge(slot_done, NSLOT)
                    xv = xs[:, t, n * 512:(n + 1) * 512]
                    ve.tensor_tensor(xv, acc(USE["dn"] + 2 * t + n)[:, :], xv, ALU.add).then_inc(res_ready, 1)

        @block.tensor
        def _(pe):
            def three(out_, l_hi, l_lo, r_hi, r_lo, start, stop):
                pe.matmul(out_, l_hi, r_hi, start=start, stop=False)
                pe.matmul(out_, l_hi, r_lo, start=False, stop=False)
                return pe.matmul(out_, l_lo, r_hi, start=False, stop=stop)

            def slot_ready(i):
                pe.wait_ge(lo_ready, i + 1)

            def direct(i, u, a_h, a_l, units=None):
                slot_ready(i)
                wait_acc_free(pe, u)
                s = i % HL
                for mt in range(2):
                    for k in range(KC):
                        if units is not None and mt == 0 and k % 2 == 0:
                            wait_misc_read(pe, units + k // 2)
                        c = k * 256 + mt * P
                        ins = three(acc(u)[:, mt * S:(mt + 1) * S], w_hi[:, s, c:c + P], w_lo[:, s, c:c + P],
                                    a_h[:, k, :], a_l[:, k, :], k == 0, k == KC - 1)
                ins.then_inc(slot_done, 1)

            def panel(i, e, u, a_h, a_l, half_done=None, between=None):
                slot_ready(i)
                s = i % HL
                for t in range(T2):
                    if e == 0:
                        wait_acc_free(pe, u + t)
                    for kk in range(4):
                        k = 4 * e + kk
                        w = slice(kk * 512, (kk + 1) * 512)
                        ins = three(acc(u + t)[:, :], a_h(k, t), a_l(k, t), w_hi[:, s, w], w_lo[:, s, w],
                                    k == 0, k == KC - 1)
                    if t == 0 and half_done is not None:
                        ins.then_inc(half_done, 1)
                    if t == 0 and between is not None:
                        between()
                ins.then_inc(slot_done, 1)

            def h_of(t_):
                return lambda k, t: t_[:, k, t * P:(t + 1) * P]

            def o_of(e):
                return lambda k, t: oT[:, k, e, t * P:(t + 1) * P]

            def transposed_unit(m, src, j):
                wait_misc_free(pe, m)
                for e in range(2):
                    for t in range(T2):
                        c = 2 * j + e
                        ins = pe.transpose(misc(m)[:, e * S + t * P:e * S + (t + 1) * P], src[:, t, c * P:(c + 1) * P], ident[:, :])
                ins.then_inc(misc_done, 1)

            def merged_transposed(v):
                pe.wait_ge(merged, 2 * v + 2)
                for j in (2 * v, 2 * v + 1):
                    transposed_unit(MISC["mT"] + j, mrg, j)

            pe.wait_ge(consts, 4)
            pe.wait_ge(xn_ready, 1)
            pe.wait_ge(xn1_ready, 1)
            for j in range(4):
                transposed_unit(MISC["xT"] + j, xn, j)
            def scores(h):
                g = h // (HEADS // GROUPS)
                m = MISC["att"] + 4 * h
                for t in range(T2):
                    wait_misc_free(pe, m + t)
                    bank = misc(m + t)
                    w = P * (t + 1)
                    q = q_st[:, h // 2, h % 2, t * P:(t + 1) * P]
                    o3 = bank[:, 0:2 * w].rearrange("p (b c) -> p b c", b=2)
                    for n, kt in enumerate((k_hh, k_ll)):
                        pe.matmul(o3, q, kt[:, g, :].rearrange("p (b c) -> p b c", b=2)[:, :, 0:w], start=n == 0, stop=n == 1)
                    pe.matmul(o3[:, :, t * P:(t + 1) * P], identr[:, :],
                              maskr[:, 0:2 * P].rearrange("p (b c) -> p b c", b=2), start=False, stop=True,
                              skip_group_check=True).then_inc(s_done, 1)

            def turn_a(h):
                m = MISC["att"] + 4 * h + 2
                pe.wait_ge(prob_ready, h + 1)
                wait_misc_free(pe, m)
                for b, t, src in ((0, 0, 0), (0, 1, 256), (1, 0, 128), (1, 1, 512)):
                    ins = pe.transpose(misc(m)[:, b * S + t * P:b * S + (t + 1) * P], prob[:, src:src + P], ident[:, :])
                ins.then_inc(ta_done, 1)

            def turn_b(h):
                m = MISC["att"] + 4 * h + 3
                wait_misc_free(pe, m)
                if h >= 2 and h % 2 == 0:
                    pe.wait_ge(o_ready, h // 2)
                for b, src in ((0, 384), (1, 640)):
                    ins = pe.transpose(misc(m)[:, b * P:(b + 1) * P], prob[:, src:src + P], ident[:, :])
                ins.then_inc(tb_done, 1)

            def values(h):
                g = h // (HEADS // GROUPS)
                m = MISC["att"] + 4 * h + 2
                o = o_bank[64 * (h % 2):64 * (h % 2) + 64, :]
                wait_misc_read(pe, m)
                wait_misc_read(pe, m + 1)
                for b in range(2):
                    pe.matmul(o, v_sb[:, 0, b * S + g * DH:b * S + (g + 1) * DH], pTa[:, b * S:(b + 1) * S],
                              start=b == 0, stop=False)
                pe.matmul(o, vcx[:, h // 8, h % 8, :], pcT[:, h // 8, :], start=False, stop=True)
                for b in range(2):
                    ins = pe.matmul(o[:, P:S], v_sb[:, 1, b * S + g * DH:b * S + (g + 1) * DH], pTb[:, b * P:(b + 1) * P],
                                    start=False, stop=True, skip_group_check=True)
                ins.then_inc(o_done, 1)

            for i in range(NSLOT):
                h = i - HEAD0
                if h == 0:
                    m = MISC["pcT"]
                    wait_misc_read(pe, MISC["cmps"])
                    wait_misc_free(pe, m)
                    for hf in range(2):
                        for t in range(T2):
                            ins = pe.transpose(misc(m)[:, hf * S + t * P:hf * S + (t + 1) * P],
                                               cexp[:, t * S + hf * P:t * S + (hf + 1) * P], ident[:, :])
                    ins.then_inc(misc_done, 1)
                if 1 <= h <= HEADS:
                    turn_a(h - 1)
                if 0 <= h < HEADS:
                    scores(h)
                if 1 <= h <= HEADS:
                    turn_b(h - 1)
                for name in ("kc", "vc", "rx", "ry", "gu"):
                    r = i - FIRST[name]
                    if 0 <= r < dict(ORDER)[name]:
                        units = {FIRST["rx"]: MISC["xT"], FIRST["gu"]: MISC["hT2"]}.get(i)
                        direct(i, USE[name] + r, h_hi, h_lo, units)
                for name in ("kk", "vv", "qa", "qb", "mg"):
                    r = i - FIRST[name]
                    if 0 <= r < dict(ORDER)[name]:
                        panel(i, r % 2, USE[name] + r // 2 * 2, h_of(h_hi), h_of(h_lo))
                for name in ("rgo", "nso", "wo"):
                    r = i - FIRST[name]
                    if 0 <= r < dict(ORDER)[name]:
                        src = {"rgo": (h_of(y_hi), h_of(y_lo)), "nso": (o_of(0), o_of(1)), "wo": (h_of(h_hi), h_of(h_lo))}[name]
                        if name == "rgo" and r % 2 == 0:
                            pe.wait_ge(y_lo_ready, r + 2)
                        if name == "nso" and r % 2 == 0:
                            pe.wait_ge(o_ready, HEADS // 4 * (r // 2 + 1))
                        if name == "wo" and r % 2 == 0:
                            wait_misc_read(pe, MISC["mT"] + r + 1)
                        between = (lambda: merged_transposed(0)) if (name, r) == ("nso", 3) else None
                        panel(i, r // 2, USE[name] + r % 2 * 2, *src, wo_half if (name, r) == ("wo", 3) else None, between)
                for j, name in enumerate(("w1k", "w1v")):
                    r = i - FIRST[name]
                    if 0 <= r < 2:
                        u = USE[name]
                        slot_ready(i)
                        if r == 0:
                            wait_acc_free(pe, u)
                            pe.wait_ge(z_lo_ready, j + 1)
                        for lp in range(8):
                            at = r * 520 + 8 * r + lp
                            cols = slice(at, at + 8 * 63 + 1, 8)
                            w = slice(lp * 256, (lp + 1) * 256)
                            ins = three(acc(u)[0:64, 0:256], z_hi[j][:, cols], z_lo[j][:, cols],
                                        w_hi[:, i % HL, w], w_lo[:, i % HL, w], r == 0 and lp == 0, r == 1 and lp == 7)
                        ins.then_inc(slot_done, 1)
                r = i - FIRST["rg"]
                if 0 <= r < 2:
                    slot_ready(i)
                    for nn in range(2):
                        n = 2 * r + nn
                        pe.wait_ge(xr_lo, n + 1)
                        for kind in range(2):
                            u = USE["rg"] + 2 * n + kind
                            wait_acc_free(pe, u)
                            for dt in range(2):
                                for c in range(2):
                                    w = ((nn * 2 + kind) * 2 + c) * 256 + dt * P
                                    ins = three(acc(u)[:, dt * S:(dt + 1) * S], w_hi[:, i % HL, w:w + P], w_lo[:, i % HL, w:w + P],
                                                y_hi[:, 2 * n + c, :], y_lo[:, 2 * n + c, :], c == 0, c == 1)
                            ins.then_inc(slot_done if (nn, kind) == (1, 1) else rg_done, 1)
                r = i - FIRST["dn"]
                if 0 <= r < FF // 2:
                    slot_ready(i)
                    pe.wait_ge(a_lo_ready, 2 * r + 2)
                    for t in range(T2):
                        for n in range(2):
                            u = USE["dn"] + 2 * t + n
                            if r == 0:
                                wait_acc_free(pe, u)
                            if r == FF // 2 - 1 and 2 * t + n > 0:
                                ins.then_inc(dn_done, 1)
                            for kk in range(2):
                                k = 2 * r + kk
                                w = slice(kk * 1024 + n * 512, kk * 1024 + (n + 1) * 512)
                                ins = three(acc(u)[:, :], a_hi[:, k, t * P:(t + 1) * P], a_lo[:, k, t * P:(t + 1) * P],
                                            w_hi[:, i % HL, w], w_lo[:, i % HL, w], k == 0, k == FF - 1)
                    ins.then_inc(slot_done, 1)

                if i == 1:
                    m = MISC["ng"]
                    pe.wait_ge(small_lo, 1)
                    wait_misc_free(pe, m)
                    for k in range(KC):
                        c = NG_W + 48 * k
                        ins = three(misc(m)[0:48, 0:S], sw_hi[:, c:c + 48], sw_lo[:, c:c + 48], h_hi[:, k, :], h_lo[:, k, :],
                                    k == 0, k == KC - 1)
                    ins.then_inc(misc_done, 1)
                if i == 2:
                    m = MISC["ngT"]
                    wait_misc_read(pe, MISC["ng"])
                    wait_misc_free(pe, m)
                    for t in range(T2):
                        ins = pe.transpose(misc(m)[:, 48 * t:48 * t + 48], gtmp[:, t * P:(t + 1) * P], ident[0:48, 0:48])
                    ins.then_inc(misc_done, 1)
                if 1 <= h <= HEADS:
                    values(h - 1)
                if i == FIRST["kk"] + 3:
                    pe.wait_ge(kn_ready, 2)
                    for g in range(GROUPS):
                        m = MISC["kT"] + g
                        wait_misc_free(pe, m)
                        for b in range(2):
                            for t in range(T2):
                                c = (4 * b + g) * P
                                ins = pe.transpose(misc(m)[:, b * S + t * P:b * S + (t + 1) * P], kn[:, t, c:c + P], ident[:, :])
                        ins.then_inc(misc_done, 1)
                if i == FIRST["w1k"] + 2 or i == FIRST["w1v"] + 2:
                    j = 0 if i == FIRST["w1k"] + 2 else 1
                    m = MISC["hidk"] if j == 0 else MISC["hidv"]
                    pe.wait_ge(hid_ready, j + 1)
                    wait_misc_free(pe, m)
                    for c in range(2):
                        ins = pe.transpose(misc(m)[:, 64 * c:64 * c + 64], hid[j][:, c * P:(c + 1) * P], ident[0:64, 0:64])
                    ins.then_inc(misc_done, 1)
                if i == FIRST["w1k"] + 3:
                    m = MISC["kcn"]
                    wait_misc_read(pe, MISC["hidk"])
                    wait_misc_free(pe, m)
                    for c in range(2):
                        w = slice(W2K + 64 * c, W2K + 64 * c + 64)
                        l = slice(64 * c, 64 * c + 64)
                        ins = three(misc(m)[0:64, 0:64], hidk_hi[:, l], hidk_lo[:, l], sw_hi[:, w], sw_lo[:, w], c == 0, c == 1)
                    ins.then_inc(misc_done, 1)
                if i == FIRST["w1k"] + 4:
                    m = MISC["kcT"]
                    wait_misc_read(pe, MISC["kcn"])
                    wait_misc_free(pe, m)
                    pe.transpose(misc(m)[:, 0:64], kcn, ident[0:64, 0:64]).then_inc(misc_done, 1)
                for pnl, name in enumerate(("qa", "qb")):
                    if i == FIRST[name] + 3:
                        pe.wait_ge(qn_ready, 2 * pnl + 2)
                        for v in range(2):
                            m = MISC[("qTa", "qTb")[pnl]] + v
                            wait_misc_free(pe, m)
                            for jj in range(2):
                                for t in range(T2):
                                    c = (4 * pnl + 2 * v + jj) * P
                                    ins = pe.transpose(misc(m)[:, jj * S + t * P:jj * S + (t + 1) * P], qz[:, t, c:c + P], ident[:, :])
                            ins.then_inc(misc_done, 1)
                if i == HEAD0 - 2:
                    m = MISC["cmps"]
                    wait_misc_read(pe, MISC["kcT"])
                    wait_misc_read(pe, MISC["qTb"] + 1)
                    pe.wait_ge(masks_r, 1)
                    wait_misc_free(pe, m)
                    for t in range(T2):
                        for hh in range(HEADS):
                            g = hh // (HEADS // GROUPS)
                            c = (t * HEADS + hh) * 16
                            for n, kt in enumerate((kc_hh, kc_ll)):
                                pe.matmul(misc(m)[:, c:c + 16], q_st[:, hh // 2, hh % 2, t * P:(t + 1) * P], kt[:, g * 16:(g + 1) * 16],
                                          start=(t, hh, n) == (0, 0, 0), stop=n == 1, skip_group_check=True)
                    for t in range(T2):
                        ins = pe.matmul(misc(m)[:, t * S:(t + 1) * S].rearrange("p (h c) -> p h c", c=16), identr[:, :],
                                        maskr[:, 2 * P + 16 * t:2 * P + 16 * t + 16].unsqueeze(1).broadcast_to([P, HEADS, 16]),
                                        start=False, stop=True, skip_group_check=True)
                    ins.then_inc(misc_done, 1)
                if i == HEAD0 - 1:
                    wait_misc_read(pe, MISC["hidv"])
                    m = MISC["vrep"]
                    wait_misc_free(pe, m)
                    for hf in range(2):
                        for c in range(2):
                            w = slice(W2V + 64 * c, W2V + 64 * c + 64)
                            l = slice(256 * c + P * hf, 256 * c + P * (hf + 1))
                            ins = three(misc(m)[:, DH * hf:DH * (hf + 1)], hidv_hi[:, l], hidv_lo[:, l], sw_hi[:, w], sw_lo[:, w],
                                        c == 0, c == 1)
                    ins.then_inc(misc_done, 1)
                if i == FIRST["wo"]:
                    merged_transposed(1)
                if i == FIRST["wo"] + 3:
                    pe.wait_ge(xn_ready, 2)
                    for t in range(T2):
                        for j in range(4):
                            m = MISC["hT2"] + j
                            if t == 0:
                                wait_misc_free(pe, m)
                            elif j == 0:
                                pe.wait_ge(xn_ready, 3)
                            elif j == 2:
                                pe.wait_ge(xn1_ready, 2)
                            for e in range(2):
                                c = 2 * j + e
                                ins = pe.transpose(misc(m)[:, e * S + t * P:e * S + (t + 1) * P], xn2[:, t, c * P:(c + 1) * P],
                                                   ident[:, :])
                            if t == 1:
                                ins.then_inc(misc_done, 1)


def _chunks(w, n):
    return w.reshape(-1, 128, n).transpose(1, 0, 2)


def _direct(w):
    c = _chunks(w, w.shape[1])
    return [c[:, :, 256 * j:256 * (j + 1)].reshape(128, SLOT) for j in range(w.shape[1] // 256)]


def _panels(w, halves_first=False):
    c = _chunks(w, w.shape[1])
    n = w.shape[1] // 512
    order = [(j, e) for e in range(2) for j in range(n)] if halves_first else [(j, e) for j in range(n) for e in range(2)]
    return [c[:, 4 * e:4 * e + 4, 512 * j:512 * (j + 1)].reshape(128, SLOT) for j, e in order]


def lay_out(inputs):
    a = {k: np.asarray(v) for k, v in inputs.items()}
    w_in = a["w_in"][0]
    at = np.cumsum([0, 1024, 1024, 1024] + [256] * 6 + [48, 2048])
    rx, ry, q, kc, vc, ks, vs, kw, vw, ng, mg = [w_in[:, at[i]:at[i + 1]] for i in range(11)]

    def pairs(w):
        return w.reshape(1024, 2, 2, 64).transpose(0, 2, 1, 3).reshape(1024, 256)

    q_slots = _panels(q)
    w1 = [[_chunks(a[n][0], 256)[:, 8 * e:8 * e + 8].reshape(128, SLOT) for e in range(2)] for n in ("cmp_k_w1", "cmp_v_w1")]
    rg = np.stack([a["rg_wa"][0], a["rg_wi"][0]], 1).reshape(4, 2, 2, 128, 256)
    slots = _direct(rx) + _panels(np.concatenate([ks, kw], 1))
    slots += [rg[2 * r:2 * r + 2].transpose(3, 0, 1, 2, 4).reshape(128, SLOT) for r in range(2)]
    slots += _direct(pairs(kc)) + _direct(pairs(vc)) + q_slots[:2] + w1[0] + q_slots[2:] + w1[1]
    slots += _panels(np.concatenate([vs, vw], 1)) + _direct(ry) + _panels(a["w_rg_out"][0], True) + _panels(mg)
    slots += _panels(a["w_nsa_out"][0], True) + _panels(a["w_o"][0], True)
    gu = np.concatenate([a["w_gate"][0].reshape(1024, FF, 1, 128), a["w_up"][0].reshape(1024, FF, 1, 128)], 2)
    slots += _direct(gu.reshape(1024, 2 * DFF))
    dn = _chunks(a["w_down"][0], 1024)
    slots += [dn[:, 2 * r:2 * r + 2].reshape(128, SLOT) for r in range(FF // 2)]
    stream = np.ascontiguousarray(np.stack(slots, 0))

    def cols(v):
        return v.reshape(-1, 128).T

    small = np.concatenate([_chunks(ng, 48).reshape(128, 384), _chunks(a["cmp_k_w2"][0], 64).reshape(128, 128),
                            _chunks(a["cmp_v_w2"][0], 64).reshape(128, 128)], 1)

    def both(v):
        return np.concatenate([v, v]).reshape(128, 1)

    params = np.concatenate(
        [cols(a["norm1"][0]), cols(a["norm2"][0])] + [cols(a["conv_w"][0, k]) for k in range(4)]
        + [cols(a["conv_b"][0]), cols(a["rg_ba"][0]), cols(a["rg_bi"][0]), cols(a["rg_lambda"][0]), both(a["q_norm"][0])]
        + [both(a["k_norm"][0, b]) for b in range(3)]
        + [a[n][0].reshape(16, 128).T for n in ("cmp_pos_k", "cmp_pos_v")], 1)
    return {"x_dram": np.ascontiguousarray(a["x"][0]), "stream_dram": stream,
            "small_dram": np.ascontiguousarray(small), "params_dram": np.ascontiguousarray(params)}


def kernel(**inputs):
    import concourse.bacc as _bacc
    from concourse.bass_utils import run_bass_kernel_spmd as _run

    nc = _bacc.Bacc("TRN2", target_bir_lowering=False, num_devices=1)
    arrays = lay_out(inputs)
    args = [nc.dram_tensor(n, a.shape, mybir.dt.from_np(a.dtype), kind="ExternalInput").ap() for n, a in arrays.items()]
    res = nc.dram_tensor("out_dram", (S, D), F32, kind="ExternalOutput").ap()
    hybrid_layer(nc, *args, res)
    r = _run(nc, [arrays], core_ids=[0])
    return r.results[0]["out_dram"].reshape(1, S, D)
```

```python
from contextlib import ExitStack

import numpy as np

import concourse.bass as bass
from concourse import mybir

F32 = mybir.dt.float32
F32R = mybir.dt.float32r
ALU = mybir.AluOpType
ACT = mybir.ActivationFunctionType
AX = mybir.AxisListType.X

P = 128
S = 256
D = 1024
T2 = S // P
KC = D // P
HEADS, GROUPS, DH = 16, 4, 64
DFF = 2816
FF = DFF // P
CONV = 4
EPS = 1e-6
NEG = -float(2 ** 120)
SCALE = DH ** -0.5
SLOT = 2048

ORDER = [("rx", 4), ("kk", 2), ("rg", 2), ("kc", 1), ("vc", 1), ("qa", 2), ("w1k", 2), ("qb", 2), ("w1v", 2), ("vv", 2),
         ("ry", 4), ("rgo", 4), ("mg", 8), ("nso", 4), ("wo", 4), ("gu", FF), ("dn", FF // 2)]
FIRST = {}
NSLOT = 0
for _name, _n in ORDER:
    FIRST[_name] = NSLOT
    NSLOT += _n
ACC_ORDER = [("rx", 4), ("kk", 2), ("rg", 8), ("kc", 1), ("vc", 1), ("qa", 2), ("w1k", 1), ("qb", 2), ("w1v", 1),
             ("vv", 2), ("ry0", 1), ("pcT", 1), ("ry1", 3), ("rgo", 4), ("mg", 8), ("nso", 4), ("wo", 4), ("gu", FF), ("dn", 4)]
USE = {}
_u = 0
for _name, _n in ACC_ORDER:
    USE[_name] = _u
    _u += _n
USE_RY = [USE["ry0"]] + [USE["ry1"] + _n for _n in range(3)]
MISC_ORDER = [("xT", 4), ("ng", 1), ("ngT", 1), ("kT", 4), ("hidk", 1), ("qTa", 2), ("kcn", 1), ("kcT", 1),
              ("qTb", 2), ("hidv", 1), ("cmps", 2), ("vrep", 1), ("att", 4 * HEADS), ("mT", 4), ("hT2", 4)]
MISC = {}
_u = 0
for _name, _n in MISC_ORDER:
    MISC[_name] = _u
    _u += _n

RAW = 3
HL = 3
AHEAD = HL - 1
RG_A = FIRST["rg"] + 3
RG_SQ = FIRST["rg"] + 7
RG_ROOT = RG_SQ + 1
RG_SCAN = (FIRST["rg"] + 9, FIRST["rg"] + 11)
SPLIT_LAST = {FIRST["rg"], FIRST["rg"] + 1, FIRST["qb"] + 1, FIRST["w1v"], FIRST["vv"] + 1, FIRST["nso"] + 3, FIRST["wo"],
              FIRST["wo"] + 3, FIRST["wo"] + 4, FIRST["dn"]}
HEAD0 = FIRST["ry"]
G1, G2, CW, CB, BA, BI, LAM, QN, KN, PK, PV, NPRM = 0, 8, 16, 48, 56, 64, 72, 80, 81, 84, 100, 116
NG_W, W2K, W2V, NSMALL = 0, 384, 512, 640


def hybrid_layer(nc, x, stream, small_w, params, out):
    ctx = ExitStack()
    with ctx:
        def sb(name, shape, dt=F32):
            return ctx.enter_context(nc.sbuf_tensor(name, shape, dt))

        def sem(name):
            return ctx.enter_context(nc.semaphore(name))

        raw = sb("raw", [P, RAW, SLOT])
        w_hi = sb("w_hi", [P, HL, SLOT], F32R)
        w_lo = sb("w_lo", [P, HL, SLOT], F32R)
        xs = sb("xs", [P, T2, D])
        scr = sb("scr", [P, 6144])
        h_hi = sb("h_hi", [P, KC, S], F32R)
        h_lo = sb("h_lo", [P, KC, S], F32R)
        act = sb("act", [P, 12416], F32R)
        v_sb = sb("v_sb", [P, T2, 512])
        pbuf = sb("pbuf", [P, 1536])
        vcx = sb("vcx", [P, 2, 8, DH])
        pcT = sb("pcT", [P, 2, S])
        asq3 = sb("asq3", [P, 512])
        cmpr = sb("cmpr", [P, 1280 + 128], F32R)
        sw_hi = sb("sw_hi", [P, NSMALL], F32R)
        sw_lo = sb("sw_lo", [P, NSMALL], F32R)
        prm = sb("prm", [P, NPRM])
        ident = sb("ident", [P, P])
        identr = sb("identr", [P, P], F32R)
        maskf = sb("maskf", [P, 2 * P + 2 * 16])
        maskr = sb("maskr", [P, 2 * P + 2 * 16], F32R)
        bd = sb("bd", [P, 8])
        half = sb("half", [P, 16])
        ss = sb("ss", [P, 6, 16])
        ms = sb("ms", [P, 6, 16])
        rs = sb("rs", [P, 6, 16])
        gates = sb("gates", [P, T2, 3, HEADS])
        gtmp = sb("gtmp", [48, S])
        sm = sb("sm", [P, 13, 8])
        cst = sb("cst", [P, 4, 32])
        ast = sb("ast", [P, 5, 4])
        psum = [ctx.enter_context(nc.psum_tensor(f"bank{b}", [P, 512], F32)) for b in range(8)]

        xn = scr[:, 0:2048].rearrange("p (t n) -> p t n", t=T2)
        smraw = scr[:, 5504:6144]
        xsq = scr[:, 2048:3072]
        zc = scr[:, 2048:2048 + 1040].rearrange("p (e n) -> p e n", e=2)
        kz = v_sb
        kn = scr[:, 2048:4096].rearrange("p (t n) -> p t n", t=T2)
        qz = scr[:, 2048:4096].rearrange("p (t n) -> p t n", t=T2)
        sq = pbuf[:, 0:1024].rearrange("p (t n) -> p t n", t=T2)
        hid = [v_sb[0:64, 0, 256 * j:256 * (j + 1)] for j in range(2)]
        kcn = v_sb[0:64, 1, 0:P]
        kcsq = v_sb[0:64, 1, P:P + 64]
        cexp = scr[:, 4096:4608]
        A = scr[:, 0:2048].rearrange("p (m s) -> p m s", m=KC)
        B = scr[:, 2048:4096].rearrange("p (m s) -> p m s", m=KC)
        C = scr[:, 4096:6144].rearrange("p (m s) -> p m s", m=KC)
        Dr = xs[:, :, :].rearrange("p t (m s) -> p (t m) s", s=S)
        asq = [(vcx[:, :, :, :].rearrange("p a b d -> p (a b d)").rearrange("p (m s) -> p m s", s=S), 0, 4),
               (pcT[:, :, :], 4, 6), (asq3[:, :].rearrange("p (m s) -> p m s", s=S), 6, 8)]
        mrg = scr[:, 0:2048].rearrange("p (t n) -> p t n", t=T2)
        mt1 = scr[:, 2048:4096].rearrange("p (t n) -> p t n", t=T2)
        mtt = scr[:, 4096:5120].rearrange("p (t n) -> p t n", t=T2)
        xn2 = scr[:, 4096:6144].rearrange("p (t n) -> p t n", t=T2)
        sg = scr[:, 0:512].rearrange("p (b n) -> p b n", b=2)
        sa = scr[:, 512:1024].rearrange("p (b n) -> p b n", b=2)
        k_hh = act[:, 0:2048].rearrange("p (g c) -> p g c", g=GROUPS)
        k_ll = act[:, 2048:4096].rearrange("p (g c) -> p g c", g=GROUPS)
        q_st = act[:, 4096:8192].rearrange("p (j e s) -> p j e s", j=8, e=2)
        oT = q_st
        y_hi = act[:, 8192:10240].rearrange("p (m s) -> p m s", m=KC)
        y_lo = act[:, 10240:12288].rearrange("p (m s) -> p m s", m=KC)
        z_hi = [act[:, 8192 + 2080 * j:8192 + 2080 * j + 1040] for j in range(2)]
        z_lo = [act[:, 8192 + 2080 * j + 1040:8192 + 2080 * (j + 1)] for j in range(2)]
        a_hi = act[:, 0:FF * S].rearrange("p (m s) -> p m s", m=FF)
        a_lo = act[:, FF * S:2 * FF * S].rearrange("p (m s) -> p m s", m=FF)
        hidk_hi, hidk_lo = cmpr[:, 0:128], cmpr[:, 128:256]
        hidv_hi, hidv_lo = cmpr[:, 256:768], cmpr[:, 768:1280]
        kc_hl = cmpr[:, 1280:1408]
        kc_hh, kc_ll = kc_hl[:, 0:64], kc_hl[:, 64:128]
        prob = pbuf[:, 0:768]
        pTa = pbuf[:, 768:1280]
        pTb = pbuf[:, 1280:1536]

        def f(ap):
            return ap.bitcast(F32)

        def acc(u):
            return psum[u % 4]

        def misc(m):
            return psum[4 + m % 4]

        o_bank = misc(MISC["att"] + 3)[:, S:2 * S]

        def misc_count(m):
            return m + 1 if m < MISC["att"] else m + 1 - 4 * HEADS

        landed = [sem(f"landed{i}") for i in range(RAW)]
        x_in, x1_in, small_in, prm_in, x_again = sem("x_in"), sem("x1_in"), sem("small_in"), sem("prm_in"), sem("x_again")
        hi_ready, lo_ready = sem("hi_ready"), sem("lo_ready")
        slot_done = sem("slot_done")
        acc_free = [sem(f"acc_free{i}") for i in range(4)]
        misc_done = sem("misc_done")
        s_done, ta_done, tb_done = sem("s_done"), sem("ta_done"), sem("tb_done")
        misc_free = [sem(f"misc_free{i}") for i in range(4)]
        consts, masks_r = sem("consts"), sem("masks_r")
        small_hi, small_lo = sem("small_hi"), sem("small_lo")
        squares, ms_ready, rs_ready = sem("squares"), sem("ms_ready"), sem("rs_ready")
        evac_hi = sem("evac_hi")
        xn_ready, xn1_ready = sem("xn_ready"), sem("xn1_ready")
        zc_ready, z_hi_ready, z_lo_ready = sem("zc_ready"), sem("z_hi_ready"), sem("z_lo_ready")
        kn_ready, qn_ready = sem("kn_ready"), sem("qn_ready")
        sq_summed = sem("sq_summed")
        hid_ready, hid_hi = sem("hid_ready"), sem("hid_hi")
        c_copied = sem("c_copied")
        c_shift, c_exp, c_ready = sem("c_shift"), sem("c_exp"), sem("c_ready")
        max_ready, scale_ready, prob_ready = sem("max_ready"), sem("scale_ready"), sem("prob_ready")
        o_done, o_hi, o_ready = sem("o_done"), sem("o_hi"), sem("o_ready")
        sp_neg, sp_exp, sp_ready = sem("sp_neg"), sem("sp_exp"), sem("sp_ready")
        conv0, xr_ready, xr_hi, xr_lo = sem("conv0"), sem("xr_ready"), sem("xr_hi"), sem("xr_lo")
        rg_done = sem("rg_done")
        gated_x, log_a, w_ready, a_ready = sem("gated_x"), sem("log_a"), sem("w_ready"), sem("a_ready")
        asq_ready, asq_used, root_ready = sem("asq_ready"), sem("asq_used"), sem("root_ready")
        gelu_ready, y_ready, y_hi_ready, y_lo_ready = sem("gelu_ready"), sem("y_ready"), sem("y_hi_ready"), sem("y_lo_ready")
        m_gated = sem("m_gated")
        merged = sem("merged")
        x1_ready, silu_ready, a_prod, a_hi_ready, a_lo_ready = sem("x1_ready"), sem("silu_ready"), sem("a_prod"), sem("a_hi_ready"), sem("a_lo_ready")
        wo_half, u_ready, pcT_done = sem("wo_half"), sem("u_ready"), sem("pcT_done")
        dn_done, res_ready, stored = sem("dn_done"), sem("res_ready"), sem("stored")
        dve_chain, pool_chain = sem("dve_chain"), sem("pool_chain")

        def wait_acc_free(eng, u):
            if u >= 4:
                eng.wait_ge(acc_free[u % 4], u // 4)

        def wait_misc_free(eng, m):
            if m >= 4:
                eng.wait_ge(misc_free[m % 4], m // 4)

        def wait_misc_read(eng, m):
            eng.wait_ge(misc_free[m % 4], m // 4 + 1)

        NORM_X, NORM_K, NORM_Q0, NORM_Q1, NORM_KC, NORM_X1 = range(6)
        NORM_SHAPE = [(P, 2), (P, 16), (P, 16), (P, 16), (64, 1), (P, 2)]
        RS_BEFORE = [0, 1, 3, 5, 7, 8]

        def rs_count(n, t=0):
            return RS_BEFORE[n] + t + 1

        def rs_wide(n, t, shape):
            r = rs[:, n, 8 * t:8 * t + 8]
            for _ in range(len(shape) - 2):
                r = r.unsqueeze(len(r.shape))
            return r.broadcast_to(shape)

        block = ctx.enter_context(nc.Block())

        @block.sync
        def _(sp):
            sp.dma_start(xs[:, 0, :], x[0:P, :]).then_inc(x_in, 16)
            def load(i, r):
                sp.dma_start(raw[:, r, :], stream[bass.ds(i, 1), :, :].rearrange("o p n -> (o p) n")).then_inc(landed[r], 16)

            for r in range(RAW):
                load(r, r)
            with sp.Fori(1, NSLOT // RAW) as rnd:
                for r in range(RAW):
                    i = rnd * RAW + r
                    sp.wait_ge(lo_ready, i - RAW + 1)
                    load(i, r)
            for i in range(NSLOT // RAW * RAW, NSLOT):
                sp.wait_ge(lo_ready, i - RAW + 1)
                load(i, i % RAW)
            for t in range(T2):
                for n in range(2):
                    sp.wait_ge(res_ready, 2 * t + n + 1)
                    sp.dma_start(out[t * P:(t + 1) * P, n * 512:(n + 1) * 512],
                                 xs[:, t, n * 512:(n + 1) * 512]).then_inc(stored, 16)
            sp.wait_ge(stored, 16 * 4)

        @block.gpsimd
        def _(pool):
            pool.memset(ident[:, :], 0.0).then_inc(pool_chain, 1)
            pool.memset(maskf[:, :], 0.0).then_inc(pool_chain, 1)
            pool.memset(bd[:, :], 1.0).then_inc(pool_chain, 1)
            pool.memset(half[:, :], -0.5).then_inc(pool_chain, 1)
            pool.wait_ge(pool_chain, 4)
            pool.affine_select(out=ident[:, :], in_=ident[:, :], compare_op=ALU.not_equal, fill=1.0,
                               base=0, pattern=[[-1, P]], channel_multiplier=1).then_inc(consts, 1)
            cm = maskf[:, 0:2 * P].rearrange("p (b j) -> p b j", b=2)
            pool.affine_select(out=cm, in_=cm, compare_op=ALU.is_ge, fill=NEG, base=0,
                               pattern=[[0, 2], [-1, P]], channel_multiplier=1).then_inc(consts, 1)
            cc = maskf[:, 2 * P:].rearrange("p (t c) -> p t c", t=T2)
            pool.affine_select(out=cc, in_=cc, compare_op=ALU.is_ge, fill=NEG, base=-31,
                               pattern=[[P, T2], [-16, 16]], channel_multiplier=1).then_inc(consts, 1)
            pool.affine_select(out=bd[:, :], in_=bd[:, :], compare_op=ALU.is_ge, fill=0.0, base=0,
                               pattern=[[-16, 8]], channel_multiplier=1).then_inc(pool_chain, 1)
            pool.wait_ge(pool_chain, 5)
            pool.affine_select(out=bd[:, :], in_=bd[:, :], compare_op=ALU.is_ge, fill=0.0, base=15,
                               pattern=[[16, 8]], channel_multiplier=-1).then_inc(consts, 1)

            def rsqrt(n, t=0, w=None):
                p = NORM_SHAPE[n][0]
                w = w or NORM_SHAPE[n][1]
                pool.wait_ge(ms_ready, rs_count(n, t))
                c = slice(w * t, w * t + w)
                pool.tensor_tensor(rs[0:p, n, c], ms[0:p, n, c], half[0:p, 0:w], ALU.pow).then_inc(rs_ready, 1)

            rsqrt(NORM_X)
            for t in range(T2):
                rsqrt(NORM_K, t, 8)
            for t in range(T2):
                rsqrt(NORM_Q0, t, 8)
                u = USE["qa"] + t
                pool.wait_ge(rs_ready, rs_count(NORM_Q0, t))
                pool.wait_ge(acc_free[u % 4], u // 4 + 1)
                qv = qz[:, t, 0:512].rearrange("p (h d) -> p h d", d=DH)
                pool.tensor_tensor(qv, qv, rs_wide(NORM_Q0, t, [P, 8, DH]), ALU.mult).then_inc(qn_ready, 1)
            pool.wait_ge(root_ready, 1)
            pool.memset(Dr[:, :, 0:1], 0.5).then_inc(pool_chain, 1)
            pool.wait_ge(pool_chain, 6)
            for v in range(2):
                pool.tensor_tensor(A[:, 4 * v:4 * v + 4, :], A[:, 4 * v:4 * v + 4, :], Dr[:, 4 * v:4 * v + 4, :],
                                   ALU.mult).then_inc(u_ready, 1)
            for t in range(T2):
                rsqrt(NORM_Q1, t, 8)
            rsqrt(NORM_KC)
            for h in range(HEADS):
                pool.wait_ge(scale_ready, h + 1)
                for j, (a, b) in enumerate(((0, 128), (128, 256), (256, 512), (512, 768))):
                    ins = pool.tensor_scalar(prob[:, a:b], prob[:, a:b], ast[:, 4, j:j + 1], 1.0, ALU.mult, ALU.mult)
                ins.then_inc(prob_ready, 1)
                if h == 12:
                    pool.wait_ge(y_lo_ready, 4)
                    pool.dma_start(xs[:, :, :], x.rearrange("(t p) n -> p t n", p=P)).then_inc(x_again, 16)
            for t in range(T2):
                rsqrt(NORM_X1, t, 1)

        @block.scalar
        def _(sc):
            sc.dma_start(xs[:, 1, :], x[P:2 * P, :]).then_inc(x1_in, 16)
            sc.dma_start(prm[:, :], params[:, :]).then_inc(prm_in, 16)
            sc.dma_start(smraw, small_w[:, :]).then_inc(small_in, 16)

            def split_hi(i):
                if i >= NSLOT:
                    return
                sc.wait_ge(landed[i % RAW], 16 * (i // RAW + 1))
                if i >= HL:
                    sc.wait_ge(slot_done, i - HL + 1)
                sc.activation(w_hi[:, i % HL, :], raw[:, i % RAW, :], ACT.Copy).then_inc(hi_ready, 1)

            def acc_ready(slot):
                sc.wait_ge(slot_done, slot + 1)

            sc.wait_ge(x_in, 16)
            sc.activation(xsq, xs[:, 0, :], ACT.Square, accum_out=ss[:, NORM_X, 0:1]).then_inc(squares, 1)
            sc.wait_ge(rs_ready, rs_count(NORM_X))
            sc.wait_ge(x1_in, 16)
            sc.activation(xn[:, 1, :], xs[:, 1, :], ACT.Copy, scale=rs[:, NORM_X, 1:2]).then_inc(xn1_ready, 1)
            split_hi(0)

            def unit_hi(m, j, gain_col):
                sc.wait_ge(misc_done, misc_count(m))
                for e in range(2):
                    c = 2 * j + e
                    ins = sc.activation(h_hi[:, c, :], misc(m)[:, e * S:(e + 1) * S], ACT.Copy,
                                        scale=prm[:, gain_col + c:gain_col + c + 1])
                ins.then_inc(evac_hi, 1)

            sc.wait_ge(prm_in, 16)
            for j in range(4):
                unit_hi(MISC["xT"] + j, j, G1)
            sc.wait_ge(small_in, 16)
            sc.activation(sw_hi[:, :], smraw, ACT.Copy).then_inc(small_hi, 1)
            split_hi(1)

            def squares_and_copy(first_slot, use, dst, n):
                acc_ready(first_slot + 1)
                if n > NORM_K:
                    sc.wait_ge(sq_summed, 2 * (n - NORM_K))
                for t in range(T2):
                    sc.activation(sq[:, t, :], acc(use + t)[:, :], ACT.Square).then_inc(squares, 1)
                for t in range(T2):
                    sc.activation(dst[:, t, :], acc(use + t)[:, :], ACT.Copy).then_inc(acc_free[(use + t) % 4], 1)

            for i in range(NSLOT + 2):
                h = i - HEAD0
                if h >= 3 and h % 2 == 1 and h <= HEADS + 1:
                    pair = (h - 3) // 2
                    sc.wait_ge(o_done, 2 * pair + 2)
                    sc.activation(oT[:, pair, 0, :], o_bank, ACT.Copy).then_inc(o_hi, 1)
                if 1 <= h <= HEADS:
                    m = MISC["att"] + 4 * (h - 1)
                    sc.wait_ge(ta_done, h)
                    if h >= 2:
                        sc.wait_ge(o_done, h - 1)
                    sc.activation(pTa, misc(m + 2)[:, :], ACT.Copy).then_inc(misc_free[(m + 2) % 4], 1)
                    sc.wait_ge(tb_done, h)
                    sc.activation(pTb, misc(m + 3)[:, 0:256], ACT.Copy).then_inc(misc_free[(m + 3) % 4], 1)
                for v in range(2):
                    if i == FIRST["ry"] + 3 + 2 * v:
                        u = USE_RY[2 * v + 1]
                        sc.wait_ge(acc_free[u % 4], u // 4 + 1)
                        sc.activation(B[:, 4 * v:4 * v + 4, :], B[:, 4 * v:4 * v + 4, :],
                                      ACT.Gelu_apprx_tanh).then_inc(gelu_ready, 1)
                if 0 <= h < HEADS:
                    m = MISC["att"] + 4 * h
                    sc.wait_ge(max_ready, h + 1)
                    if h >= 1:
                        sc.wait_ge(tb_done, h)
                    for j, (a, b) in enumerate(((0, 128), (128, 256), (256, 512), (512, 768))):
                        bank = misc(m + j // 2)
                        off = 0 if j % 2 == 0 else (b - a)
                        ins = sc.activation(prob[:, a:b], bank[:, off:off + b - a], ACT.Exp, bias=ast[:, 1, j:j + 1],
                                            scale=SCALE, accum_out=ast[:, 2, j:j + 1])
                        if j % 2 == 1:
                            ins.then_inc(misc_free[(m + j // 2) % 4], 1)

                if i == HEAD0:
                    sc.wait_ge(c_shift, 1)
                    sc.activation(cexp, cexp, ACT.Exp, scale=SCALE).then_inc(c_exp, 1)
                for v in range(2):
                    if i == FIRST["ry"] + 3 + 2 * v:
                        for n in (2 * v, 2 * v + 1):
                            sc.wait_ge(y_ready, n + 1)
                            sc.activation(y_hi[:, 2 * n:2 * n + 2, :], A[:, 2 * n:2 * n + 2, :], ACT.Copy).then_inc(y_hi_ready, 1)
                if i not in SPLIT_LAST:
                    split_hi(i + AHEAD)
                if i == 2:
                    sc.wait_ge(misc_done, misc_count(MISC["ng"]))
                    sc.activation(gtmp[:, :], misc(MISC["ng"])[0:48, 0:S], ACT.Tanh,
                                  scale=0.5).then_inc(misc_free[MISC["ng"] % 4], 1)
                if i == 0:
                    sc.wait_ge(sp_neg, 1)
                    sc.activation(sm[:, 1, :], sm[:, 0, :], ACT.Exp).then_inc(sp_exp, 1)
                for j, name in enumerate(("kc", "vc")):
                    if i == FIRST[name] + 2:
                        sc.wait_ge(zc_ready, j + 1)
                        sc.activation(z_hi[j], zc.rearrange("p e n -> p (e n)"), ACT.Copy).then_inc(z_hi_ready, 1)
                if i == FIRST["kk"] + 2:
                    squares_and_copy(FIRST["kk"], USE["kk"], kz, NORM_K)
                if i == FIRST["vv"] + 2:
                    acc_ready(FIRST["vv"] + 1)
                    for t in range(T2):
                        u = USE["vv"] + t
                        sc.activation(v_sb[:, t, :], acc(u)[:, :], ACT.Copy).then_inc(acc_free[u % 4], 1)
                if i == FIRST["kk"] + 4:
                    for g in range(GROUPS):
                        m = MISC["kT"] + g
                        sc.wait_ge(misc_done, misc_count(m))
                        for b in range(2):
                            ins = sc.activation(k_hh[:, g, b * S:(b + 1) * S], misc(m)[:, b * S:(b + 1) * S], ACT.Copy,
                                                scale=prm[:, KN + 1 + b:KN + 2 + b])
                        ins.then_inc(evac_hi, 1)
                for pnl, name in enumerate(("qa", "qb")):
                    if i == FIRST[name] + 2:
                        if pnl == 0:
                            sc.wait_ge(z_lo_ready, 2)
                        squares_and_copy(FIRST[name], USE[name], qz[:, :, pnl * 512:(pnl + 1) * 512], NORM_Q0 + pnl)
                    if i == FIRST[name] + 5:
                        for v in range(2):
                            m = MISC[("qTa", "qTb")[pnl]] + v
                            sc.wait_ge(misc_done, misc_count(m))
                            pr = 4 * pnl + 2 * v
                            for e in range(2):
                                ins = sc.activation(q_st[0:64, pr:pr + 2, e, :],
                                                    misc(m)[64 * e:64 * e + 64, :].rearrange("p (j s) -> p j s", j=2),
                                                    ACT.Copy, scale=prm[64 * e:64 * e + 64, QN:QN + 1])
                            ins.then_inc(evac_hi, 1)
                for j, name in enumerate(("w1k", "w1v")):
                    if i == FIRST[name] + 2:
                        acc_ready(FIRST[name] + 1)
                        sc.activation(hid[j], acc(USE[name])[0:64, 0:256], ACT.Gelu_apprx_tanh).then_inc(hid_ready, 1)
                    if i == FIRST[name] + 3:
                        m = MISC["hidk"] if j == 0 else MISC["hidv"]
                        sc.wait_ge(misc_done, misc_count(m))
                        if j == 0:
                            ins = sc.activation(hidk_hi, misc(m)[:, 0:128], ACT.Copy)
                        else:
                            ins = sc.activation(hidv_hi.rearrange("p (c j n) -> p c j n", c=8, j=4),
                                                misc(m)[:, 0:128].rearrange("p (c n) -> p c n", c=8).unsqueeze(2)
                                                .broadcast_to([P, 8, 4, 16]), ACT.Copy)
                        ins.then_inc(hid_hi, 1)
                if i == FIRST["w1k"] + 4:
                    sc.wait_ge(misc_done, misc_count(MISC["kcn"]))
                    sc.activation(kcsq, misc(MISC["kcn"])[0:64, 0:64], ACT.Square,
                                  accum_out=ss[0:64, NORM_KC, 0:1]).then_inc(squares, 1)
                if i == FIRST["w1k"] + 7:
                    sc.wait_ge(misc_done, misc_count(MISC["kcT"]))
                    sc.activation(kc_hh, misc(MISC["kcT"])[:, 0:64], ACT.Copy, scale=prm[:, KN:KN + 1]).then_inc(evac_hi, 1)
                r = i - FIRST["rx"] - 2
                if 0 <= r < 4:
                    sc.wait_ge(xr_ready, r + 1)
                    sc.activation(y_hi[:, 2 * r:2 * r + 2, :], A[:, 2 * r:2 * r + 2, :], ACT.Copy).then_inc(xr_hi, 1)
                r = i - FIRST["rx"] - 1
                if 0 <= r < 4:
                    acc_ready(FIRST["rx"] + r)
                    for e in range(2):
                        m = 2 * r + e
                        ins = sc.activation(A[:, m, :], acc(USE["rx"] + r)[:, e * S:(e + 1) * S], ACT.Identity,
                                            scale=prm[:, CW + 24 + m:CW + 25 + m], bias=prm[:, CB + m:CB + m + 1])
                        ins.then_inc(conv0, 1)
                for n in range(4):
                    if i == FIRST["rg"] + n // 2 + n % 2:
                        if n == 0:
                            sc.wait_ge(sp_ready, 1)
                        for kind in range(2):
                            u = USE["rg"] + 2 * n + kind
                            if n % 2 == 1 and kind == 1:
                                acc_ready(FIRST["rg"] + n // 2)
                            else:
                                sc.wait_ge(rg_done, 3 * (n // 2) + 2 * (n % 2) + kind + 1)
                            for e in range(2):
                                m = 2 * n + e
                                dst = (C, Dr)[kind]
                                ins = sc.activation(dst[:, m, :], acc(u)[:, e * S:(e + 1) * S], ACT.Tanh, scale=0.5,
                                                    bias=sm[:, 10 + kind, m:m + 1])
                            ins.then_inc(acc_free[u % 4], 1)
                if i == RG_A:
                    sc.wait_ge(log_a, 8)
                    for e, (buf, a, b) in enumerate(asq):
                        sc.activation(buf, C[:, a:b, :], ACT.Exp, scale=2.0).then_inc(asq_ready, 1)
                if i == RG_A + 1:
                    sc.wait_ge(gated_x, 4)
                    sc.activation(Dr[:, :, :], C[:, :, :], ACT.Tanh, scale=-1.0).then_inc(w_ready, 1)
                if i == RG_A + 2:
                    sc.wait_ge(w_ready, 1)
                    sc.wait_ge(asq_ready, 3)
                    sc.activation(C[:, :, :], C[:, :, :], ACT.Exp).then_inc(a_ready, 1)
                if i == RG_ROOT:
                    sc.wait_ge(asq_used, 3)
                    sc.activation(Dr[:, :, :], Dr[:, :, :], ACT.Sqrt, scale=0.25).then_inc(root_ready, 1)
                r = i - FIRST["ry"] - 1
                if 0 <= r < 4:
                    acc_ready(FIRST["ry"] + r)
                    u = USE_RY[r]
                    sc.activation(B[:, 2 * r:2 * r + 2, :], acc(u)[:, :].rearrange("p (m s) -> p m s", m=2),
                                  ACT.Copy).then_inc(acc_free[u % 4], 1)
                if i == HEAD0 + 1:
                    u = USE["pcT"]
                    sc.wait_ge(pcT_done, 1)
                    sc.activation(pcT[:, :, :].rearrange("p a s -> p (a s)"), acc(u)[:, :], ACT.Copy).then_inc(acc_free[u % 4], 1)
                for pnl in range(2):
                    if i == FIRST["rgo"] + pnl + 3:
                        acc_ready(FIRST["rgo"] + pnl + 2)
                        if pnl == 0:
                            sc.wait_ge(y_lo_ready, 4)
                        for t in range(T2):
                            u = USE["rgo"] + 2 * pnl + t
                            sc.activation(mrg[:, t, pnl * 512:(pnl + 1) * 512], acc(u)[:, :], ACT.Copy).then_inc(acc_free[u % 4], 1)
                for pnl in range(4):
                    if i == FIRST["mg"] + 2 * pnl + 2:
                        acc_ready(FIRST["mg"] + 2 * pnl + 1)
                        if pnl == 1:
                            sc.wait_ge(m_gated, 2)
                        for t in range(T2):
                            u = USE["mg"] + 2 * pnl + t
                            dst = mtt[:, t, :] if pnl < 2 else mt1[:, t, (pnl - 2) * 512:(pnl - 1) * 512]
                            sc.activation(dst, acc(u)[:, :], ACT.Tanh, scale=0.5).then_inc(acc_free[u % 4], 1)
                for v in range(2):
                    if i == FIRST["wo"] - 1 + 2 * v:
                        for j in (2 * v, 2 * v + 1):
                            m = MISC["mT"] + j
                            sc.wait_ge(misc_done, misc_count(m))
                            sc.activation(h_hi[:, 2 * j:2 * j + 2, :], misc(m)[:, :].rearrange("p (c s) -> p c s", c=2),
                                          ACT.Copy, scale=0.5).then_inc(evac_hi, 1)
                for pnl in range(2):
                    if i == FIRST["wo"] + pnl + 3:
                        for t in range(T2):
                            sc.wait_ge(x1_ready, 2 * pnl + t + 1)
                            c = 2 * pnl + t
                            sc.activation(scr[:, 512 * c:512 * (c + 1)], xs[:, t, pnl * 512:(pnl + 1) * 512], ACT.Square,
                                          accum_out=ss[:, NORM_X1, c:c + 1]).then_inc(squares, 1)
                            if (pnl, t) == (1, 0):
                                split_hi(i + AHEAD - 1)
                if i == FIRST["wo"] + 4:
                    sc.wait_ge(rs_ready, rs_count(NORM_X1, 1))
                    sc.activation(xn2[:, 1, 512:1024], xs[:, 1, 512:1024], ACT.Copy, scale=rs[:, NORM_X1, 1:2]).then_inc(xn1_ready, 1)
                    for j in range(4):
                        unit_hi(MISC["hT2"] + j, j, G2)
                j = i - FIRST["gu"] - 1
                if 0 <= j < FF:
                    acc_ready(FIRST["gu"] + j)
                    if j >= 2:
                        sc.wait_ge(a_prod, j - 1)
                    sc.activation(sg[:, j % 2, :], acc(USE["gu"] + j)[:, 0:S], ACT.Silu).then_inc(silu_ready, 1)
                if 1 <= j <= FF:
                    sc.wait_ge(a_prod, j)
                    sc.activation(a_hi[:, j - 1, :], sa[:, (j - 1) % 2, :], ACT.Copy).then_inc(a_hi_ready, 1)
                if i in SPLIT_LAST and i != FIRST["wo"] + 3:
                    split_hi(i + AHEAD)

        @block.vector
        def _(ve):
            chain = [0]

            def link(ins):
                chain[0] += 1
                ins.then_inc(dve_chain, 1)
                ve.wait_ge(dve_chain, chain[0])

            def split_lo(i):
                if i >= NSLOT:
                    return
                ve.wait_ge(hi_ready, i + 1)
                ve.tensor_tensor(w_lo[:, i % HL, :], raw[:, i % RAW, :], f(w_hi[:, i % HL, :]),
                                 ALU.subtract).then_inc(lo_ready, 1)

            def mean(n, scale):
                p, w = NORM_SHAPE[n]
                ve.tensor_scalar(ms[0:p, n, 0:w], ss[0:p, n, 0:w], scale, EPS, ALU.mult, ALU.add).then_inc(ms_ready, 1)

            ve.wait_ge(x1_in, 16)
            ve.scalar_tensor_tensor(out=scr[:, 3072:4096], in0=xs[:, 1, :], scalar=1.0, in1=xs[:, 1, :], op0=ALU.mult,
                                    op1=ALU.mult, accum_out=ss[:, NORM_X, 1:2]).then_inc(dve_chain, 1)
            chain[0] += 1
            ve.wait_ge(dve_chain, chain[0])
            ve.wait_ge(squares, 1)
            mean(NORM_X, 1.0 / D)
            ve.wait_ge(rs_ready, rs_count(NORM_X))
            ve.wait_ge(x_in, 16)
            ve.tensor_scalar(xn[:, 0, :], xs[:, 0, :], rs[:, NORM_X, 0:1], None, ALU.mult).then_inc(xn_ready, 1)
            split_lo(0)
            ve.wait_ge(prm_in, 16)

            def softplus():
                lam = prm[:, LAM:LAM + 8]
                link(ve.tensor_scalar(sm[:, 2, :], lam, -1.0, None, ALU.mult))
                ve.tensor_tensor(sm[:, 0, :], sm[:, 2, :], lam, ALU.min).then_inc(sp_neg, 1)
                link(ve.tensor_scalar(sm[:, 3, :], sm[:, 2, :], 0.0, None, ALU.max))
                ve.wait_ge(sp_exp, 1)
                link(ve.tensor_scalar(sm[:, 4, :], sm[:, 1, :], 2.0, None, ALU.add))
                link(ve.reciprocal(sm[:, 5, :], sm[:, 4, :]))
                link(ve.tensor_tensor(sm[:, 6, :], sm[:, 1, :], sm[:, 5, :], ALU.mult))
                link(ve.tensor_tensor(sm[:, 7, :], sm[:, 6, :], sm[:, 6, :], ALU.mult))
                link(ve.tensor_scalar(sm[:, 8, :], sm[:, 7, :], 1.0 / 17, 1.0 / 15, ALU.mult, ALU.add))
                for c in (13, 11, 9, 7, 5, 3, 1):
                    link(ve.tensor_tensor(sm[:, 9, :], sm[:, 8, :], sm[:, 7, :], ALU.mult))
                    link(ve.tensor_scalar(sm[:, 8, :], sm[:, 9, :], 1.0 / c, None, ALU.add))
                link(ve.scalar_tensor_tensor(out=sm[:, 9, :], in0=sm[:, 8, :], scalar=2.0, in1=sm[:, 6, :],
                                             op0=ALU.mult, op1=ALU.mult))
                link(ve.tensor_tensor(sm[:, 4, :], sm[:, 9, :], sm[:, 3, :], ALU.add))
                link(ve.tensor_scalar(sm[:, 12, :], sm[:, 4, :], -4.0, None, ALU.mult))
                ve.tensor_scalar(sm[:, 10, :], prm[:, BA:BA + 8], 0.5, None, ALU.mult)
                ve.tensor_scalar(sm[:, 11, :], prm[:, BI:BI + 8], 0.5, None, ALU.mult).then_inc(sp_ready, 1)

            def unit_lo(m, j, gain_col, count):
                ve.wait_ge(evac_hi, count)
                for e in range(2):
                    c = 2 * j + e
                    ins = ve.scalar_tensor_tensor(out=h_lo[:, c, :], in0=misc(m)[:, e * S:(e + 1) * S],
                                                  scalar=prm[:, gain_col + c:gain_col + c + 1],
                                                  in1=f(h_hi[:, c, :]), op0=ALU.mult, op1=ALU.subtract)
                ins.then_inc(misc_free[m % 4], 1)

            for j in range(4):
                unit_lo(MISC["xT"] + j, j, G1, j + 1)
            ve.wait_ge(small_hi, 1)
            ve.tensor_tensor(sw_lo[:, :], smraw, f(sw_hi[:, :]), ALU.subtract).then_inc(small_lo, 1)
            split_lo(1)
            ve.wait_ge(consts, 4)
            ve.tensor_copy(identr[:, :], ident[:, :])
            ve.tensor_copy(maskr[:, :], maskf[:, :]).then_inc(masks_r, 1)

            def sums(n, count):
                for t in range(T2):
                    c = slice(8 * t, 8 * t + 8)
                    ve.wait_ge(squares, count + t + 1)
                    ve.tensor_reduce(ss[:, n, c], sq[:, t, :].rearrange("p (h d) -> p h d", d=DH), AX, ALU.add).then_inc(sq_summed, 1)
                    ve.wait_ge(sq_summed, 2 * (n - NORM_K) + t + 1)
                    ve.tensor_scalar(ms[:, n, c], ss[:, n, c], 1.0 / DH, EPS, ALU.mult, ALU.add).then_inc(ms_ready, 1)

            for i in range(NSLOT + 2):
                h = i - HEAD0
                if h >= 3 and h % 2 == 1 and h <= HEADS + 1:
                    pair = (h - 3) // 2
                    ve.wait_ge(o_hi, pair + 1)
                    ve.tensor_tensor(oT[:, pair, 1, :], o_bank, f(oT[:, pair, 0, :]),
                                     ALU.subtract).then_inc(o_ready, 1)
                if i == HEAD0:
                    ex3 = cexp.rearrange("p (c n) -> p c n", n=16)
                    for t in range(T2):
                        m = MISC["cmps"] + t
                        ve.wait_ge(misc_done, misc_count(m))
                        ve.tensor_copy(cexp[:, t * S:(t + 1) * S], misc(m)[:, 0:S]).then_inc(c_copied, 1)
                    for t in range(T2):
                        m = MISC["cmps"] + t
                        ve.wait_ge(c_copied, t + 1)
                        ct = cexp[:, t * S:(t + 1) * S]
                        ve.tensor_tensor(ct, misc(m)[:, S:2 * S], ct, ALU.add).then_inc(misc_free[m % 4], 1)
                    wait_misc_read(ve, m)
                    link(ve.tensor_reduce(cst[:, 0, :], ex3, AX, ALU.max))
                    link(ve.tensor_scalar(cst[:, 1, :], cst[:, 0, :], -1e30, None, ALU.max))
                    ve.tensor_tensor(ex3, ex3, cst[:, 1, :].unsqueeze(2).broadcast_to([P, 32, 16]), ALU.subtract).then_inc(c_shift, 1)
                if 0 <= h < HEADS:
                    m = MISC["att"] + 4 * h
                    for t in range(T2):
                        ve.wait_ge(s_done, 2 * h + t + 1)
                        w = P * (t + 1)
                        ins = ve.tensor_reduce(ast[:, 0, 2 * t:2 * t + 2],
                                               misc(m + t)[:, 0:2 * w].rearrange("p (b c) -> p b c", b=2), AX, ALU.max)
                    link(ins)
                    ve.tensor_scalar(ast[:, 1, :], ast[:, 0, :], -SCALE, None, ALU.mult).then_inc(max_ready, 1)
                for v in range(2):
                    if i == FIRST["ry"] + 3 + 2 * v:
                        for n in (2 * v, 2 * v + 1):
                            ve.wait_ge(gelu_ready, v + 1)
                            ve.tensor_tensor(A[:, 2 * n:2 * n + 2, :], Dr[:, 2 * n:2 * n + 2, :], B[:, 2 * n:2 * n + 2, :],
                                             ALU.mult).then_inc(y_ready, 1)
                if 0 <= h < HEADS:
                    wait_misc_read(ve, MISC["att"] + 4 * h)
                    wait_misc_read(ve, MISC["att"] + 4 * h + 1)
                    link(ve.reciprocal(ast[:, 3, :], ast[:, 2, :]))
                    ve.tensor_tensor(ast[:, 4, :].rearrange("p (t b) -> p t b", t=T2),
                                     ast[:, 3, :].rearrange("p (t b) -> p t b", t=T2),
                                     gates[:, :, 1:3, h], ALU.mult).then_inc(scale_ready, 1)

                for v in range(2):
                    if i == FIRST["ry"] + 3 + 2 * v:
                        for n in (2 * v, 2 * v + 1):
                            ve.wait_ge(y_hi_ready, n + 1)
                            ve.tensor_tensor(y_lo[:, 2 * n:2 * n + 2, :], A[:, 2 * n:2 * n + 2, :], f(y_hi[:, 2 * n:2 * n + 2, :]),
                                             ALU.subtract).then_inc(y_lo_ready, 1)
                if i == HEAD0:
                    ex3 = cexp.rearrange("p (c n) -> p c n", n=16)
                    ve.wait_ge(c_exp, 1)
                    link(ve.tensor_reduce(cst[:, 0, :], ex3, AX, ALU.add))
                    link(ve.tensor_scalar(cst[:, 2, :], cst[:, 0, :], 1e-30, None, ALU.max))
                    link(ve.reciprocal(cst[:, 3, :], cst[:, 2, :]))
                    link(ve.tensor_tensor(cst[:, 2, :].rearrange("p (t h) -> p t h", t=T2),
                                          cst[:, 3, :].rearrange("p (t h) -> p t h", t=T2), gates[:, :, 0, :], ALU.mult))
                    ve.tensor_tensor(ex3, ex3, cst[:, 2, :].unsqueeze(2).broadcast_to([P, 32, 16]), ALU.mult).then_inc(c_ready, 1)
                if i not in SPLIT_LAST:
                    split_lo(i + AHEAD)
                if i == HEAD0:
                    m = MISC["vrep"]
                    ve.wait_ge(misc_done, misc_count(m))
                    for hf in range(2):
                        ins = ve.tensor_tensor(vcx[:, hf, :, :], misc(m)[:, hf * DH:(hf + 1) * DH].unsqueeze(1).broadcast_to([P, 8, DH]),
                                               bd[:, :].unsqueeze(2).broadcast_to([P, 8, DH]), ALU.mult)
                    ins.then_inc(misc_free[m % 4], 1)
                if i == FIRST["kk"] + 3:
                    for t in range(T2):
                        ve.wait_ge(rs_ready, rs_count(NORM_K, t))
                        u = USE["kk"] + t
                        ve.wait_ge(acc_free[u % 4], u // 4 + 1)
                        ve.tensor_tensor(kn[:, t, :].rearrange("p (c e d) -> p c e d", c=8, e=2),
                                         kz[:, t, :].rearrange("p (c d) -> p c d", c=8).unsqueeze(2).broadcast_to([P, 8, 2, DH]),
                                         rs_wide(NORM_K, t, [P, 8, 2, DH]), ALU.mult).then_inc(kn_ready, 1)
                if i == FIRST["qb"] + 3:
                    for t in range(T2):
                        ve.wait_ge(rs_ready, rs_count(NORM_Q1, t))
                        u = USE["qb"] + t
                        ve.wait_ge(acc_free[u % 4], u // 4 + 1)
                        qv = qz[:, t, 512:1024].rearrange("p (h d) -> p h d", d=DH)
                        ve.tensor_tensor(qv, qv, rs_wide(NORM_Q1, t, [P, 8, DH]), ALU.mult).then_inc(qn_ready, 1)
                if i == 0:
                    softplus()
                if i == 3:
                    m = MISC["ngT"]
                    ve.wait_ge(misc_done, misc_count(m))
                    ve.tensor_scalar(gates[:, :, :, :].rearrange("p t b h -> p (t b h)"), misc(m)[:, 0:96], 1.0, 0.5,
                                     ALU.add, ALU.mult).then_inc(misc_free[m % 4], 1)
                for j, name in enumerate(("kc", "vc")):
                    if i == FIRST[name] + 2:
                        ve.wait_ge(z_hi_ready, j + 1)
                        ve.tensor_tensor(z_lo[j], zc.rearrange("p e n -> p (e n)"), f(z_hi[j]),
                                         ALU.subtract).then_inc(z_lo_ready, 1)
                for j, name in enumerate(("kc", "vc")):
                    if i == FIRST[name] + 1:
                        ve.wait_ge(slot_done, FIRST[name] + 1)
                        if j == 0:
                            ve.memset(zc[:, :, 512:520], 0.0)
                        else:
                            ve.wait_ge(z_lo_ready, 1)
                        u = USE[name]
                        pos = (PK, PV)[j]
                        last = None
                        for e in range(2):
                            for par in range(2):
                                for gp in range(2):
                                    src = acc(u)[64 * gp:64 * gp + 64, :].rearrange("p (n l r) -> p n l r", l=8, r=2)[:, :, :, par]
                                    pv = prm[64 * par:64 * par + 64, pos + 8 * e:pos + 8 * e + 8].unsqueeze(1).broadcast_to([64, 32, 8])
                                    dst = zc[64 * par:64 * par + 64, e, 256 * gp:256 * gp + 256].rearrange("p (n l) -> p n l", l=8)
                                    last = (dst, src, pv)
                                    if (e, par, gp) != (1, 1, 1):
                                        ve.tensor_tensor(dst, src, pv, ALU.add)
                        ve.tensor_tensor(*last, ALU.add).then_inc(zc_ready, 1)
                        ve.wait_ge(zc_ready, j + 1)
                        ve.engine_nop().then_inc(acc_free[u % 4], 1)
                if i == FIRST["kk"] + 2:
                    sums(NORM_K, 1)
                if i == FIRST["kk"] + 4:
                    for g in range(GROUPS):
                        m = MISC["kT"] + g
                        ve.wait_ge(evac_hi, 4 + g + 1)
                        for b in range(2):
                            ins = ve.scalar_tensor_tensor(out=k_ll[:, g, b * S:(b + 1) * S], in0=misc(m)[:, b * S:(b + 1) * S],
                                                          scalar=prm[:, KN + 1 + b:KN + 2 + b],
                                                          in1=f(k_hh[:, g, b * S:(b + 1) * S]), op0=ALU.mult, op1=ALU.subtract)
                        ins.then_inc(misc_free[m % 4], 1)
                for pnl, name in enumerate(("qa", "qb")):
                    if i == FIRST[name] + 2:
                        sums(NORM_Q0 + pnl, 3 + 2 * pnl)
                    if i == FIRST[name] + 5:
                        for v in range(2):
                            m = MISC[("qTa", "qTb")[pnl]] + v
                            pr = 4 * pnl + 2 * v
                            ve.wait_ge(evac_hi, 8 + 2 * pnl + v + 1)
                            for e in range(2):
                                ins = ve.scalar_tensor_tensor(out=q_st[64:128, pr:pr + 2, e, :],
                                                              in0=misc(m)[64 * e:64 * e + 64, :].rearrange("p (j s) -> p j s", j=2),
                                                              scalar=prm[0:64, QN:QN + 1], in1=f(q_st[0:64, pr:pr + 2, e, :]),
                                                              op0=ALU.mult, op1=ALU.subtract)
                            ins.then_inc(misc_free[m % 4], 1)
                for j, name in enumerate(("w1k", "w1v")):
                    if i == FIRST[name] + 2:
                        ve.wait_ge(hid_ready, j + 1)
                        ve.engine_nop().then_inc(acc_free[USE[name] % 4], 1)
                    if i == FIRST[name] + 3:
                        m = MISC["hidk"] if j == 0 else MISC["hidv"]
                        ve.wait_ge(hid_hi, j + 1)
                        if j == 0:
                            ins = ve.tensor_tensor(hidk_lo, misc(m)[:, 0:128], f(hidk_hi), ALU.subtract)
                        else:
                            ins = ve.tensor_tensor(hidv_lo.rearrange("p (c j n) -> p c j n", c=8, j=4),
                                                   misc(m)[:, 0:128].rearrange("p (c n) -> p c n", c=8).unsqueeze(2)
                                                   .broadcast_to([P, 8, 4, 16]),
                                                   f(hidv_hi).rearrange("p (c j n) -> p c j n", c=8, j=4), ALU.subtract)
                        ins.then_inc(misc_free[m % 4], 1)
                if i == FIRST["w1k"] + 4:
                    ve.wait_ge(squares, 8)
                    mean(NORM_KC, 1.0 / DH)
                if i == FIRST["w1k"] + 5:
                    ve.wait_ge(rs_ready, rs_count(NORM_KC))
                    ve.tensor_scalar(kcn.rearrange("p (e d) -> p e d", e=2),
                                     misc(MISC["kcn"])[0:64, 0:64].unsqueeze(1).broadcast_to([64, 2, DH]),
                                     rs[0:64, NORM_KC, 0:1], None, ALU.mult).then_inc(misc_free[MISC["kcn"] % 4], 1)
                if i == FIRST["w1k"] + 7:
                    m = MISC["kcT"]
                    ve.wait_ge(evac_hi, 13)
                    ve.scalar_tensor_tensor(out=kc_ll, in0=misc(m)[:, 0:64], scalar=prm[:, KN:KN + 1], in1=f(kc_hh),
                                            op0=ALU.mult, op1=ALU.subtract).then_inc(misc_free[m % 4], 1)
                r = i - FIRST["rx"] - 2
                if 0 <= r < 4:
                    ve.wait_ge(xr_hi, r + 1)
                    ve.tensor_tensor(y_lo[:, 2 * r:2 * r + 2, :], A[:, 2 * r:2 * r + 2, :], f(y_hi[:, 2 * r:2 * r + 2, :]),
                                     ALU.subtract).then_inc(xr_lo, 1)
                r = i - FIRST["rx"] - 1
                if 0 <= r < 4:
                    ve.wait_ge(conv0, 2 * r + 2)
                    ps = acc(USE["rx"] + r)
                    for s in range(1, CONV):
                        for e in range(2):
                            m = 2 * r + e
                            ins = ve.scalar_tensor_tensor(out=A[:, m, s:S], in0=ps[:, e * S:(e + 1) * S - s],
                                                          scalar=prm[:, CW + 8 * (3 - s) + m:CW + 8 * (3 - s) + m + 1],
                                                          in1=A[:, m, s:S], op0=ALU.mult, op1=ALU.add)
                        if s < CONV - 1:
                            link(ins)
                    ins.then_inc(xr_ready, 1)
                    ve.wait_ge(xr_ready, r + 1)
                    ve.engine_nop().then_inc(acc_free[(USE["rx"] + r) % 4], 1)
                for n in range(4):
                    if i == FIRST["rg"] + n // 2 + 1:
                        u = USE["rg"] + 2 * n
                        ve.wait_ge(acc_free[u % 4], u // 4 + 1)
                        for m in (2 * n, 2 * n + 1):
                            ve.tensor_scalar(C[:, m, :], C[:, m, :], 1.0, sm[:, 12, m:m + 1], ALU.add, ALU.mult).then_inc(log_a, 1)
                        ve.wait_ge(acc_free[(u + 1) % 4], (u + 1) // 4 + 1)
                        ve.scalar_tensor_tensor(out=A[:, 2 * n:2 * n + 2, :], in0=Dr[:, 2 * n:2 * n + 2, :], scalar=1.0,
                                                in1=A[:, 2 * n:2 * n + 2, :], op0=ALU.add, op1=ALU.mult).then_inc(gated_x, 1)
                if i == RG_SQ:
                    ve.wait_ge(w_ready, 1)
                    for e, (buf, a, b) in enumerate(asq):
                        ve.wait_ge(asq_ready, e + 1)
                        ve.scalar_tensor_tensor(out=Dr[:, a:b, :], in0=buf, scalar=1.0, in1=Dr[:, a:b, :],
                                                op0=ALU.add, op1=ALU.mult).then_inc(asq_used, 1)
                for v in range(2):
                    if i == RG_SCAN[v]:
                        ve.wait_ge(a_ready, 1)
                        ve.wait_ge(u_ready, v + 1)
                        for m in range(4 * v, 4 * v + 4):
                            ins = ve.tensor_tensor_scan(Dr[:, m, :], C[:, m, :], A[:, m, :], 0.0, ALU.mult, ALU.add)
                        link(ins)
                for pnl in range(2):
                    if i == FIRST["mg"] + 2 * pnl + 3:
                        for t in range(T2):
                            u = USE["mg"] + 2 * pnl + t
                            ve.wait_ge(acc_free[u % 4], u // 4 + 1)
                            mv = mrg[:, t, pnl * 512:(pnl + 1) * 512]
                            ve.scalar_tensor_tensor(out=mv, in0=mtt[:, t, :], scalar=1.0, in1=mv, op0=ALU.add,
                                                    op1=ALU.mult).then_inc(m_gated, 1)
                for pnl in range(2):
                    if i == FIRST["nso"] + pnl + 3:
                        ve.wait_ge(slot_done, FIRST["nso"] + pnl + 3)
                        ug = USE["mg"] + 4 + 2 * pnl + 1
                        ve.wait_ge(acc_free[ug % 4], ug // 4 + 1)
                        for t in range(T2):
                            u = USE["nso"] + 2 * pnl + t
                            tv = mt1[:, t, pnl * 512:(pnl + 1) * 512]
                            ve.scalar_tensor_tensor(out=tv, in0=tv, scalar=1.0, in1=acc(u)[:, :], op0=ALU.add,
                                                    op1=ALU.mult).then_inc(acc_free[u % 4], 1)
                        for t in range(T2):
                            u = USE["nso"] + 2 * pnl + t
                            ve.wait_ge(acc_free[u % 4], u // 4 + 1)
                            mv, tv = (z[:, t, pnl * 512:(pnl + 1) * 512] for z in (mrg, mt1))
                            ve.tensor_tensor(mv, mv, tv, ALU.add).then_inc(merged, 1)
                for v in range(2):
                    if i == FIRST["wo"] - 1 + 2 * v:
                        for j in (2 * v, 2 * v + 1):
                            m = MISC["mT"] + j
                            ve.wait_ge(evac_hi, 13 + j + 1)
                            ve.scalar_tensor_tensor(out=h_lo[:, 2 * j:2 * j + 2, :], in0=misc(m)[:, :].rearrange("p (c s) -> p c s", c=2),
                                                    scalar=0.5, in1=f(h_hi[:, 2 * j:2 * j + 2, :]), op0=ALU.mult,
                                                    op1=ALU.subtract).then_inc(misc_free[m % 4], 1)
                if i == FIRST["wo"] + 3:
                    ve.wait_ge(slot_done, FIRST["wo"] + 3)
                    ve.wait_ge(x_again, 16)
                    for t in range(T2):
                        u = USE["wo"] + t
                        ve.tensor_tensor(xs[:, t, 0:512], acc(u)[:, :], xs[:, t, 0:512], ALU.add).then_inc(x1_ready, 1)
                    ve.wait_ge(x1_ready, 2)
                    for t in range(T2):
                        ve.engine_nop().then_inc(acc_free[(USE["wo"] + t) % 4], 1)
                    ve.wait_ge(squares, 10)
                    link(ve.tensor_scalar(ss[:, NORM_X1, 4:6], ss[:, NORM_X1, 0:2], 1.0 / D, EPS, ALU.mult, ALU.add))
                if i == FIRST["wo"] + 4:
                    for t in range(T2):
                        if t == 0:
                            ve.wait_ge(wo_half, 1)
                        else:
                            ve.wait_ge(slot_done, FIRST["wo"] + 4)
                        ve.tensor_tensor(xs[:, t, 512:1024], acc(USE["wo"] + 2 + t)[:, :], xs[:, t, 512:1024], ALU.add).then_inc(x1_ready, 1)
                        ve.wait_ge(squares, 11 + t)
                        ve.tensor_scalar(ms[:, NORM_X1, t:t + 1], ss[:, NORM_X1, 2 + t:3 + t], 1.0 / D, ss[:, NORM_X1, 4 + t:5 + t],
                                         ALU.mult, ALU.add).then_inc(ms_ready, 1)
                        ve.wait_ge(rs_ready, rs_count(NORM_X1, t))
                        w = (D, 512)[t]
                        ve.tensor_scalar(xn2[:, t, 0:w], xs[:, t, 0:w], rs[:, NORM_X1, t:t + 1], None, ALU.mult).then_inc(xn_ready, 1)
                    ve.wait_ge(x1_ready, 4)
                    for t in range(T2):
                        ve.engine_nop().then_inc(acc_free[(USE["wo"] + 2 + t) % 4], 1)
                    for j in range(4):
                        unit_lo(MISC["hT2"] + j, j, G2, 17 + j + 1)
                j = i - FIRST["gu"] - 1
                if 1 <= j <= FF:
                    ve.wait_ge(a_hi_ready, j)
                    ve.tensor_tensor(a_lo[:, j - 1, :], sa[:, (j - 1) % 2, :], f(a_hi[:, j - 1, :]), ALU.subtract).then_inc(a_lo_ready, 1)
                if 0 <= j < FF:
                    u = USE["gu"] + j
                    ve.wait_ge(silu_ready, j + 1)
                    ve.tensor_tensor(sa[:, j % 2, :], acc(u)[:, S:2 * S], sg[:, j % 2, :], ALU.mult).then_inc(a_prod, 1)
                    ve.wait_ge(a_prod, j + 1)
                    ve.engine_nop().then_inc(acc_free[u % 4], 1)
                if i in SPLIT_LAST and i != FIRST["wo"] + 3:
                    if i == FIRST["wo"] + 4:
                        split_lo(i + AHEAD - 1)
                    split_lo(i + AHEAD)
            for t in range(T2):
                for n in range(2):
                    if 2 * t + n < 3:
                        ve.wait_ge(dn_done, 2 * t + n + 1)
                    else:
                        ve.wait_ge(slot_done, NSLOT)
                    xv = xs[:, t, n * 512:(n + 1) * 512]
                    ve.tensor_tensor(xv, acc(USE["dn"] + 2 * t + n)[:, :], xv, ALU.add).then_inc(res_ready, 1)

        @block.tensor
        def _(pe):
            def three(out_, l_hi, l_lo, r_hi, r_lo, start, stop):
                pe.matmul(out_, l_hi, r_hi, start=start, stop=False)
                pe.matmul(out_, l_hi, r_lo, start=False, stop=False)
                return pe.matmul(out_, l_lo, r_hi, start=False, stop=stop)

            def slot_ready(i):
                pe.wait_ge(lo_ready, i + 1)

            def direct(i, u, a_h, a_l, units=None, between=None):
                slot_ready(i)
                wait_acc_free(pe, u)
                s = i % HL
                for mt in range(2):
                    if mt == 1 and between is not None:
                        between()
                    for k in range(KC):
                        if units is not None and mt == 0 and k % 2 == 0:
                            wait_misc_read(pe, units + k // 2)
                        c = k * 256 + mt * P
                        ins = three(acc(u)[:, mt * S:(mt + 1) * S], w_hi[:, s, c:c + P], w_lo[:, s, c:c + P],
                                    a_h[:, k, :], a_l[:, k, :], k == 0, k == KC - 1)
                ins.then_inc(slot_done, 1)

            def panel(i, e, u, a_h, a_l, half_done=None, between=None):
                slot_ready(i)
                s = i % HL
                for t in range(T2):
                    if e == 0:
                        wait_acc_free(pe, u + t)
                    for kk in range(4):
                        k = 4 * e + kk
                        w = slice(kk * 512, (kk + 1) * 512)
                        ins = three(acc(u + t)[:, :], a_h(k, t), a_l(k, t), w_hi[:, s, w], w_lo[:, s, w],
                                    k == 0, k == KC - 1)
                    if t == 0 and half_done is not None:
                        ins.then_inc(half_done, 1)
                    if t == 0 and between is not None:
                        between()
                ins.then_inc(slot_done, 1)

            def h_of(t_):
                return lambda k, t: t_[:, k, t * P:(t + 1) * P]

            def o_of(e):
                return lambda k, t: oT[:, k, e, t * P:(t + 1) * P]

            def transposed_unit(m, src, j):
                wait_misc_free(pe, m)
                for e in range(2):
                    for t in range(T2):
                        c = 2 * j + e
                        ins = pe.transpose(misc(m)[:, e * S + t * P:e * S + (t + 1) * P], src[:, t, c * P:(c + 1) * P], ident[:, :])
                ins.then_inc(misc_done, 1)

            def merged_transposed(v):
                pe.wait_ge(merged, 2 * v + 2)
                for j in (2 * v, 2 * v + 1):
                    transposed_unit(MISC["mT"] + j, mrg, j)

            def compressed_transposed():
                u = USE["pcT"]
                pe.wait_ge(c_ready, 1)
                wait_acc_free(pe, u)
                for hf in range(2):
                    for t in range(T2):
                        ins = pe.transpose(acc(u)[:, hf * S + t * P:hf * S + (t + 1) * P],
                                           cexp[:, t * S + hf * P:t * S + (hf + 1) * P], ident[:, :])
                ins.then_inc(pcT_done, 1)

            pe.wait_ge(consts, 4)
            def keep_busy(n):
                for _ in range(n):
                    pe.transpose(psum[3][:, 0:P], ident[:, :], ident[:, :])

            keep_busy(28)
            pe.wait_ge(xn_ready, 1)
            pe.wait_ge(xn1_ready, 1)
            for j in range(4):
                transposed_unit(MISC["xT"] + j, xn, j)
            keep_busy(24)
            def scores(h):
                g = h // (HEADS // GROUPS)
                m = MISC["att"] + 4 * h
                for t in range(T2):
                    wait_misc_free(pe, m + t)
                    bank = misc(m + t)
                    w = P * (t + 1)
                    q = q_st[:, h // 2, h % 2, t * P:(t + 1) * P]
                    o3 = bank[:, 0:2 * w].rearrange("p (b c) -> p b c", b=2)
                    for n, kt in enumerate((k_hh, k_ll)):
                        pe.matmul(o3, q, kt[:, g, :].rearrange("p (b c) -> p b c", b=2)[:, :, 0:w], start=n == 0, stop=n == 1)
                    pe.matmul(o3[:, :, t * P:(t + 1) * P], identr[:, :],
                              maskr[:, 0:2 * P].rearrange("p (b c) -> p b c", b=2), start=False, stop=True,
                              skip_group_check=True).then_inc(s_done, 1)

            def turn_a(h):
                m = MISC["att"] + 4 * h + 2
                pe.wait_ge(prob_ready, h + 1)
                wait_misc_free(pe, m)
                for b, t, src in ((0, 0, 0), (0, 1, 256), (1, 0, 128), (1, 1, 512)):
                    ins = pe.transpose(misc(m)[:, b * S + t * P:b * S + (t + 1) * P], prob[:, src:src + P], ident[:, :])
                ins.then_inc(ta_done, 1)

            def turn_b(h):
                m = MISC["att"] + 4 * h + 3
                wait_misc_free(pe, m)
                if h >= 2 and h % 2 == 0:
                    pe.wait_ge(o_ready, h // 2)
                for b, src in ((0, 384), (1, 640)):
                    ins = pe.transpose(misc(m)[:, b * P:(b + 1) * P], prob[:, src:src + P], ident[:, :])
                ins.then_inc(tb_done, 1)

            def values(h):
                g = h // (HEADS // GROUPS)
                m = MISC["att"] + 4 * h + 2
                o = o_bank[64 * (h % 2):64 * (h % 2) + 64, :]
                wait_misc_read(pe, m)
                wait_misc_read(pe, m + 1)
                if h == 0:
                    u = USE["pcT"]
                    wait_misc_read(pe, MISC["vrep"])
                    pe.wait_ge(acc_free[u % 4], u // 4 + 1)
                for b in range(2):
                    pe.matmul(o, v_sb[:, 0, b * S + g * DH:b * S + (g + 1) * DH], pTa[:, b * S:(b + 1) * S],
                              start=b == 0, stop=False)
                pe.matmul(o, vcx[:, h // 8, h % 8, :], pcT[:, h // 8, :], start=False, stop=True)
                for b in range(2):
                    ins = pe.matmul(o[:, P:S], v_sb[:, 1, b * S + g * DH:b * S + (g + 1) * DH], pTb[:, b * P:(b + 1) * P],
                                    start=False, stop=True, skip_group_check=True)
                ins.then_inc(o_done, 1)

            for i in range(NSLOT):
                h = i - HEAD0
                if 1 <= h <= HEADS:
                    turn_a(h - 1)
                if 0 <= h < HEADS:
                    scores(h)
                if 1 <= h <= HEADS:
                    turn_b(h - 1)
                for name in ("kc", "vc", "rx", "ry", "gu"):
                    r = i - FIRST[name]
                    if 0 <= r < dict(ORDER)[name]:
                        units = {FIRST["rx"]: MISC["xT"], FIRST["gu"]: MISC["hT2"]}.get(i)
                        direct(i, USE_RY[r] if name == "ry" else USE[name] + r, h_hi, h_lo, units,
                               compressed_transposed if i == HEAD0 + 1 else None)
                for name in ("kk", "vv", "qa", "qb", "mg"):
                    r = i - FIRST[name]
                    if 0 <= r < dict(ORDER)[name]:
                        panel(i, r % 2, USE[name] + r // 2 * 2, h_of(h_hi), h_of(h_lo))
                for name in ("rgo", "nso", "wo"):
                    r = i - FIRST[name]
                    if 0 <= r < dict(ORDER)[name]:
                        src = {"rgo": (h_of(y_hi), h_of(y_lo)), "nso": (o_of(0), o_of(1)), "wo": (h_of(h_hi), h_of(h_lo))}[name]
                        if name == "rgo" and r % 2 == 0:
                            pe.wait_ge(y_lo_ready, r + 2)
                        if name == "nso" and r % 2 == 0:
                            pe.wait_ge(o_ready, HEADS // 4 * (r // 2 + 1))
                        if name == "wo" and r % 2 == 0:
                            wait_misc_read(pe, MISC["mT"] + r + 1)
                        between = (lambda: merged_transposed(0)) if (name, r) == ("nso", 3) else None
                        panel(i, r // 2, USE[name] + r % 2 * 2, *src, wo_half if (name, r) == ("wo", 3) else None, between)
                for j, name in enumerate(("w1k", "w1v")):
                    r = i - FIRST[name]
                    if 0 <= r < 2:
                        u = USE[name]
                        slot_ready(i)
                        if r == 0:
                            wait_acc_free(pe, u)
                            pe.wait_ge(z_lo_ready, j + 1)
                        for lp in range(8):
                            at = r * 520 + 8 * r + lp
                            cols = slice(at, at + 8 * 63 + 1, 8)
                            w = slice(lp * 256, (lp + 1) * 256)
                            ins = three(acc(u)[0:64, 0:256], z_hi[j][:, cols], z_lo[j][:, cols],
                                        w_hi[:, i % HL, w], w_lo[:, i % HL, w], r == 0 and lp == 0, r == 1 and lp == 7)
                        ins.then_inc(slot_done, 1)
                r = i - FIRST["rg"]
                if 0 <= r < 2:
                    slot_ready(i)
                    for nn in range(2):
                        n = 2 * r + nn
                        pe.wait_ge(xr_lo, n + 1)
                        for kind in range(2):
                            u = USE["rg"] + 2 * n + kind
                            wait_acc_free(pe, u)
                            for dt in range(2):
                                for c in range(2):
                                    w = ((nn * 2 + kind) * 2 + c) * 256 + dt * P
                                    ins = three(acc(u)[:, dt * S:(dt + 1) * S], w_hi[:, i % HL, w:w + P], w_lo[:, i % HL, w:w + P],
                                                y_hi[:, 2 * n + c, :], y_lo[:, 2 * n + c, :], c == 0, c == 1)
                            ins.then_inc(slot_done if (nn, kind) == (1, 1) else rg_done, 1)
                r = i - FIRST["dn"]
                if 0 <= r < FF // 2:
                    slot_ready(i)
                    pe.wait_ge(a_lo_ready, 2 * r + 2)
                    for t in range(T2):
                        for n in range(2):
                            u = USE["dn"] + 2 * t + n
                            if r == 0:
                                wait_acc_free(pe, u)
                            if r == FF // 2 - 1 and 2 * t + n > 0:
                                ins.then_inc(dn_done, 1)
                            for kk in range(2):
                                k = 2 * r + kk
                                w = slice(kk * 1024 + n * 512, kk * 1024 + (n + 1) * 512)
                                ins = three(acc(u)[:, :], a_hi[:, k, t * P:(t + 1) * P], a_lo[:, k, t * P:(t + 1) * P],
                                            w_hi[:, i % HL, w], w_lo[:, i % HL, w], k == 0, k == FF - 1)
                    ins.then_inc(slot_done, 1)

                if i == 1:
                    m = MISC["ng"]
                    pe.wait_ge(small_lo, 1)
                    wait_misc_free(pe, m)
                    for k in range(KC):
                        c = NG_W + 48 * k
                        ins = three(misc(m)[0:48, 0:S], sw_hi[:, c:c + 48], sw_lo[:, c:c + 48], h_hi[:, k, :], h_lo[:, k, :],
                                    k == 0, k == KC - 1)
                    ins.then_inc(misc_done, 1)
                if i == 2:
                    m = MISC["ngT"]
                    wait_misc_read(pe, MISC["ng"])
                    wait_misc_free(pe, m)
                    for t in range(T2):
                        ins = pe.transpose(misc(m)[:, 48 * t:48 * t + 48], gtmp[:, t * P:(t + 1) * P], ident[0:48, 0:48])
                    ins.then_inc(misc_done, 1)
                if 1 <= h <= HEADS:
                    values(h - 1)
                if i == FIRST["kk"] + 3:
                    pe.wait_ge(kn_ready, 2)
                    for g in range(GROUPS):
                        m = MISC["kT"] + g
                        wait_misc_free(pe, m)
                        for b in range(2):
                            for t in range(T2):
                                c = (4 * b + g) * P
                                ins = pe.transpose(misc(m)[:, b * S + t * P:b * S + (t + 1) * P], kn[:, t, c:c + P], ident[:, :])
                        ins.then_inc(misc_done, 1)
                if i == FIRST["w1k"] + 2:
                    j, m = 0, MISC["hidk"]
                    pe.wait_ge(hid_ready, j + 1)
                    wait_misc_free(pe, m)
                    for c in range(2):
                        ins = pe.transpose(misc(m)[:, 64 * c:64 * c + 64], hid[j][:, c * P:(c + 1) * P], ident[0:64, 0:64])
                    ins.then_inc(misc_done, 1)
                if i == FIRST["w1k"] + 3:
                    m = MISC["kcn"]
                    wait_misc_read(pe, MISC["hidk"])
                    wait_misc_free(pe, m)
                    for c in range(2):
                        w = slice(W2K + 64 * c, W2K + 64 * c + 64)
                        l = slice(64 * c, 64 * c + 64)
                        ins = three(misc(m)[0:64, 0:64], hidk_hi[:, l], hidk_lo[:, l], sw_hi[:, w], sw_lo[:, w], c == 0, c == 1)
                    ins.then_inc(misc_done, 1)
                if i == FIRST["w1k"] + 6:
                    m = MISC["kcT"]
                    wait_misc_read(pe, MISC["kcn"])
                    wait_misc_free(pe, m)
                    pe.transpose(misc(m)[:, 0:64], kcn, ident[0:64, 0:64]).then_inc(misc_done, 1)
                for pnl, name in enumerate(("qa", "qb")):
                    if i == FIRST[name] + 4:
                        pe.wait_ge(qn_ready, 2 * pnl + 2)
                        for v in range(2):
                            m = MISC[("qTa", "qTb")[pnl]] + v
                            wait_misc_free(pe, m)
                            for jj in range(2):
                                for t in range(T2):
                                    c = (4 * pnl + 2 * v + jj) * P
                                    ins = pe.transpose(misc(m)[:, jj * S + t * P:jj * S + (t + 1) * P], qz[:, t, c:c + P], ident[:, :])
                            ins.then_inc(misc_done, 1)
                if i == FIRST["w1v"] + 2:
                    j, m = 1, MISC["hidv"]
                    pe.wait_ge(hid_ready, j + 1)
                    wait_misc_free(pe, m)
                    for c in range(2):
                        ins = pe.transpose(misc(m)[:, 64 * c:64 * c + 64], hid[j][:, c * P:(c + 1) * P], ident[0:64, 0:64])
                    ins.then_inc(misc_done, 1)
                if i == HEAD0 - 1:
                    m = MISC["cmps"]
                    wait_misc_read(pe, MISC["kcT"])
                    wait_misc_read(pe, MISC["qTb"] + 1)
                    pe.wait_ge(masks_r, 1)
                    for t in range(T2):
                        wait_misc_free(pe, m + t)
                        bank = misc(m + t)[:, :].rearrange("p (e h c) -> p e h c", e=2, h=HEADS)
                        for hh in range(HEADS):
                            g = hh // (HEADS // GROUPS)
                            pe.matmul(bank[:, :, hh, :], q_st[:, hh // 2, hh % 2, t * P:(t + 1) * P],
                                      kc_hl.rearrange("p (e g c) -> p e g c", e=2, g=GROUPS)[:, :, g, :],
                                      start=hh == 0, stop=True, skip_group_check=True)
                        pe.matmul(bank[:, 0, :, :], identr[:, :],
                                  maskr[:, 2 * P + 16 * t:2 * P + 16 * t + 16].unsqueeze(1).broadcast_to([P, HEADS, 16]),
                                  start=False, stop=True, skip_group_check=True).then_inc(misc_done, 1)
                if i == HEAD0 - 1:
                    wait_misc_read(pe, MISC["hidv"])
                    m = MISC["vrep"]
                    wait_misc_free(pe, m)
                    for hf in range(2):
                        for c in range(2):
                            w = slice(W2V + 64 * c, W2V + 64 * c + 64)
                            l = slice(256 * c + P * hf, 256 * c + P * (hf + 1))
                            ins = three(misc(m)[:, DH * hf:DH * (hf + 1)], hidv_hi[:, l], hidv_lo[:, l], sw_hi[:, w], sw_lo[:, w],
                                        c == 0, c == 1)
                    ins.then_inc(misc_done, 1)
                if i == FIRST["wo"]:
                    merged_transposed(1)
                if i == FIRST["wo"] + 3:
                    pe.wait_ge(xn_ready, 2)
                    for t in range(T2):
                        for j in range(4):
                            m = MISC["hT2"] + j
                            if t == 0:
                                wait_misc_free(pe, m)
                            elif j == 0:
                                pe.wait_ge(xn_ready, 3)
                            elif j == 2:
                                pe.wait_ge(xn1_ready, 2)
                            for e in range(2):
                                c = 2 * j + e
                                ins = pe.transpose(misc(m)[:, e * S + t * P:e * S + (t + 1) * P], xn2[:, t, c * P:(c + 1) * P],
                                                   ident[:, :])
                            if t == 1:
                                ins.then_inc(misc_done, 1)


def _chunks(w, n):
    return w.reshape(-1, 128, n).transpose(1, 0, 2)


def _direct(w):
    c = _chunks(w, w.shape[1])
    return [c[:, :, 256 * j:256 * (j + 1)].reshape(128, SLOT) for j in range(w.shape[1] // 256)]


def _panels(w, halves_first=False):
    c = _chunks(w, w.shape[1])
    n = w.shape[1] // 512
    order = [(j, e) for e in range(2) for j in range(n)] if halves_first else [(j, e) for j in range(n) for e in range(2)]
    return [c[:, 4 * e:4 * e + 4, 512 * j:512 * (j + 1)].reshape(128, SLOT) for j, e in order]


def lay_out(inputs):
    a = {k: np.asarray(v) for k, v in inputs.items()}
    w_in = a["w_in"][0]
    at = np.cumsum([0, 1024, 1024, 1024] + [256] * 6 + [48, 2048])
    rx, ry, q, kc, vc, ks, vs, kw, vw, ng, mg = [w_in[:, at[i]:at[i + 1]] for i in range(11)]

    def pairs(w):
        return w.reshape(1024, 2, 2, 64).transpose(0, 2, 1, 3).reshape(1024, 256)

    q_slots = _panels(q)
    w1 = [[_chunks(a[n][0], 256)[:, 8 * e:8 * e + 8].reshape(128, SLOT) for e in range(2)] for n in ("cmp_k_w1", "cmp_v_w1")]
    rg = np.stack([a["rg_wa"][0], a["rg_wi"][0]], 1).reshape(4, 2, 2, 128, 256)
    slots = _direct(rx) + _panels(np.concatenate([ks, kw], 1))
    slots += [rg[2 * r:2 * r + 2].transpose(3, 0, 1, 2, 4).reshape(128, SLOT) for r in range(2)]
    slots += _direct(pairs(kc)) + _direct(pairs(vc)) + q_slots[:2] + w1[0] + q_slots[2:] + w1[1]
    slots += _panels(np.concatenate([vs, vw], 1)) + _direct(ry) + _panels(a["w_rg_out"][0], True) + _panels(mg)
    slots += _panels(a["w_nsa_out"][0], True) + _panels(a["w_o"][0], True)
    gu = np.concatenate([a["w_gate"][0].reshape(1024, FF, 1, 128), a["w_up"][0].reshape(1024, FF, 1, 128)], 2)
    slots += _direct(gu.reshape(1024, 2 * DFF))
    dn = _chunks(a["w_down"][0], 1024)
    slots += [dn[:, 2 * r:2 * r + 2].reshape(128, SLOT) for r in range(FF // 2)]
    stream = np.ascontiguousarray(np.stack(slots, 0))

    def cols(v):
        return v.reshape(-1, 128).T

    small = np.concatenate([_chunks(ng, 48).reshape(128, 384), _chunks(a["cmp_k_w2"][0], 64).reshape(128, 128),
                            _chunks(a["cmp_v_w2"][0], 64).reshape(128, 128)], 1)

    def both(v):
        return np.concatenate([v, v]).reshape(128, 1)

    params = np.concatenate(
        [cols(a["norm1"][0]), cols(a["norm2"][0])] + [cols(a["conv_w"][0, k]) for k in range(4)]
        + [cols(a["conv_b"][0]), cols(a["rg_ba"][0]), cols(a["rg_bi"][0]), cols(a["rg_lambda"][0]), both(a["q_norm"][0])]
        + [both(a["k_norm"][0, b]) for b in range(3)]
        + [a[n][0].reshape(16, 128).T for n in ("cmp_pos_k", "cmp_pos_v")], 1)
    return {"x_dram": np.ascontiguousarray(a["x"][0]), "stream_dram": stream,
            "small_dram": np.ascontiguousarray(small), "params_dram": np.ascontiguousarray(params)}


def kernel(**inputs):
    import concourse.bacc as _bacc
    from concourse.bass_utils import run_bass_kernel_spmd as _run

    nc = _bacc.Bacc("TRN2", target_bir_lowering=False, num_devices=1)
    arrays = lay_out(inputs)
    args = [nc.dram_tensor(n, a.shape, mybir.dt.from_np(a.dtype), kind="ExternalInput").ap() for n, a in arrays.items()]
    res = nc.dram_tensor("out_dram", (S, D), F32, kind="ExternalOutput").ap()
    hybrid_layer(nc, *args, res)
    r = _run(nc, [arrays], core_ids=[0])
    return r.results[0]["out_dram"].reshape(1, S, D)
```
